# Optimizing a Trainium2 kernel written in Bass

```python
import math
import jax, jax.numpy as jnp
from jax import lax
import numpy as np

D_MODEL = 1024
BATCH = 1
SEQ = 512
DEPTH = 2
DEC_BATCH = 8
DEC_SEQ = 8
PAST_LEN = 4096
PAGE_SIZE = 128

N_MIXERS = 2
N_A = (DEPTH + 1) // 2
N_B = DEPTH // 2
HG_DK = 128
HG_HEADS = D_MODEL // HG_DK
HG_DV = D_MODEL // HG_HEADS
ML_INNER = 2 * D_MODEL
ML_HEADS = 4
ML_DH = ML_INNER // ML_HEADS
ML_CONV = 4
ML_QKV_BLOCK = 4
MOE_GROUPS = 4
MOE_EPG = 4
MOE_EXPERTS = MOE_GROUPS * MOE_EPG
MOE_TOPK = 2
MOE_DFF = 256
CHUNK = 64
EPS = 1e-6

kernel_name = 'hgrn2_mlstm_hier_moe_adaln_step'

F32 = jnp.float32

def rmsnorm(x, g):
    x32 = x.astype(F32)
    y = x32 * lax.rsqrt(jnp.mean(x32 * x32, axis=-1, keepdims=True) + EPS)
    return (y * g.astype(F32)).astype(x.dtype)

def _to_chunks(a, L):
    B, T = a.shape[:2]
    a = a.reshape((B, T // L, L) + a.shape[2:])
    return a.transpose((1, 0, 3, 2) + tuple(range(4, a.ndim)))

def _from_chunks(a):
    nC, B, H, L = a.shape[:4]
    a = a.transpose((1, 0, 3, 2) + tuple(range(4, a.ndim)))
    return a.reshape((B, nC * L, H) + a.shape[4:])

def gla_chunk_scan(q, k, v, log_f, S0):
    T = q.shape[1]
    L = math.gcd(T, CHUNK)
    mask = jnp.tril(jnp.ones((L, L), dtype=bool))

    def step(S, inp):
        qc, kc, vc, gc = inp
        b = jnp.cumsum(gc, axis=2)
        diff = b[:, :, :, None, :] - b[:, :, None, :, :]
        decay = jnp.exp(jnp.where(mask[:, :, None], diff, -jnp.inf))
        A = jnp.einsum('bhtk,bhsk,bhtsk->bhts', qc, kc, decay)
        o = jnp.einsum('bhtk,bhkv->bhtv', qc * jnp.exp(b), S) + jnp.einsum('bhts,bhsv->bhtv', A, vc)
        bL = b[:, :, -1:, :]
        S_new = jnp.exp(bL[:, :, 0, :])[..., None] * S + jnp.einsum('bhsk,bhsv->bhkv', kc * jnp.exp(bL - b), vc)
        return S_new, o

    S_T, o = lax.scan(step, S0, (_to_chunks(q, L), _to_chunks(k, L), _to_chunks(v, L), _to_chunks(log_f, L)))
    return _from_chunks(o), S_T

def hgrn2_mixer(h, S0, w_in, w_o, g_norm, lb):
    B, T, _ = h.shape
    HK = HG_HEADS * HG_DK
    HV = HG_HEADS * HG_DV
    proj = h @ w_in
    zq = proj[..., :HK]
    zf = proj[..., HK:2 * HK]
    zi = proj[..., 2 * HK:2 * HK + HV]
    zg = proj[..., 2 * HK + HV:]
    lb32 = lb.astype(F32)
    f = lb32 + (1.0 - lb32) * jax.nn.sigmoid(zf.astype(F32))
    q = jax.nn.silu(zq.astype(F32)).reshape(B, T, HG_HEADS, HG_DK)
    k = (1.0 - f).reshape(B, T, HG_HEADS, HG_DK)
    log_f = jnp.log(f).reshape(B, T, HG_HEADS, HG_DK)
    v = zi.astype(F32).reshape(B, T, HG_HEADS, HG_DV)
    o, S_T = gla_chunk_scan(q, k, v, log_f, S0.astype(F32))
    o = o * lax.rsqrt(jnp.mean(o * o, axis=-1, keepdims=True) + EPS) * g_norm.astype(F32)
    o = o.reshape(B, T, HV) * jax.nn.silu(zg.astype(F32))
    return o.astype(h.dtype) @ w_o, S_T

def mlstm_chunk_scan(q, k, v, ig, lf, C0, n0, m0):
    T = q.shape[1]
    L = math.gcd(T, CHUNK)
    mask = jnp.tril(jnp.ones((L, L), dtype=bool))

    def step(carry, inp):
        C, n, m = carry
        qc, kc, vc, igc, lfc = inp
        b = jnp.cumsum(lfc, axis=-1)
        a = b + m[..., None]
        Dm = jnp.where(mask, b[..., :, None] - b[..., None, :] + igc[..., None, :], -jnp.inf)
        m_t = jnp.maximum(a, jnp.max(Dm, axis=-1))
        w_c = jnp.exp(a - m_t)
        W = jnp.exp(Dm - m_t[..., None])
        S = jnp.einsum('bhtk,bhsk->bhts', qc, kc) * W
        num = w_c[..., None] * jnp.einsum('bhtk,bhkv->bhtv', qc, C) + jnp.einsum('bhts,bhsv->bhtv', S, vc)
        den = w_c * jnp.einsum('bhtk,bhk->bht', qc, n) + jnp.sum(S, axis=-1)
        hc = num / jnp.maximum(jnp.abs(den), jnp.exp(-m_t))[..., None]
        mL = m_t[..., -1]
        wL_c = jnp.exp(a[..., -1] - mL)
        wL = jnp.exp(Dm[..., -1, :] - mL[..., None])
        C_new = wL_c[..., None, None] * C + jnp.einsum('bhs,bhsk,bhsv->bhkv', wL, kc, vc)
        n_new = wL_c[..., None] * n + jnp.einsum('bhs,bhsk->bhk', wL, kc)
        return (C_new, n_new, mL), hc

    (C_T, n_T, m_T), hs = lax.scan(step, (C0, n0, m0), (_to_chunks(q, L), _to_chunks(k, L), _to_chunks(v, L), _to_chunks(ig, L), _to_chunks(lf, L)))
    return _from_chunks(hs), C_T, n_T, m_T

def mlstm_mixer(h, C0, n0, m0, conv0, p, j):
    B, T, _ = h.shape
    up = h @ p['ml_wup'][j]
    xm = up[..., :ML_INNER]
    z = up[..., ML_INNER:]
    xpad = jnp.concatenate([conv0.astype(xm.dtype), xm], axis=1)
    conv_w = p['ml_conv_w'][j]
    xc = p['ml_conv_b'][j]
    for tap in range(ML_CONV):
        xc = xc + xpad[:, tap:tap + T] * conv_w[tap]
    xc = jax.nn.silu(xc)
    new_conv = xpad[:, -(ML_CONV - 1):]

    def headwise(u, w):
        return jnp.einsum('btni,noi->btno', u.reshape(B, T, ML_INNER // ML_QKV_BLOCK, ML_QKV_BLOCK), w).reshape(B, T, ML_INNER)

    q = headwise(xc, p['ml_wq'][j])
    k = headwise(xc, p['ml_wk'][j])
    v = headwise(xm, p['ml_wv'][j])
    gin = jnp.concatenate([q, k, v], axis=-1)
    ig = (gin @ p['ml_wig'][j] + p['ml_big'][j]).astype(F32)
    lf = jax.nn.log_sigmoid((gin @ p['ml_wfg'][j] + p['ml_bfg'][j]).astype(F32))

    def rs(u):
        return u.astype(F32).reshape(B, T, ML_HEADS, ML_DH)

    hc, C_T, n_T, m_T = mlstm_chunk_scan(rs(q), rs(k) * (ML_DH ** -0.5), rs(v), ig, lf,
                                         C0.astype(F32), n0.astype(F32), m0.astype(F32))
    mu = jnp.mean(hc, axis=-1, keepdims=True)
    var = jnp.mean((hc - mu) ** 2, axis=-1, keepdims=True)
    hn = ((hc - mu) * lax.rsqrt(var + EPS)).reshape(B, T, ML_INNER) * p['ml_norm'][j].astype(F32)
    ho = (hn + p['ml_skip'][j].astype(F32) * xc.astype(F32)) * jax.nn.silu(z.astype(F32))
    return ho.astype(h.dtype) @ p['ml_wdown'][j], C_T, n_T, m_T, new_conv

def hier_moe(h, w_rg, b_rg, w_re, b_re, w1, w3, w2):
    B, T, D = h.shape
    hf = h.reshape(B * T, D)
    g_logits = (hf @ w_rg + b_rg).astype(F32)
    p_group = jax.nn.softmax(g_logits, axis=-1)
    g_star = jnp.argmax(g_logits, axis=-1)
    p_star = jnp.max(p_group, axis=-1)
    e_logits = (jnp.einsum('nd,dge->nge', hf, w_re) + b_re).astype(F32)
    e_sel = jnp.einsum('nge,ng->ne', e_logits, jax.nn.one_hot(g_star, MOE_GROUPS, dtype=F32))
    top_v, top_i = lax.top_k(e_sel, MOE_TOPK)
    w_top = p_star[:, None] * jax.nn.softmax(top_v, axis=-1)
    eid = g_star[:, None] * MOE_EPG + top_i
    combine = jnp.sum(jax.nn.one_hot(eid, MOE_EXPERTS, dtype=F32) * w_top[..., None], axis=1)
    hid = jax.nn.silu(jnp.einsum('nd,edf->nef', hf, w1)) * jnp.einsum('nd,edf->nef', hf, w3)
    out = jnp.einsum('nef,efd->nd', hid * combine[..., None].astype(hid.dtype), w2)
    return out.reshape(B, T, D)

def trunk(x, c, s_hg, s_c, s_n, s_m, s_conv, p):
    lb_all = jnp.cumsum(jax.nn.softmax(p['hg_lb'].astype(F32), axis=0), axis=0)
    cmod = jax.nn.silu(c)
    new_hg, new_c, new_n, new_m, new_conv = [], [], [], [], []
    for l in range(DEPTH):
        mod = cmod @ p['w_ada'][l] + p['b_ada'][l]
        sh1, sc1, g1, sh2, sc2, g2 = [u[:, None, :] for u in jnp.split(mod, 6, axis=-1)]
        h = rmsnorm(x, p['norm_g'][l, 0]) * (1 + sc1) + sh1
        if l % N_MIXERS == 0:
            a = l // N_MIXERS
            mix, S = hgrn2_mixer(h, s_hg[a], p['hg_win'][a], p['hg_wo'][a], p['hg_norm'][a], lb_all[l])
            new_hg.append(S.astype(x.dtype))
        else:
            j = l // N_MIXERS
            mix, C, n, m, cv = mlstm_mixer(h, s_c[j], s_n[j], s_m[j], s_conv[j], p, j)
            new_c.append(C.astype(x.dtype))
            new_n.append(n.astype(x.dtype))
            new_m.append(m.astype(x.dtype))
            new_conv.append(cv.astype(x.dtype))
        x = x + g1 * mix
        h = rmsnorm(x, p['norm_g'][l, 1]) * (1 + sc2) + sh2
        x = x + g2 * hier_moe(h, p['moe_wrg'][l], p['moe_brg'][l], p['moe_wre'][l], p['moe_bre'][l],
                              p['moe_w1'][l], p['moe_w3'][l], p['moe_w2'][l])
    y = rmsnorm(x, p['final_g'])
    return y, jnp.stack(new_hg), jnp.stack(new_c), jnp.stack(new_n), jnp.stack(new_m), jnp.stack(new_conv)

def setup_inputs(seed: int = 0) -> dict:
    key = jax.random.key(seed)
    ks = iter(jax.random.split(key, 48))

    def nrm(shape, scale):
        return jax.random.normal(next(ks), shape, F32) * scale

    D = D_MODEL
    HK = HG_HEADS * HG_DK
    HV = HG_HEADS * HG_DV
    NBLK = ML_INNER // ML_QKV_BLOCK
    inp = {}
    inp['x_prompt'] = nrm((BATCH, SEQ, D), 1.0)
    inp['x_sample'] = nrm((DEC_BATCH, DEC_SEQ, D), 1.0)
    inp['c_prompt'] = nrm((BATCH, D), 1.0)
    inp['c_sample'] = nrm((DEC_BATCH, D), 1.0)
    inp['state_hgrn'] = nrm((N_A, DEC_BATCH, HG_HEADS, HG_DK, HG_DV), 0.1)
    inp['state_mlstm_c'] = nrm((N_B, DEC_BATCH, ML_HEADS, ML_DH, ML_DH), 0.05)
    inp['state_mlstm_n'] = nrm((N_B, DEC_BATCH, ML_HEADS, ML_DH), 0.05)
    inp['state_mlstm_m'] = jax.random.uniform(next(ks), (N_B, DEC_BATCH, ML_HEADS), F32, 0.0, 3.0)
    inp['state_conv'] = nrm((N_B, DEC_BATCH, ML_CONV - 1, ML_INNER), 1.0)
    inp['w_ada'] = nrm((DEPTH, D, 6 * D), 0.5 * D ** -0.5)
    inp['b_ada'] = nrm((DEPTH, 6 * D), 0.02)
    inp['norm_g'] = 1.0 + nrm((DEPTH, 2, D), 0.02)
    inp['final_g'] = 1.0 + nrm((D,), 0.02)
    inp['hg_win'] = nrm((N_A, D, 2 * HK + 2 * HV), D ** -0.5)
    inp['hg_wo'] = nrm((N_A, HV, D), HV ** -0.5)
    inp['hg_norm'] = 1.0 + nrm((N_A, HG_DV), 0.02)
    inp['hg_lb'] = 1.0 + nrm((DEPTH + 1, HK), 0.1)
    inp['ml_wup'] = nrm((N_B, D, 2 * ML_INNER), D ** -0.5)
    inp['ml_conv_w'] = nrm((N_B, ML_CONV, ML_INNER), ML_CONV ** -0.5)
    inp['ml_conv_b'] = nrm((N_B, ML_INNER), 0.02)
    inp['ml_wq'] = nrm((N_B, NBLK, ML_QKV_BLOCK, ML_QKV_BLOCK), ML_QKV_BLOCK ** -0.5)
    inp['ml_wk'] = nrm((N_B, NBLK, ML_QKV_BLOCK, ML_QKV_BLOCK), ML_QKV_BLOCK ** -0.5)
    inp['ml_wv'] = nrm((N_B, NBLK, ML_QKV_BLOCK, ML_QKV_BLOCK), ML_QKV_BLOCK ** -0.5)
    inp['ml_wig'] = nrm((N_B, 3 * ML_INNER, ML_HEADS), (3 * ML_INNER) ** -0.5)
    inp['ml_big'] = nrm((N_B, ML_HEADS), 0.1)
    inp['ml_wfg'] = nrm((N_B, 3 * ML_INNER, ML_HEADS), (3 * ML_INNER) ** -0.5)
    inp['ml_bfg'] = jnp.linspace(3.0, 6.0, ML_HEADS, dtype=F32)[None, :] + nrm((N_B, ML_HEADS), 0.1)
    inp['ml_norm'] = 1.0 + nrm((N_B, ML_INNER), 0.02)
    inp['ml_skip'] = 1.0 + nrm((N_B, ML_INNER), 0.02)
    inp['ml_wdown'] = nrm((N_B, ML_INNER, D), ML_INNER ** -0.5)
    inp['moe_wrg'] = nrm((DEPTH, D, MOE_GROUPS), D ** -0.5)
    inp['moe_brg'] = nrm((DEPTH, MOE_GROUPS), 0.01)
    inp['moe_wre'] = nrm((DEPTH, D, MOE_GROUPS, MOE_EPG), D ** -0.5)
    inp['moe_bre'] = nrm((DEPTH, MOE_GROUPS, MOE_EPG), 0.01)
    inp['moe_w1'] = nrm((DEPTH, MOE_EXPERTS, D, MOE_DFF), D ** -0.5)
    inp['moe_w3'] = nrm((DEPTH, MOE_EXPERTS, D, MOE_DFF), D ** -0.5)
    inp['moe_w2'] = nrm((DEPTH, MOE_EXPERTS, MOE_DFF, D), MOE_DFF ** -0.5)
    return inp

def reference(x_prompt, x_sample, c_prompt, c_sample, state_hgrn, state_mlstm_c, state_mlstm_n, state_mlstm_m, state_conv,
              w_ada, b_ada, norm_g, final_g, hg_win, hg_wo, hg_norm, hg_lb,
              ml_wup, ml_conv_w, ml_conv_b, ml_wq, ml_wk, ml_wv, ml_wig, ml_big, ml_wfg, ml_bfg, ml_norm, ml_skip, ml_wdown,
              moe_wrg, moe_brg, moe_wre, moe_bre, moe_w1, moe_w3, moe_w2):
    p = dict(w_ada=w_ada, b_ada=b_ada, norm_g=norm_g, final_g=final_g,
             hg_win=hg_win, hg_wo=hg_wo, hg_norm=hg_norm, hg_lb=hg_lb,
             ml_wup=ml_wup, ml_conv_w=ml_conv_w, ml_conv_b=ml_conv_b, ml_wq=ml_wq, ml_wk=ml_wk, ml_wv=ml_wv,
             ml_wig=ml_wig, ml_big=ml_big, ml_wfg=ml_wfg, ml_bfg=ml_bfg, ml_norm=ml_norm, ml_skip=ml_skip, ml_wdown=ml_wdown,
             moe_wrg=moe_wrg, moe_brg=moe_brg, moe_wre=moe_wre, moe_bre=moe_bre, moe_w1=moe_w1, moe_w3=moe_w3, moe_w2=moe_w2)
    Bp = x_prompt.shape[0]
    z_hg = jnp.zeros((N_A, Bp, HG_HEADS, HG_DK, HG_DV), F32)
    z_c = jnp.zeros((N_B, Bp, ML_HEADS, ML_DH, ML_DH), F32)
    z_n = jnp.zeros((N_B, Bp, ML_HEADS, ML_DH), F32)
    z_m = jnp.zeros((N_B, Bp, ML_HEADS), F32)
    z_conv = jnp.zeros((N_B, Bp, ML_CONV - 1, ML_INNER), x_prompt.dtype)
    y_prompt, hg_p, mc_p, mn_p, mm_p, conv_p = trunk(x_prompt, c_prompt, z_hg, z_c, z_n, z_m, z_conv, p)
    y_sample, hg_s, mc_s, mn_s, mm_s, conv_s = trunk(x_sample, c_sample, state_hgrn, state_mlstm_c, state_mlstm_n,
                                                     state_mlstm_m, state_conv, p)
    return (y_prompt, y_sample, hg_p, mc_p, mn_p, mm_p, conv_p, hg_s, mc_s, mn_s, mm_s, conv_s)


_drawn_inputs = setup_inputs


def setup_inputs(seed=0):
    import zlib

    import numpy as np

    out = dict(_drawn_inputs(seed))
    spreads = {}
    factors = {'state_hgrn': 5.888,
     'final_g': 8.303,
     'hg_norm': 4.87,
     'ml_norm': 27.678,
     'ml_skip': 40.02,
     'moe_brg': 3.302,
     'moe_bre': 24.595}
    for name, (base, spread) in spreads.items():
        noise = np.random.default_rng([zlib.crc32(name.encode()), seed]).standard_normal(out[name].shape)
        drawn = base * np.exp(spread * noise) if base else spread * noise
        out[name] = __import__('jax').numpy.asarray(drawn.astype(out[name].dtype))
    for name, factor in factors.items():
        out[name] = (out[name] * factor).astype(out[name].dtype)
    return out
```

```python
from contextlib import ExitStack, contextmanager

import numpy as np

import concourse.bass as bass
from concourse import mybir

F32 = mybir.dt.float32
ALU = mybir.AluOpType
ACT = mybir.ActivationFunctionType
AX = mybir.AxisListType

P = 128
D = 1024
DC = D // P
TP = 512
NB, TS = 8, 8
T = TP + NB * TS
TH = T // 2
TJ = 5
NV = NB + 1
H = 8
BLK = 32
MI = 2048
MT = MI // P
MH = 4
MD = MI // MH
HT = MD // P
G, E, NE, FF = 4, 4, 16, 256
FT = FF // P
HIDT = NE * FT
EPS = 1e-6
BIG = 1e30
CLAMP = 60.0
LAYERS = 2

R = 8
SLOT = 1024
N_ADA = 6 * D // 512 * 4
N_HG, N_WO = 4 * H, DC
N_UPGATE, N_DOWN = NE * FT * 2, DC * HIDT // 8
N_XM, N_Z, N_MD = MT, MT, DC * MT // 8
SLOTS = {}
_at = 0
for _name, _n in (("ada0", N_ADA), ("hg", N_HG), ("wo", N_WO), ("up0", N_UPGATE), ("down0", N_DOWN),
                  ("ada1", N_ADA), ("xm", N_XM), ("z", N_Z), ("md", N_MD), ("up1", N_UPGATE),
                  ("down1", N_DOWN)):
    SLOTS[_name] = _at
    _at += _n
NSLOT = _at
USES = {}
_at = 0
N_HEADB = 26
for _name, _n in (("ada0", 12), ("hg", 4 * H), ("wo", DC), ("up0", 4 * NE), ("down0", DC), ("ada1", 12),
                  ("xm", MT), ("b", N_HEADB * MH), ("md", DC), ("up1", 4 * NE), ("down1", DC)):
    USES[_name] = _at
    _at += _n


def offsets(spec):
    at, out = 0, {}
    for name, n in spec:
        out[name] = (at, n)
        at += n
    return out, at


COLS, NCOL = offsets([
    ("c", DC * NV), ("bada", LAYERS * 48), ("ng", LAYERS * 2 * DC), ("fg", DC), ("hgn", 1), ("lb", 3 * H),
    ("cw", 4 * MT), ("cb", MT), ("wE", 3 * MT * 4), ("mln", MT), ("skip", MT), ("wr", LAYERS * DC * 20),
    ("rb", LAYERS), ("n0", MT * NB), ("big", 1), ("bfg", 1), ("m0", NB),
    ("ident", P), ("ones", P), ("causal", P), ("causal_s", 64), ("own", NB), ("keep", T), ("whole", T),
    ("rank", 4), ("bd", 32), ("eps", 1)])


class Signal:

    def __init__(self, sem):
        self.sem, self.base, self.n = sem, 0, 0

    def on(self, ins):
        ins.then_inc(self.sem, 1)
        self.n += 1

    def link(self, eng, ins):
        self.on(ins)
        eng.wait_ge(self.sem, self.base + self.n)


@contextmanager
def looped(eng, n, per):
    kept = {s: s.base + s.n for s in per}
    with eng.Fori(0, n) as i:
        for s, k in per.items():
            s.base, s.n = kept[s] + i * k, 0
        yield i
    for s, k in per.items():
        assert s.n == k, f"a signal is raised {s.n} times in a pass, not {k}"
        s.base, s.n = kept[s] + n * k, 0


def build(nc, io):
    with ExitStack() as ctx:
        def sb(name, *dims):
            return ctx.enter_context(nc.sbuf_tensor(name, [P, int(np.prod(dims))], F32))

        def sem(name):
            return ctx.enter_context(nc.semaphore(name))

        def shaped(ap, *dims):
            if len(dims) == 1:
                return ap
            names = "abcd"[:len(dims)]
            return ap.rearrange(f"p ({' '.join(names)}) -> p {' '.join(names)}", **dict(zip(names, dims)))

        ring = shaped(sb("ring", R * SLOT)[:, :], R, SLOT)
        xT = shaped(sb("xT", DC * T)[:, :], DC, T)
        hT = shaped(sb("hT", DC * T)[:, :], DC, T)
        cols = sb("cols", NCOL)
        modt = shaped(sb("modt", 48 * NV)[:, :], 48, NV)
        amod = shaped(sb("amod", 2 * DC * NV)[:, :], 2, DC, NV)
        ARENA = 32504
        arena = sb("arena", ARENA)
        ps = ctx.enter_context(nc.psum_tensor("ps", [P, 8, 512], F32))

        def col(name, *dims):
            at, n = COLS[name]
            return shaped(cols[:, at:at + n], *dims) if dims else cols[:, at:at + n]

        def carve(spec, start=0):
            at, out = start, {}
            for name, *dims in spec:
                n = int(np.prod(dims))
                out[name] = shaped(arena[:, at:at + n], *dims)
                at += n
            assert at <= ARENA, at
            return out, at

        ident, ones, keep = col("ident"), col("ones"), col("keep")
        causal, causal_s, own = col("causal"), col("causal_s"), col("own")
        eps = col("eps")

        ada, _ = carve([("modrow", 6 * D)])
        silc = shaped(sb("silc", DC * NV)[:, :], DC, NV)
        rstd = arena[:, 24000:24000 + T]
        hg, _ = carve([
            ("og", H, T), ("S0", 2, NB * P), ("Vx", NB, P), ("th", 2, T), ("q", 2, T), ("zg", 2, T),
            ("v", 2, TJ * P), ("k", T), ("g", T), ("b", T), ("eq", T), ("K", 16, P), ("Ks", 64),
            ("qe", T), ("kw", T), ("at", TJ, P), ("ktw", TJ, P), ("S", 4, P), ("sq", T),
            ("rs", T), ("Sn", NB, P), ("half", H), ("low", H), ("t1", 3, H), ("t2", H)])
        mo, _ = carve([
            ("hid", HIDT, T), ("sil", T), ("tmp", T), ("cb", 2, T), ("ce", T), ("lgT", T), ("combT", T),
            ("lg", TJ, 20), ("r1", TJ, 4), ("r2", TJ, 4), ("r3", TJ, 4), ("oh1", TJ, 4), ("oh2", TJ, 4),
            ("s1", TJ), ("s2", TJ), ("s3", TJ), ("s4", TJ), ("ps", TJ), ("ohg", TJ, 4), ("sel", TJ, 4, 4),
            ("comb", TJ, 4, 4)])
        ml, _ = carve([
            ("vtok", TJ, MI), ("xc", MT, T), ("q", HT, T), ("kz", HT, T), ("ktok", TJ, MD),
            ("C", 2, HT * MD), ("W", 2, 512), ("rows", T), ("nout", MT, NV), ("utok", TJ, MH),
            ("wtok", TJ, MH)])
        c_at = TJ * MI + MT * T + 2 * HT * T + TJ * MD
        first, first_end = carve([
            ("xpad", 2, 3 + TP + NB * 11), ("xs", 2, 64), ("acc", T), ("bdv", 2, P), ("gx", 2, 64),
            ("gm", 2, 64), ("wg", 3, MT, 8, 4), ("conv0", MT, 3 * NB), ("pr", 8, 4), ("pr2", 8, 4),
            ("convout", MT, 3 * NV)], c_at)
        assert first_end <= c_at + 2 * HT * MD + 1024
        gate, gate_end = carve([("ig", T), ("b", T), ("u", T), ("t1", T), ("t2", T), ("cut", T)], c_at)
        assert gate_end <= first_end - MT * 3 * NV
        x_flat = xT.rearrange("p a b -> p (a b)")
        mx, at = {}, 0
        for name, *dims in (("P0", 512), ("P1", 384), ("P2", 256), ("P3", 128), ("Ps", 64), ("kb", 512),
                            ("mu", T), ("rs", T), ("emn", T), ("nM", T), ("qw", HT, 64), ("wcb", 64)):
            n = int(np.prod(dims))
            mx[name] = shaped(x_flat[:, at:at + n], *dims)
            at += n
        assert at <= DC * T
        slot_full = [sem(f"slot_full{r}") for r in range(R)]
        pair_free = [Signal(sem(f"pair_free{p}")) for p in range(2)]
        small_in, x_in, conv_in, x_kept, x_back, out_done, sn_out, c_out = (
            sem(n) for n in ("small_in", "x_in", "conv_in", "x_kept", "x_back", "out_done", "sn_out", "c_out"))
        s0_in, c_in, cp_out = ([sem(f"{n}{u}") for u in range(2)] for n in ("s0_in", "c_in", "cp_out"))
        names = (
            "dve act num_full lb_in lb_out conv_acc rsh_ready slot_used silc turned mod_ready sq_ready ss_ready rstd_ready h_ready x_tile y_ready "
            "zf_read heads_in decay f_ready diffs exps elem_ready scored scored_s at_ready upd upd_s vx_ready s_ready "
            "o_full o_read sq_head head_ss head_rs head_done sn_ready "
            "lgT_full lg_ready lg_turned top_in top_out comb_ready combT_full combT_ready ce_ready cb_full "
            "cb_ready sil_ready hid_ready g_ready xm_ready bdv_ready xc_ready v_full v_read gates_full "
            "conv_done abs_ready soft_ready dec_ready dec_exp rows_ready turned_g tok_ready gates_read "
            "bd_ready b_full b_read kt_full kt_read s_full w_ready w_exp p_ready qw_ready kb_ready num_s "
            "upd_c c_done cp_full cp_ready n_ready hc_ready mu_full sqh_ready var_full ho_ready "
            "z_ready rs_h x_done_b").split()
        s = {n: Signal(sem(n)) for n in names}
        wstream, out = io["wstream"], io["out"]

        block = ctx.enter_context(nc.Block())

        @block.sync
        def _(sp):
            sp.dma_start(cols[:, :], io["cols"]).then_inc(small_in, 16)
            for r in range(R):
                sp.dma_start(ring[:, r, :], wstream[r]).then_inc(slot_full[r], 16)
            sp.dma_start(xT, io["xT"]).then_inc(x_in, 16)
            with sp.Fori(1, NSLOT // R) as i:
                for r in range(R):
                    sp.wait_ge(s["slot_used"].sem, R * i + (r + 1 - R))
                    sp.dma_start(ring[:, r, :], wstream[bass.ds(R * i + r, 1)].rearrange("a p n -> p (a n)")
                                 ).then_inc(slot_full[r], 16)

        @block.gpsimd
        def _(pool):
            pool.wait_ge(s["turned"].sem, 1)
            for h in range(2):
                pool.dma_start(hg["S0"][:, h, :], io["hg0"][h]).then_inc(s0_in[h], 16)
            def states_out(h):
                pool.wait_ge(s["sn_ready"].sem, h + 1)
                pool.dma_start(out["hg_s"][bass.ds(h, 1)].rearrange("a p n -> p (a n)"),
                               hg["Sn"].rearrange("p a b -> p (a b)")).then_inc(sn_out, 16)
                pool.dma_start(out["hg_p"][bass.ds(h, 1)].rearrange("a p n -> p (a n)"),
                               hg["S"][:, 3, :]).then_inc(sn_out, 16)

            with pool.Fori(0, H // 2 - 1) as i:
                for u in range(2):
                    states_out(2 * i + u)
                    pool.wait_ge(s["head_done"].sem, 2 * i + u + 1)
                    pool.dma_start(hg["S0"][:, u, :], io["hg0"][bass.ds(2 * i + u + 2, 1)].rearrange(
                        "a p n -> p (a n)")).then_inc(s0_in[u], 16)
            for h in range(H - 2, H):
                states_out(h)
            pool.wait_ge(s["x_tile"].sem, 2 * DC)
            pool.dma_start(first["wg"].rearrange("p a b c d -> p (a b c d)"), io["wg"]).then_inc(conv_in, 16)
            pool.dma_start(first["conv0"].rearrange("p a b -> p (a b)"), io["conv0"]).then_inc(conv_in, 16)
            pool.wait_ge(s["h_ready"].sem, 3)
            pool.dma_start(io["x_dram"], xT).then_inc(x_kept, 16)
            pool.wait_ge(s["conv_done"].sem, 1)
            pool.dma_start(out["conv"], first["convout"].rearrange("p a b -> p (a b)")).then_inc(out_done, 16)
            pool.wait_ge(s["rows_ready"].sem, 1)
            pool.dma_start(out["mm"], gate["t2"][0:MH, 0:NV]).then_inc(out_done, 16)
            pool.wait_ge(out_done, 32)
            pool.wait_ge(s["turned_g"].sem, 1)
            for n in range(2):
                pool.dma_start(ml["C"][:, n, :], io["c0"][n]).then_inc(c_in[n], 16)
            for h in range(MH):
                for b in range(NB):
                    n = NB * h + b
                    pool.wait_ge(s["c_done"].sem, HT * (n + 1))
                    pool.dma_start(out["mc_s"][n], ml["C"][:, n % 2, :]).then_inc(c_out, 16)
                    if n + 2 < NB * MH:
                        pool.wait_ge(c_out, 16 * (n + 1))
                        pool.dma_start(ml["C"][:, n % 2, :], io["c0"][n + 2]).then_inc(c_in[n % 2], 16)
                for kt in range(HT):
                    pool.wait_ge(s["cp_ready"].sem, HT * h + kt + 1)
                    pool.dma_start(out["mc_p"][h, kt], ml["W"][:, kt % 2, :]).then_inc(cp_out[kt % 2], 16)
            pool.wait_ge(s["n_ready"].sem, MH)
            pool.dma_start(out["mn"], ml["nout"].rearrange("p a b -> p (a b)")).then_inc(out_done, 16)
            pool.wait_ge(s["ho_ready"].sem, MH)
            pool.dma_start(xT, io["x_dram"]).then_inc(x_back, 16)
            pool.wait_ge(s["y_ready"].sem, 1)
            pool.dma_start(out["y"], hT).then_inc(out_done, 16)
            pool.wait_ge(out_done, 64)
            pool.wait_ge(sn_out, 32 * H)
            pool.wait_ge(c_out, 16 * NB * MH)
            for u in range(2):
                pool.wait_ge(cp_out[u], 16 * MH * HT // 2)

        @block.tensor
        def _(pe):
            used = s["slot_used"]

            def feature_tile(phase, turn, rs, p, freed, rhs, nk):
                pe.wait_ge(pair_free[p].sem, freed)
                for si, r in enumerate(rs):
                    pe.wait_ge(slot_full[r], 16 * (turn + 1))
                    for c in range(8):
                        k = 8 * si + c
                        for half in range(2):
                            mm = pe.matmul(ps[:, 2 * p + half, 0:TH], ring[:, r, c * P:(c + 1) * P],
                                           rhs(k)[:, TH * half:TH * (half + 1)], start=(k == 0), stop=(k == nk - 1))
                    used.on(mm)

            def h_rhs(k):
                return hT[:, k, :]

            def wide(banks, lhs, rhs, last=True):
                n = len(lhs)
                for k in range(n):
                    for half in range(2):
                        mm = pe.matmul(ps[:, banks[half], 0:TH], lhs[k], rhs[k][:, TH * half:TH * (half + 1)],
                                       start=(k == 0), stop=(k == n - 1))
                return mm

            def ada_rows(layer):
                if layer == 0:
                    pe.wait_ge(small_in, 16)
                pe.wait_ge(s["silc"].sem, 1)
                base, ub = SLOTS[f"ada{layer}"] // R, USES[f"ada{layer}"] // 2
                with looped(pe, 6, {used: R}) as i:
                    for p in range(2):
                        pe.wait_ge(pair_free[p].sem, i + ub)
                        for si in range(4):
                            r = 4 * p + si
                            pe.wait_ge(slot_full[r], 16 * (i + base + 1))
                            for kk in range(2):
                                mm = pe.matmul(ps[0:NV, 2 * p, :], silc[:, 2 * si + kk, :],
                                               ring[:, r, kk * 512:(kk + 1) * 512],
                                               start=(si + kk == 0), stop=(si == 3 and kk == 1))
                            used.on(mm)
                for p in range(2):
                    pe.wait_ge(pair_free[p].sem, ub + 6)
                for j in range(48):
                    mm = pe.transpose(ps[:, 4, NV * j:NV * (j + 1)], ada["modrow"][0:NV, P * j:P * (j + 1)],
                                      ident[0:NV, 0:NV])
                s["turned"].on(mm)

            def norm_sums(n):
                for c in range(DC):
                    pe.wait_ge(s["sq_ready"].sem, DC * n + c + 1)
                    for half in range(2):
                        mm = pe.matmul(ps[:, 6 + half, 0:TH], ones, hT[:, c, TH * half:TH * (half + 1)],
                                       start=(c == 0), stop=(c == DC - 1))
                s["ss_ready"].on(mm)
                if n < 2 * LAYERS:
                    pe.wait_ge(s["h_ready"].sem, n + 1)

            ada_rows(0)
            pe.wait_ge(x_in, 16)
            norm_sums(0)

            sh, uh = SLOTS["hg"] // R, USES["hg"] // 2

            def project(u, i):
                for q in range(3):
                    feature_tile("hg", i + sh, [4 * u + q], q % 2, 4 * i + (uh + 2 * u + q // 2), h_rhs, DC)
                pe.wait_ge(pair_free[1].sem, 4 * i + (uh + 2 * u + 1))
                pe.wait_ge(slot_full[4 * u + 3], 16 * (i + sh + 1))
                for j in range(TJ):
                    m = P if j < 4 else 64
                    dst = ps[:, 2, P * j:P * (j + 1)] if j < 4 else ps[0:64, 3, 0:P]
                    for c in range(DC):
                        mm = pe.matmul(dst, hT[:, c, P * j:P * j + m], ring[:, 4 * u + 3, c * P:(c + 1) * P],
                                       start=(c == 0), stop=(c == DC - 1))
                used.on(mm)

            def scan(u, pair):
                h = 2 * pair + u
                v = shaped(hg["v"][:, u, :], TJ, P)
                pe.wait_ge(s["elem_ready"].sem, h + 1)
                pe.wait_ge(pair_free[1].sem, 2 * h + (uh + 2))
                pe.wait_ge(s["head_rs"].sem, h)
                for c in range(4):
                    for i in range(4):
                        at = c * P + i * BLK
                        pe.matmul(ps[:, 4, at:at + BLK], hg["K"][:, 4 * c + i, :], hg["eq"][:, at:at + BLK],
                                  start=True, stop=True)
                for c in range(4):
                    mm = pe.transpose(ps[:, 6, c * P:(c + 1) * P], hg["kw"][:, c * P:(c + 1) * P], ident)
                s["scored"].on(mm)
                pe.matmul(ps[0:64, 5, 0:64], hg["Ks"], hg["eq"][:, TP:T], start=True, stop=True)
                s["scored_s"].on(pe.transpose(ps[0:64, 5, P:2 * P], hg["kw"][:, TP:T], ident))
                pe.wait_ge(s["at_ready"].sem, 2 * h + 2)
                for c in range(4):
                    mm = pe.matmul(ps[:, 7, c * P:(c + 1) * P], hg["ktw"][:, c, :], v[:, c, :], start=True, stop=True)
                s["upd"].on(mm)
                pe.wait_ge(s["vx_ready"].sem, h + 1)
                for half in range(2):
                    mm = pe.matmul(ps[:, 4 + 2 * half, :], hg["ktw"][0:64, 4, :],
                                   hg["Vx"].rearrange("p a b -> p (a b)")[0:64, 512 * half:512 * (half + 1)],
                                   start=True, stop=True)
                s["upd_s"].on(mm)
                for c in range(4):
                    mm = pe.matmul(ps[:, 5, c * P:(c + 1) * P], v[:, c, :], hg["at"][:, c, :], start=True,
                                   stop=(c == 0))
                    if c:
                        pe.wait_ge(s["s_ready"].sem, 4 * h + c)
                        mm = pe.matmul(ps[:, 5, c * P:(c + 1) * P], hg["S"][:, c - 1, :],
                                       hg["qe"][:, c * P:(c + 1) * P], start=False, stop=True)
                s["o_full"].on(mm)
                pe.wait_ge(s["s_ready"].sem, 4 * h + 4)
                pe.wait_ge(s0_in[u], 16 * (pair + 1))
                for b in range(NB):
                    pe.matmul(ps[:, 7, TS * b:TS * (b + 1)], hg["S0"][:, u, P * b:P * (b + 1)],
                              hg["qe"][:, TP + TS * b:TP + TS * (b + 1)], start=(b == 0), stop=False,
                              skip_group_check=True)
                mm = pe.matmul(ps[:, 7, 0:64], v[0:64, 4, :], hg["at"][0:64, 4, 0:64], start=False, stop=True,
                               skip_group_check=True)
                s["o_full"].on(mm)
                pe.wait_ge(s["sq_head"].sem, 2 * h + 2)
                pe.wait_ge(s["o_read"].sem, 2 * h + 2)
                s["head_ss"].on(wide((5, 7), [ones], [hg["sq"]]))

            project(0, 0)
            per = {used: 8, s["scored"]: 2, s["scored_s"]: 2, s["upd"]: 2, s["upd_s"]: 2, s["o_full"]: 4,
                   s["head_ss"]: 2}
            with looped(pe, H // 2 - 1, per) as i:
                project(1, i)
                scan(0, i)
                project(0, i + 1)
                scan(1, i)
            project(1, H // 2 - 1)
            scan(0, H // 2 - 1)
            scan(1, H // 2 - 1)

            def out_proj(phase, nslot, rhs, nk):
                base, ub = SLOTS[phase], USES[phase]
                for m in range(DC):
                    n = base + m * nslot
                    feature_tile(phase, n // R, [(n + k) % R for k in range(nslot)], m % 2, (ub + m) // 2, rhs, nk)

            pe.wait_ge(s["head_done"].sem, H)
            out_proj("wo", 1, lambda k: hg["og"][:, k, :], DC)

            def moe(layer):
                nr = 2 * layer + 1
                norm_sums(nr)
                wr = col("wr", LAYERS, DC, 20)
                for c in range(DC):
                    for half in range(2):
                        mm = pe.matmul(ps[0:20, 6 + half, 0:TH], wr[:, layer, c, :], hT[:, c, TH * half:TH * (half + 1)],
                                       start=(c == 0), stop=(c == DC - 1))
                s["lgT_full"].on(mm)
                pe.wait_ge(s["lg_ready"].sem, layer + 1)
                for j in range(TJ):
                    m = P if j < 4 else 64
                    mm = pe.transpose(ps[0:m, 4, 20 * j:20 * (j + 1)], mo["lgT"][0:20, P * j:P * j + m], ident[0:20, 0:20])
                s["lg_turned"].on(mm)
                pe.wait_ge(s["comb_ready"].sem, layer + 1)
                for j in range(TJ):
                    m = P if j < 4 else 64
                    dst = ps[0:NE, 6, P * j:P * j + m] if j < 4 else ps[0:NE, 7, 0:64]
                    mm = pe.transpose(dst, mo["comb"].rearrange("p j a b -> p j (a b)")[0:m, j, :], ident[0:m, 0:m])
                s["combT_full"].on(mm)
                pe.wait_ge(s["combT_ready"].sem, layer + 1)
                base, ub = SLOTS[f"up{layer}"] // R, USES[f"up{layer}"] // 2
                with looped(pe, NE // 2, {used: 8, s["cb_full"]: 2}) as i:
                    for u in range(2):
                        e = 2 * i + u
                        pe.wait_ge(s["ce_ready"].sem, e + (NE * layer + 1))
                        pe.wait_ge(s["cb_ready"].sem, e + NE * layer)
                        s["cb_full"].on(wide((4, 5), [ones[0:NE, :]], [mo["ce"][0:NE, :]]))
                        for f in range(FT):
                            for p in range(2):
                                feature_tile("up", i + base, [4 * u + 2 * f + p], p, 4 * i + (ub + 2 * u + f), h_rhs, DC)
                pe.wait_ge(s["hid_ready"].sem, HIDT * (layer + 1))
                out_proj(f"down{layer}", HIDT // 8, lambda k: mo["hid"][:, k, :], HIDT)

            moe(0)
            ada_rows(1)
            norm_sums(2)

            sx, ux = SLOTS["xm"] // R, USES["xm"] // 2

            def values_and_gates(j, k):
                u, i = k % 2, 8 * j + k
                pe.wait_ge(s["bdv_ready"].sem, i + 1)
                pe.wait_ge(s["xm_ready"].sem, 3 * i + 3)
                pe.wait_ge(pair_free[u].sem, ux + i // 2 + 1)
                pe.wait_ge(s["v_read"].sem, i)
                for t in range(4):
                    pe.matmul(ps[:, 4, P * t:P * (t + 1)], first["xpad"][:, u, 3 + P * t:3 + P * (t + 1)],
                              first["bdv"][:, u, :], start=True, stop=True)
                mm = pe.matmul(ps[0:64, 5, 0:P], first["xs"][:, u, :], first["bdv"][:, u, :], start=True, stop=True)
                s["v_full"].on(mm)
                pe.wait_ge(s["xc_ready"].sem, i + 1)
                return i, u, ml["xc"][:, i, :]

            def gates(j, k, start, stop):
                i, u, xc_i = values_and_gates(j, k)
                gm, gx = first["gm"][:, u, :], first["gx"][:, u, :]
                pe.matmul(ps[0:64, 6, 0:TP], gm, first["xpad"][:, u, 3:3 + TP], start=start, stop=False)
                pe.matmul(ps[0:64, 6, 0:TP], gx, xc_i[:, 0:TP], start=False, stop=stop)
                pe.matmul(ps[0:64, 7, 0:64], gm, first["xs"][:, u, :], start=start, stop=False)
                s["gates_full"].on(pe.matmul(ps[0:64, 7, 0:64], gx, xc_i[:, TP:T], start=False, stop=stop))

            for j in range(2):
                for k in range(8):
                    feature_tile("xm", sx + j, [k], k % 2, ux + 4 * j + k // 2, h_rhs, DC)
                    if k:
                        gates(j, k - 1, j == 0 and k == 1, False)
                gates(j, 7, False, j == 1)

            pe.wait_ge(s["rows_ready"].sem, 1)
            for n, src in enumerate((gate["u"], gate["t1"])):
                for j in range(TJ):
                    m = P if j < 4 else 64
                    mm = pe.transpose(ps[0:m, 4, 32 * n + MH * j:32 * n + MH * (j + 1)], src[0:MH, P * j:P * j + m],
                                      ident[0:MH, 0:MH])
            s["turned_g"].on(mm)
            pe.wait_ge(s["tok_ready"].sem, 2)

            ub = USES["b"]
            un = [ub]

            def use():
                n = un[0]
                un[0] += 1
                pe.wait_ge(pair_free[n % 2].sem, n // 2)
                return n % 2

            full = s["b_full"]
            W = [mx[f"P{j}"] for j in range(4)]
            bdq = ml["W"].rearrange("p a b -> p (a b)")
            for h in range(MH):
                hb = ub + N_HEADB * h
                for k in range(4):
                    p = use()
                    sel = ident[32 * k:32 * k + MH, 32 * k + h:32 * k + h + 1].broadcast_to([MH, P])
                    row = ml["rows"][32 * k:32 * k + MH, :]
                    if k < 3:
                        mm = wide((2 * p, 2 * p + 1), [sel], [row])
                    else:
                        mm = pe.matmul(ps[:, 2 * p, 0:64], sel, row[:, TP:T], start=True, stop=True)
                    full.on(mm)
                pe.wait_ge(s["bd_ready"].sem, h + 1)
                for w in range(2):
                    for i in range(HT):
                        p = use()
                        at = (HT * w + i) * P
                        full.on(wide((2 * p, 2 * p + 1), [bdq[:, at:at + P]], [ml["xc"][:, HT * h + i, :]]))
                pe.wait_ge(s["c_done"].sem, HT * NB * h)
                pe.wait_ge(s["cp_ready"].sem, HT * h)
                for j in range(TJ):
                    m = P if j < 4 else 64
                    bank = 4 + j if j < 4 else 2 * use()
                    for i in range(HT):
                        mm = pe.matmul(ps[0:m, bank, P * i:P * (i + 1)], ml["xc"][:, HT * h + i, P * j:P * j + m],
                                       bdq[:, (HT + i) * P:(HT + i + 1) * P], start=True, stop=True)
                s["kt_full"].on(mm)
                pe.wait_ge(pair_free[(hb + 12) % 2].sem, (hb + 12) // 2 + 1)
                for j in range(TJ):
                    m = P if j < 4 else 64
                    bank = 4 + j if j < 4 else 2 * use()
                    hi = TP if j < 4 else T
                    for p in range(2):
                        pe.wait_ge(pair_free[p].sem, (ub + N_HEADB * h + 12) // 2)
                    for i in range(HT):
                        mm = pe.matmul(ps[0:m, bank, 0:hi - P * j], ml["kz"][:, i, P * j:P * j + m],
                                       ml["q"][:, i, P * j:hi], start=(i == 0), stop=(i == HT - 1))
                s["s_full"].on(mm)
                pe.wait_ge(s["p_ready"].sem, 5 * h + 5)
                pe.wait_ge(s["qw_ready"].sem, h + 1)
                p = use()
                ns, dn = ps[:, 2 * p, 0:4 * 64], ps[:, 2 * p + 1, 0:64]
                pe.matmul(dn, ones[0:64, :], mx["Ps"][0:64, :], start=True, stop=False)
                qn = shaped(mx["kb"][:, 0:256], HT, 64)
                for i in range(HT):
                    mm = pe.matmul(dn, ones, qn[:, i, :], start=False, stop=(i == HT - 1))
                s["num_s"].on(mm)
                for b in range(NB):
                    n = NB * h + b
                    C = shaped(ml["C"][:, n % 2, :], HT, MD)
                    pe.wait_ge(c_in[n % 2], 16 * (n // 2 + 1))
                    for i in range(HT):
                        for k in range(HT):
                            mm = pe.matmul(ns[:, 64 * i + TS * b:64 * i + TS * (b + 1)], C[:, k, P * i:P * (i + 1)],
                                           mx["qw"][:, k, TS * b:TS * (b + 1)], start=(b == 0 and i == 0 and k == 0),
                                           stop=False, skip_group_check=True)
                    s["num_s"].on(mm)
                    pe.wait_ge(s["kb_ready"].sem, n + 1)
                    for k in range(HT):
                        pe.wait_ge(s["c_done"].sem, HT * n)
                        mm = pe.matmul(ps[:, 4 + k, :], mx["kb"][0:64, P * k:P * (k + 1)],
                                       ml["vtok"][0:64, 4, MD * h:MD * (h + 1)], start=True, stop=True)
                        s["upd_c"].on(mm)
                for i in range(HT):
                    mm = pe.matmul(ns[:, 64 * i:64 * (i + 1)],
                                   ml["vtok"][0:64, 4, MD * h + P * i:MD * h + P * (i + 1)], mx["Ps"][0:64, :],
                                   start=False, stop=True, skip_group_check=True)
                s["num_full"].on(mm)
                pe.wait_ge(s["c_done"].sem, HT * NB * (h + 1))
                for k in range(HT):
                    for j in range(4):
                        mm = pe.matmul(ps[:, 4 + k, :], ml["ktok"][:, j, P * k:P * (k + 1)],
                                       ml["vtok"][:, j, MD * h:MD * (h + 1)], start=(j == 0), stop=(j == 3))
                    s["cp_full"].on(mm)
                for i in range(HT + 1):
                    p = use()
                    for j in range(4):
                        lhs = ones if i == 0 else ml["vtok"][:, j, MD * h + P * (i - 1):MD * h + P * i]
                        mm = pe.matmul(ps[:, 2 * p, P * j:TP], lhs, W[j], start=(j == 0), stop=(j == 3),
                                       skip_group_check=True)
                    full.on(mm)
                for i in range(HT):
                    n = SLOTS["z"] + HT * h + i
                    m = un[0]
                    un[0] += 1
                    feature_tile("z", n // R, [n % R], m % 2, m // 2, h_rhs, DC)
                pe.wait_ge(pair_free[(hb + 19) % 2].sem, (hb + 19) // 2 + 1)
                p = use()
                s["mu_full"].on(wide((2 * p, 2 * p + 1), [ones] * HT, [ml["q"][:, i, :] for i in range(HT)]))
                pe.wait_ge(s["sqh_ready"].sem, h + 1)
                p = use()
                sqh = shaped(ml["ktok"].rearrange("p a b -> p (a b)")[:, 0:HT * T], HT, T)
                s["var_full"].on(wide((2 * p, 2 * p + 1), [ones] * HT, [sqh[:, i, :] for i in range(HT)]))
            assert un[0] == USES["md"], (un[0], USES["md"])
            pe.wait_ge(s["ho_ready"].sem, MH)
            out_proj("md", 2, lambda k: ml["xc"][:, k, :], MT)
            moe(1)
            norm_sums(4)

        def halves(p):
            return ps[:, 2 * p:2 * p + 2, 0:TH]

        def two(ap):
            return ap.rearrange("p (a n) -> p a n", a=2)

        def at(tensor, i):
            return tensor[:, i] if isinstance(i, int) else tensor[:, bass.ds(i, 1)].rearrange(
                "p a n -> p (a n)")

        KS = float(MD) ** -0.5

        @block.scalar
        def _(act):
            A = s["act"]
            used = s["slot_used"].sem

            def norm(n):
                for c in range(DC):
                    if n:
                        act.wait_ge(s["x_tile"].sem, DC * (n - 1) + c + 1)
                    s["sq_ready"].on(act.activation(hT[:, c, :], xT[:, c, :], ACT.Square))
                act.wait_ge(s["ss_ready"].sem, n + 1)
                A.link(act, act.activation(two(rstd), halves(3), ACT.Ln, bias=eps, scale=1.0 / D))
                s["rstd_ready"].on(act.activation(rstd, rstd, ACT.Exp, scale=-0.5))

            def ada_rows(layer):
                base, ub = SLOTS[f"ada{layer}"], USES[f"ada{layer}"] // 2
                with looped(act, 6, {}) as i:
                    for p in range(2):
                        act.wait_ge(used, R * i + (base + 4 * (p + 1)))
                        dst = ada["modrow"][0:NV, bass.ds((2 * i + p) * 512, 512)]
                        pair_free[p].on(act.copy(dst, ps[0:NV, 2 * p, :]))

            act.wait_ge(small_in, 16)
            s["silc"].on(act.activation(silc, col("c", DC, NV), ACT.Silu))
            ada_rows(0)
            act.wait_ge(x_in, 16)
            norm(0)

            act.wait_ge(s["lb_in"].sem, 1)
            s["lb_out"].on(act.activation(hg["t1"], hg["t1"], ACT.Exp))
            base = SLOTS["hg"]

            def evict(u, h, guarded):
                if guarded:
                    act.wait_ge(s["head_done"].sem, h - 1)
                for q, (dst, f, k) in enumerate(((hg["th"], ACT.Tanh, 0.5), (hg["q"], ACT.Silu, 1.0),
                                                 (hg["zg"], ACT.Silu, 1.0))):
                    act.wait_ge(used, 4 * h + (base + q + 1))
                    pair_free[q % 2].on(act.activation(two(dst[:, u, :]), halves(q % 2), f, scale=k))
                act.wait_ge(used, 4 * h + (base + 4))
                act.copy(hg["v"][:, u, 0:512], ps[:, 2, :])
                pair_free[1].on(act.copy(hg["v"][0:64, u, 512:512 + P], ps[0:64, 3, 0:P]))

            def exponentials(h):
                act.wait_ge(s["decay"].sem, h + 1)
                s["f_ready"].on(act.activation(hg["g"], hg["g"], ACT.Ln))
                act.wait_ge(s["diffs"].sem, 3 * h + 1)
                A.link(act, act.activation(hg["Ks"], hg["eq"][:, TP:T], ACT.Exp, scale=-1.0))
                s["exps"].on(act.activation(hg["eq"], hg["eq"], ACT.Exp))
                act.wait_ge(s["diffs"].sem, 3 * h + 2)
                s["exps"].on(act.activation(hg["K"], hg["K"], ACT.Exp))
                act.wait_ge(s["diffs"].sem, 3 * h + 3)
                s["exps"].on(act.activation(hg["qe"], hg["b"], ACT.Exp))
                s["exps"].on(act.activation(hg["kw"], hg["kw"], ACT.Exp))

            def head_norm(h):
                act.wait_ge(s["o_read"].sem, 2 * h + 1)
                s["sq_head"].on(act.activation(hg["sq"][:, 0:TP], ps[:, 5, :], ACT.Square))
                act.wait_ge(s["o_read"].sem, 2 * h + 2)
                s["sq_head"].on(act.activation(hg["sq"][:, TP:T], ps[:, 7, 0:64], ACT.Square))
                act.wait_ge(s["head_ss"].sem, h + 1)
                act.activation(hg["rs"][:, 0:TH], ps[:, 5, 0:TH], ACT.Ln, bias=eps, scale=1.0 / P)
                A.link(act, act.activation(hg["rs"][:, TH:T], ps[:, 7, 0:TH], ACT.Ln, bias=eps, scale=1.0 / P))
                s["head_rs"].on(act.activation(hg["rs"], hg["rs"], ACT.Exp, scale=-0.5))

            evict(0, 0, False)
            exponentials(0)
            evict(1, 1, False)
            head_norm(0)
            per = {A: 4, s["f_ready"]: 2, s["exps"]: 8, s["sq_head"]: 4, s["head_rs"]: 2}
            with looped(act, H // 2 - 1, per) as i:
                for u in range(2):
                    h = 2 * i + (u + 1)
                    exponentials(h)
                    evict(u, h + 1, True)
                    head_norm(h)
            exponentials(H - 1)
            head_norm(H - 1)

            def moe(layer):
                norm(2 * layer + 1)
                act.wait_ge(s["lgT_full"].sem, layer + 1)
                act.wait_ge(sn_out, 32 * H)
                s["lg_ready"].on(act.activation(two(mo["lgT"][0:20, :]), ps[0:20, 6:8, 0:TH], ACT.Identity,
                                                bias=col("rb")[0:20, layer:layer + 1]))
                act.wait_ge(s["top_in"].sem, layer + 1)
                A.link(act, act.activation(mo["r1"], mo["r1"], ACT.Exp))
                s["top_out"].on(act.activation(mo["s2"], mo["s2"], ACT.Exp))
                act.wait_ge(s["combT_full"].sem, layer + 1)
                A.link(act, act.copy(mo["combT"][0:NE, 0:TP], ps[0:NE, 6, :]))
                s["combT_ready"].on(act.copy(mo["combT"][0:NE, TP:T], ps[0:NE, 7, 0:64]))
                base, ub = SLOTS[f"up{layer}"], USES[f"up{layer}"] // 2
                with looped(act, NE // 2, {s["cb_ready"]: 2}) as i:
                    for u in range(2):
                        e = 2 * i + u
                        act.wait_ge(s["cb_full"].sem, e + (NE * layer + 1))
                        act.wait_ge(s["hid_ready"].sem, 2 * e + HIDT * layer)
                        s["cb_ready"].on(act.copy(two(mo["cb"][:, 0, :]), ps[:, 4:6, 0:TH]))
                        for f in range(FT):
                            act.wait_ge(used, 8 * i + (base + 4 * u + 2 * f + 1))
                            act.wait_ge(pair_free[1].sem, 4 * i + (ub + 2 * u + f))
                            pair_free[0].on(act.activation(two(mo["sil"]), halves(0), ACT.Silu))

            moe(0)
            ada_rows(1)
            norm(2)

            base = SLOTS["xm"]

            def inner(u, i, guarded):
                act.wait_ge(used, i + (base + 1))
                if guarded:
                    act.wait_ge(s["gates_full"].sem, i - 1)
                    act.wait_ge(s["conv_acc"].sem, i - 1)
                xp = first["xpad"][:, u, :]
                s["xm_ready"].on(act.copy(xp[:, 3:3 + TH], ps[:, 2 * u, 0:TH]))
                s["xm_ready"].on(act.copy(xp[:, 3 + TH:3 + TP], ps[:, 2 * u + 1, 0:TP - TH]))
                src = ps[:, 2 * u + 1, TP - TH:TH].rearrange("p (b t) -> p b t", b=NB)
                s["xm_ready"].on(act.copy(xp[:, 3 + TP:].rearrange("p (b t) -> p b t", b=NB)[:, :, 3:], src))
                pair_free[u].on(act.copy(first["xs"][:, u, :].rearrange("p (b t) -> p b t", b=NB), src))
                act.wait_ge(s["conv_acc"].sem, i + 1)
                s["xc_ready"].on(act.activation(at(ml["xc"], i), first["acc"], ACT.Silu))

            inner(0, 0, False)
            inner(1, 1, False)
            with looped(act, MT // 2 - 1, {s["xm_ready"]: 6, s["xc_ready"]: 2}) as i:
                for u in range(2):
                    inner(u, 2 * i + (u + 2), True)

            act.wait_ge(s["abs_ready"].sem, 1)
            t1, t2, gb = gate["t1"][0:MH, :], gate["t2"][0:MH, :], gate["b"][0:MH, :]
            A.link(act, act.activation(t2, t2, ACT.Exp, scale=-1.0))
            s["soft_ready"].on(act.activation(t2, t2, ACT.Ln, bias=ones[0:MH, 0:1]))
            act.wait_ge(s["dec_ready"].sem, 1)
            A.link(act, act.activation(t1, t1, ACT.Exp))
            s["dec_exp"].on(act.activation(gb[:, TP:T], gb[:, TP:T], ACT.Exp))

            act.wait_ge(x_kept, 16)
            un = [USES["b"]]

            def use(sem, value):
                n = un[0]
                un[0] += 1
                act.wait_ge(sem, value)
                return n % 2

            nf = [0]

            def read_full():
                nf[0] += 1
                return use(s["b_full"].sem, nf[0])

            for h in range(MH):
                act.wait_ge(s["ho_ready"].sem, h)
                p = read_full()
                pair_free[p].on(act.copy(two(mx["nM"]), halves(p)))
                p = read_full()
                pair_free[p].on(act.activation(two(mx["emn"]), halves(p), ACT.Exp, scale=-1.0))
                p = read_full()
                pair_free[p].on(act.copy(two(mx["mu"]), halves(p)))
                p = read_full()
                pair_free[p].on(act.copy(mx["wcb"], ps[:, 2 * p, 0:64]))
                for i in range(HT):
                    p = read_full()
                    pair_free[p].on(act.copy(two(ml["q"][:, i, :]), halves(p)))
                for i in range(HT):
                    p = read_full()
                    pair_free[p].on(act.activation(two(ml["kz"][:, i, :]), halves(p), ACT.Identity, scale=KS))
                un[0] += 2
                for j in range(TJ):
                    act.wait_ge(s["w_ready"].sem, 5 * h + j + 1)
                    n = TP - P * j if j < 4 else 64
                    w = ml["W"][:, j % 2, 0:n] if j < 4 else ml["W"][0:64, 0, 0:64]
                    s["w_exp"].on(act.activation(w, w, ACT.Exp))
                un[0] += 1
                act.wait_ge(s["num_s"].sem, 9 * h + 1)
                for b in range(NB):
                    n = NB * h + b
                    act.wait_ge(s["upd_c"].sem, HT * n)
                    s["kb_ready"].on(act.activation(mx["kb"][0:64, :], ml["ktok"][0:64, 4, :], ACT.Identity,
                                                    scale=own[0:64, b:b + 1]))
                for k in range(HT):
                    n = HT * h + k
                    act.wait_ge(s["cp_full"].sem, n + 1)
                    if n >= 2:
                        act.wait_ge(cp_out[k % 2], 16 * (n // 2))
                    s["cp_ready"].on(act.copy(ml["W"][:, k % 2, :], ps[:, 4 + k, :]))
                un[0] += 5
                nf[0] += 5
                act.wait_ge(s["n_ready"].sem, h + 1)
                for i in range(HT):
                    p = use(used, SLOTS["z"] + HT * h + i + 1)
                    pair_free[p].on(act.activation(two(ml["kz"][:, i, :]), halves(p), ACT.Silu))
                un[0] += 1
                act.wait_ge(s["rs_h"].sem, h + 1)
                sqh = shaped(ml["ktok"].rearrange("p a b -> p (a b)")[:, 0:HT * T], HT, T)
                s["sqh_ready"].on(act.activation(sqh, ml["q"], ACT.Square))
                n = un[0]
                p = use(s["var_full"].sem, h + 1)
                pair_free[p].on(act.activation(two(mx["rs"]), halves(p), ACT.Ln, bias=eps, scale=1.0 / MD))
                act.wait_ge(pair_free[p].sem, n // 2 + 1)
                s["rsh_ready"].on(act.activation(mx["rs"], mx["rs"], ACT.Exp, scale=-0.5))
            moe(1)
            norm(4)

        @block.vector
        def _(dve):
            V = s["dve"]
            used = s["slot_used"].sem
            tt, ts, stt = dve.tensor_tensor, dve.tensor_scalar, dve.scalar_tensor_tensor

            def over_t(ap):
                return ap.unsqueeze(len(ap.shape)).broadcast_to(list(ap.shape) + [TS])

            def by_seq(ap):
                return ap.rearrange("p (b t) -> p b t", b=NB)

            def modulation(layer):
                dve.wait_ge(s["turned"].sem, layer + 1)
                V.link(dve, tt(modt, shaped(ps[:, 4, 0:48 * NV], 48, NV),
                               col("bada", LAYERS, 48)[:, layer, :].unsqueeze(2).broadcast_to([P, 48, NV]), ALU.add))
                for k in range(2):
                    g = col("ng", LAYERS, 2, DC)[:, layer, k, :].unsqueeze(2).broadcast_to([P, DC, NV])
                    V.link(dve, stt(amod[:, k], modt[:, 24 * k + 8:24 * k + 16, :], 1.0, g, ALU.add, ALU.mult))

            def norm(n):
                k = n % 2
                dve.wait_ge(s["rstd_ready"].sem, n + 1)
                V.link(dve, tt(hT, xT, rstd.unsqueeze(1).broadcast_to([P, DC, T]), ALU.mult))
                if n == 2 * LAYERS:
                    for c in range(DC):
                        ins = ts(hT[:, c, :], hT[:, c, :], col("fg")[:, c:c + 1], None, ALU.mult)
                    s["y_ready"].on(ins)
                    return
                for c in range(DC):
                    ts(hT[:, c, 0:TP], hT[:, c, 0:TP], amod[:, k, c, 0:1], modt[:, 24 * k + c, 0:1], ALU.mult, ALU.add)
                hs = hT[:, :, TP:T].rearrange("p c (b t) -> p c b t", b=NB)
                V.link(dve, tt(hs, hs, over_t(amod[:, k, :, 1:NV]), ALU.mult))
                s["h_ready"].link(dve, tt(hs, hs, over_t(modt[:, 24 * k:24 * k + DC, 1:NV]), ALU.add))

            def gated(phase, nslot, k, tmp):
                base = SLOTS[phase]
                for m in range(DC):
                    p = m % 2
                    dve.wait_ge(used, base + (m + 1) * nslot)
                    g = modt[:, 24 * k + 16 + m, :]
                    stt(xT[:, m, 0:TH], ps[:, 2 * p, 0:TH], g[:, 0:1], xT[:, m, 0:TH], ALU.mult, ALU.add)
                    stt(xT[:, m, TH:TP], ps[:, 2 * p + 1, 0:TP - TH], g[:, 0:1], xT[:, m, TH:TP], ALU.mult, ALU.add)
                    pair_free[p].on(tt(by_seq(tmp), by_seq(ps[:, 2 * p + 1, TP - TH:TH]), over_t(g[:, 1:NV]), ALU.mult))
                    dve.wait_ge(pair_free[p].sem, (USES[phase] + m) // 2 + 1)
                    s["x_tile"].link(dve, tt(xT[:, m, TP:T], xT[:, m, TP:T], tmp, ALU.add))

            dve.wait_ge(small_in, 16)
            modulation(0)
            norm(0)
            lb = col("lb", 3, H)
            V.link(dve, tt(hg["t2"], lb[:, 0], lb[:, 1], ALU.max))
            V.link(dve, tt(hg["t2"], hg["t2"], lb[:, 2], ALU.max))
            s["lb_in"].on(tt(hg["t1"], lb, hg["t2"].unsqueeze(1).broadcast_to([P, 3, H]), ALU.subtract))
            dve.wait_ge(s["lb_out"].sem, 1)
            V.link(dve, tt(hg["t2"], hg["t1"][:, 0], hg["t1"][:, 1], ALU.add))
            V.link(dve, tt(hg["t2"], hg["t2"], hg["t1"][:, 2], ALU.add))
            V.link(dve, dve.reciprocal(hg["t2"], hg["t2"]))
            V.link(dve, tt(hg["t2"], hg["t1"][:, 0], hg["t2"], ALU.mult))
            V.link(dve, ts(hg["half"], hg["t2"], -0.5, 0.5, ALU.mult, ALU.add))
            V.link(dve, tt(hg["low"], hg["half"], hg["t2"], ALU.add))

            uh = USES["hg"] // 2

            def elementwise(u, h):
                th, q = hg["th"][:, u, :], hg["q"][:, u, :]
                k, g, b, eq, K, Ks, qe, kw = (hg[n] for n in ("k", "g", "b", "eq", "K", "Ks", "qe", "kw"))
                half = hg["half"][:, h:h + 1] if isinstance(h, int) else hg["half"][:, bass.ds(h, 1)]
                low = hg["low"][:, h:h + 1] if isinstance(h, int) else hg["low"][:, bass.ds(h, 1)]
                dve.wait_ge(pair_free[0].sem, 2 * h + (uh + 1))
                V.link(dve, ts(g, th, half, low, ALU.mult, ALU.add))
                s["decay"].link(dve, ts(k, g, -1.0, 1.0, ALU.mult, ALU.add))
                dve.wait_ge(s["f_ready"].sem, h + 1)
                V.link(dve, dve.tensor_tensor_scan(b, keep, g, 0.0, ALU.mult, ALU.add))
                b3 = b[:, 0:TP].rearrange("p (i t) -> p i t", t=BLK)
                mid = b3[:, :, BLK // 2]
                bs = by_seq(b[:, TP:T])
                tt(eq[:, 0:TP].rearrange("p (i t) -> p i t", t=BLK), b3,
                   mid.unsqueeze(2).broadcast_to([P, 16, BLK]), ALU.subtract)
                s["diffs"].on(tt(by_seq(eq[:, TP:T]), bs, over_t(bs[:, :, TS // 2]), ALU.subtract))
                V.link(dve, tt(K.rearrange("p (c i) t -> p c i t", c=4),
                               mid.rearrange("p (c i) -> p c i", c=4).unsqueeze(3).broadcast_to([P, 4, 4, P]),
                               b[:, 0:TP].rearrange("p (c t) -> p c t", c=4).unsqueeze(2).broadcast_to([P, 4, 4, P]),
                               ALU.subtract))
                s["diffs"].on(dve.tensor_scalar_min(K, K, CLAMP))
                bc = b[:, 0:TP].rearrange("p (c t) -> p c t", c=4)
                tt(kw[:, 0:TP].rearrange("p (c t) -> p c t", c=4),
                   bc[:, :, P - 1].unsqueeze(2).broadcast_to([P, 4, P]), bc, ALU.subtract)
                s["diffs"].on(tt(by_seq(kw[:, TP:T]), over_t(bs[:, :, TS - 1]), bs, ALU.subtract))
                dve.wait_ge(pair_free[1].sem, 2 * h + (uh + 1))
                dve.wait_ge(s["exps"].sem, 4 * h + 1)
                tt(eq, q, eq, ALU.mult)
                tt(Ks, k[:, TP:T], Ks, ALU.mult)
                dve.wait_ge(s["exps"].sem, 4 * h + 2)
                K4 = K.rearrange("p (c i) t -> p c i t", c=4)
                tt(K4, K4, k[:, 0:TP].rearrange("p (c t) -> p c t", c=4).unsqueeze(2).broadcast_to([P, 4, 4, P]),
                   ALU.mult)
                dve.wait_ge(s["exps"].sem, 4 * h + 4)
                el = hg["sq"][:, 0:12]
                tt(el[:, 0:4].unsqueeze(2), qe[:, 0:TP].rearrange("p (c t) -> p c t", c=4)[:, :, P - 1:P],
                   col("ones")[:, 0:4].unsqueeze(2), ALU.mult)
                V.link(dve, tt(el[:, 4:12].unsqueeze(2), by_seq(qe[:, TP:T])[:, :, TS - 1:TS],
                               col("ones")[:, 0:8].unsqueeze(2), ALU.mult))
                V.link(dve, dve.tensor_copy(hg["t1"].rearrange("p a b -> p (a b)")[:, 0:12], el))
                tt(qe, q, qe, ALU.mult)
                s["elem_ready"].on(tt(kw, k, kw, ALU.mult))

            def scan(u, pair):
                h = 2 * pair + u
                v = shaped(hg["v"][:, u, :], TJ, P)
                el = hg["t1"].rearrange("p a b -> p (a b)")
                dve.wait_ge(s["scored"].sem, h + 1)
                tt(hg["at"][:, 0:4, :], shaped(ps[:, 4, :], 4, P), causal.unsqueeze(1).broadcast_to([P, 4, P]), ALU.mult)
                s["at_ready"].on(dve.tensor_copy(hg["ktw"][:, 0:4, :], shaped(ps[:, 6, :], 4, P)))
                dve.wait_ge(s["scored_s"].sem, h + 1)
                tt(hg["at"][0:64, 4, 0:64], ps[0:64, 5, 0:64], causal_s[0:64, :], ALU.mult)
                s["at_ready"].on(dve.tensor_copy(hg["ktw"][0:64, 4, :], ps[0:64, 5, P:2 * P]))
                dve.wait_ge(pair_free[1].sem, 2 * h + (uh + 2))
                s["vx_ready"].on(tt(hg["Vx"][0:64], v[0:64, 4, :].unsqueeze(1).broadcast_to([64, NB, P]),
                                    own[0:64, :].unsqueeze(2).broadcast_to([64, NB, P]), ALU.mult))
                dve.wait_ge(s["upd"].sem, h + 1)
                dve.wait_ge(sn_out, 32 * h)
                s["s_ready"].link(dve, dve.tensor_copy(hg["S"][:, 0, :], ps[:, 7, 0:P]))
                for c in range(1, 4):
                    s["s_ready"].link(dve, stt(hg["S"][:, c, :], hg["S"][:, c - 1, :], el[:, c:c + 1],
                                               ps[:, 7, c * P:(c + 1) * P], ALU.mult, ALU.add))
                dve.wait_ge(s["upd_s"].sem, h + 1)
                dve.wait_ge(s0_in[u], 16 * (pair + 1))
                Sn = hg["Sn"]
                V.link(dve, tt(Sn, shaped(hg["S0"][:, u, :], NB, P), el[:, 4:12].unsqueeze(2).broadcast_to([P, NB, P]),
                               ALU.mult))
                Sn2 = Sn.rearrange("p (a b) n -> p a (b n)", a=2)
                tt(Sn2[:, 0], Sn2[:, 0], ps[:, 4, :], ALU.add)
                s["sn_ready"].on(tt(Sn2[:, 1], Sn2[:, 1], ps[:, 6, :], ALU.add))
                og = at(hg["og"], h)
                gn = col("hgn")
                dve.wait_ge(s["o_full"].sem, 2 * h + 1)
                s["o_read"].on(ts(og[:, 0:TP], ps[:, 5, :], gn, None, ALU.mult))
                dve.wait_ge(s["o_full"].sem, 2 * h + 2)
                s["o_read"].link(dve, ts(og[:, TP:T], ps[:, 7, 0:64], gn, None, ALU.mult))
                dve.wait_ge(s["head_rs"].sem, h + 1)
                V.link(dve, tt(og, og, hg["rs"], ALU.mult))
                dve.wait_ge(pair_free[0].sem, 2 * h + (uh + 2))
                s["head_done"].link(dve, tt(og, og, hg["zg"][:, u, :], ALU.mult))

            names = {"decay": 1, "diffs": 3, "elem_ready": 1, "at_ready": 2, "vx_ready": 1, "s_ready": 4,
                     "sn_ready": 1, "o_read": 2, "head_done": 1}
            per = {s[n]: 2 * k for n, k in names.items()} | {V: 2 * 7}
            with looped(dve, H // 2, per) as i:
                for u in range(2):
                    elementwise(u, 2 * i + u)
                    scan(u, i)
            gated("wo", 1, 0, hg["sq"][:, 0:64])

            def first_of(dst, eq, tmp, s1):
                rank = col("rank").unsqueeze(1).broadcast_to([P, TJ, 4])
                V.link(dve, tt(tmp, eq, rank, ALU.mult))
                V.link(dve, dve.tensor_reduce(s1, tmp, AX.X, ALU.max))
                V.link(dve, tt(dst, tmp, s1.unsqueeze(2).broadcast_to([P, TJ, 4]), ALU.is_equal))

            def moe(layer):
                norm(2 * layer + 1)
                lg, r1, r2, r3, s1, s2, s3, s4, pst = (mo[n] for n in "lg r1 r2 r3 s1 s2 s3 s4 ps".split())
                four = lambda ap: ap.unsqueeze(2).broadcast_to([P, TJ, 4])
                dve.wait_ge(sn_out, 32 * H)
                V.link(dve, dve.memset(lg, 0.0))
                dve.wait_ge(s["lg_turned"].sem, layer + 1)
                V.link(dve, dve.tensor_copy(lg[:, 0:4, :], shaped(ps[:, 4, 0:80], 4, 20)))
                V.link(dve, dve.tensor_copy(lg[0:64, 4, :], ps[0:64, 4, 80:100]))
                V.link(dve, dve.tensor_reduce(s1, lg[:, :, 0:4], AX.X, ALU.max))
                V.link(dve, tt(r1, lg[:, :, 0:4], four(s1), ALU.subtract))
                V.link(dve, ts(r2, r1, 0.0, None, ALU.is_equal))
                first_of(mo["ohg"], r2, r3, s3)
                el = lg[:, :, 4:20].rearrange("p j (g e) -> p j g e", g=G)
                for g in range(G):
                    oh = mo["ohg"][:, :, g:g + 1].broadcast_to([P, TJ, E])
                    V.link(dve, tt(mo["sel"][:, :, g, :], lg[:, :, 4 + E * g:4 + E * (g + 1)], oh, ALU.mult))
                V.link(dve, tt(r2, mo["sel"][:, :, 0, :], mo["sel"][:, :, 1, :], ALU.add))
                V.link(dve, tt(r2, r2, mo["sel"][:, :, 2, :], ALU.add))
                V.link(dve, tt(r2, r2, mo["sel"][:, :, 3, :], ALU.add))
                V.link(dve, dve.tensor_reduce(s1, r2, AX.X, ALU.max))
                V.link(dve, tt(r3, r2, four(s1), ALU.is_equal))
                first_of(mo["oh1"], r3, r3, s3)
                V.link(dve, stt(r2, mo["oh1"], -BIG, r2, ALU.mult, ALU.add))
                V.link(dve, dve.tensor_reduce(s4, r2, AX.X, ALU.max))
                V.link(dve, tt(r3, r2, four(s4), ALU.is_equal))
                first_of(mo["oh2"], r3, r3, s3)
                s["top_in"].on(tt(s2, s4, s1, ALU.subtract))
                dve.wait_ge(s["top_out"].sem, layer + 1)
                V.link(dve, dve.tensor_reduce(pst, r1, AX.X, ALU.add))
                V.link(dve, ts(s3, s2, 1.0, None, ALU.add))
                V.link(dve, tt(s3, s3, pst, ALU.mult))
                V.link(dve, dve.reciprocal(s3, s3))
                V.link(dve, tt(s2, s2, s3, ALU.mult))
                V.link(dve, tt(r1, mo["oh1"], four(s3), ALU.mult))
                V.link(dve, tt(r2, mo["oh2"], four(s2), ALU.mult))
                V.link(dve, tt(r1, r1, r2, ALU.add))
                for g in range(G):
                    ins = tt(mo["comb"][:, :, g, :], r1, mo["ohg"][:, :, g:g + 1].broadcast_to([P, TJ, E]), ALU.mult)
                s["comb_ready"].link(dve, ins)
                dve.wait_ge(s["combT_ready"].sem, layer + 1)
                base, ub = SLOTS[f"up{layer}"], USES[f"up{layer}"] // 2
                with looped(dve, NE // 2, {s["ce_ready"]: 2, s["hid_ready"]: 2 * FT}) as i:
                    for u in range(2):
                        e = 2 * i + u
                        dve.wait_ge(s["cb_full"].sem, e + NE * layer)
                        s["ce_ready"].on(ts(mo["ce"][0:NE, :], mo["combT"][0:NE, :], ident[0:NE, bass.ds(e, 1)],
                                            None, ALU.mult))
                        for f in range(FT):
                            dve.wait_ge(used, 8 * i + (base + 4 * u + 2 * f + 2))
                            dve.wait_ge(pair_free[0].sem, 4 * i + (ub + 2 * u + f + 1))
                            pair_free[1].on(tt(two(mo["tmp"]), halves(1), two(mo["sil"]), ALU.mult))
                            dve.wait_ge(s["cb_ready"].sem, e + (NE * layer + 1))
                            dve.wait_ge(pair_free[1].sem, 4 * i + (ub + 2 * u + f + 1))
                            hid = mo["hid"][:, bass.ds(2 * e + f, 1), :].rearrange("p a n -> p (a n)")
                            s["hid_ready"].link(dve, tt(hid, mo["tmp"], mo["cb"][:, 0, :], ALU.mult))
                gated(f"down{layer}", HIDT // 8, 1, mo["tmp"][:, 0:64])

            moe(0)
            modulation(1)
            norm(2)

            wE = col("wE", 3, MT, 4)
            V.link(dve, dve.memset(first["gx"], 0.0))
            V.link(dve, dve.memset(first["gm"], 0.0))
            V.link(dve, dve.memset(first["xpad"][:, :, 0:3], 0.0))
            dve.wait_ge(conv_in, 32)
            cw = col("cw", 4, MT)

            def weight_of(w, i):
                return wE[:, w, i, :] if isinstance(i, int) else wE[:, w, bass.ds(i, 1), :].rearrange("p a o -> p (a o)")

            def block_diagonal(dst, w, i):
                return tt(dst.rearrange("p (m o) -> p m o", o=4), col("bd").unsqueeze(2).broadcast_to([P, 32, 4]),
                          weight_of(w, i).unsqueeze(1).broadcast_to([P, 32, 4]), ALU.mult)

            def gate_weights(dst, w, i):
                g = first["wg"][:, w, bass.ds(i, 1)].rearrange("p a n o -> p (a n) o")
                return tt(dst, g, weight_of(w, i).unsqueeze(1).broadcast_to([P, 8, 4]), ALU.mult)

            def inner(u, i, guarded):
                if guarded:
                    dve.wait_ge(s["gates_full"].sem, i - 1)
                two4 = lambda ap: ap.rearrange("p (a b) -> p a b", a=2)[:, :, 0:4]
                V.link(dve, gate_weights(first["pr"], 0, i))
                V.link(dve, gate_weights(first["pr2"], 1, i))
                V.link(dve, tt(first["pr"], first["pr"], first["pr2"], ALU.add))
                V.link(dve, dve.tensor_reduce(two4(first["gx"][:, u, :]), first["pr"].rearrange(
                    "p (a b) o -> p a b o", a=2), AX.X, ALU.add))
                V.link(dve, gate_weights(first["pr"], 2, i))
                V.link(dve, dve.tensor_reduce(two4(first["gm"][:, u, :]), first["pr"].rearrange(
                    "p (a b) o -> p a b o", a=2), AX.X, ALU.add))
                s["bdv_ready"].on(block_diagonal(first["bdv"][:, u, :], 2, i))
                xp = first["xpad"][:, u, :]
                pads = xp[:, 3 + TP:].rearrange("p (b t) -> p b t", b=NB)
                c0 = first["conv0"][:, bass.ds(i, 1), :].rearrange("p a (b t) -> p (a b) t", t=3)
                V.link(dve, dve.tensor_copy(pads[:, :, 0:3], c0))
                dve.wait_ge(s["xm_ready"].sem, 3 * i + 3)
                dve.wait_ge(s["xc_ready"].sem, i)
                acc = first["acc"]
                for tap in range(4):
                    w = cw[:, tap, i:i + 1] if isinstance(i, int) else cw[:, tap, bass.ds(i, 1)]
                    cb = col("cb")[:, bass.ds(i, 1)]
                    for dst, src in ((acc[:, 0:TP], xp[:, tap:tap + TP]), (by_seq(acc[:, TP:T]), pads[:, :, tap:tap + TS])):
                        if tap == 0:
                            ins = ts(dst, src, w, cb, ALU.mult, ALU.add)
                        else:
                            ins = stt(dst, src, w, dst, ALU.mult, ALU.add)
                    if tap < 3:
                        V.link(dve, ins)
                co = at(first["convout"], i)
                s["conv_acc"].on(ins)
                dve.tensor_copy(co[:, 0:3], xp[:, TP:TP + 3])
                dve.tensor_copy(co[:, 3:].rearrange("p (b t) -> p b t", b=NB), pads[:, :, TS:TS + 3])
                dve.wait_ge(s["v_full"].sem, i + 1)
                vt = ml["vtok"][:, :, bass.ds(P * i, P)]
                dve.tensor_copy(vt[:, 0:4, :], shaped(ps[:, 4, :], 4, P))
                s["v_read"].link(dve, dve.tensor_copy(vt[0:64, 4, :], ps[0:64, 5, 0:P]))

            inner(0, 0, False)
            inner(1, 1, False)
            with looped(dve, MT // 2 - 1, {V: 2 * 10, s["bdv_ready"]: 2, s["conv_acc"]: 2, s["v_read"]: 2}) as i:
                for u in range(2):
                    inner(u, 2 * i + (u + 2), True)
            s["conv_done"].link(dve, dve.memset(first["pr"][:, 0, 0:1], 0.0))

            dve.wait_ge(s["gates_full"].sem, MT)
            dve.wait_ge(out_done, 16)
            ig, gb, gu, t1, t2 = (gate[n][0:MH, :] for n in ("ig", "b", "u", "t1", "t2"))
            for dst, r0 in ((ig, 0), (t1, 32)):
                V.link(dve, dve.tensor_copy(dst[:, 0:TP], ps[r0:r0 + MH, 6, :]))
                V.link(dve, dve.tensor_copy(dst[:, TP:T], ps[r0:r0 + MH, 7, 0:64]))
            V.link(dve, ts(ig, ig, col("big")[0:MH, :], None, ALU.add))
            V.link(dve, ts(t1, t1, col("bfg")[0:MH, :], None, ALU.add))
            s["abs_ready"].link(dve, stt(t2, t1, -1.0, t1, ALU.mult, ALU.max))
            V.link(dve, ts(t1, t1, 0.0, None, ALU.min))
            dve.wait_ge(s["soft_ready"].sem, 1)
            V.link(dve, tt(t1, t1, t2, ALU.subtract))
            V.link(dve, dve.tensor_tensor_scan(gb, col("whole")[0:MH, :], t1, 0.0, ALU.mult, ALU.add))
            V.link(dve, tt(gu, ig, gb, ALU.subtract))
            V.link(dve, dve.tensor_copy(t2, gu))
            V.link(dve, ts(t2[:, 0:1], gu[:, 0:1], 0.0, None, ALU.max))
            m0 = col("m0")[0:MH, :]
            V.link(dve, tt(by_seq(t2[:, TP:T])[:, :, 0:1], by_seq(gu[:, TP:T])[:, :, 0:1], m0.unsqueeze(2), ALU.max))
            cut = gate["cut"][0:MH, :]
            V.link(dve, ts(cut, col("whole")[0:MH, :], -1.0, BIG, ALU.add, ALU.mult))
            V.link(dve, dve.tensor_tensor_scan(ig, cut, t2, 0.0, ALU.add, ALU.max))
            V.link(dve, tt(gb, gb, ig, ALU.add))
            rows = ml["rows"]
            V.link(dve, ts(rows[0:MH, :], ig, -1.0, None, ALU.mult))
            V.link(dve, dve.tensor_copy(rows[32:32 + MH, :], gb))
            V.link(dve, dve.tensor_copy(t2[:, 0:1], gb[:, TP - 1:TP]))
            V.link(dve, dve.tensor_copy(t2[:, 1:NV].unsqueeze(2), by_seq(gb[:, TP:T])[:, :, TS - 1:TS]))
            V.link(dve, ts(t1[:, 0:TP], gu[:, 0:TP], ig[:, TP - 1:TP], None, ALU.subtract))
            V.link(dve, tt(by_seq(t1[:, TP:T]), by_seq(gu[:, TP:T]), over_t(by_seq(ig[:, TP:T])[:, :, TS - 1]), ALU.subtract))
            s["dec_ready"].on(tt(by_seq(gb[:, TP:T]), over_t(m0), by_seq(ig[:, TP:T]), ALU.subtract))
            dve.wait_ge(s["dec_exp"].sem, 1)
            V.link(dve, dve.tensor_copy(rows[64:64 + MH, :], t1))
            s["rows_ready"].link(dve, dve.tensor_copy(rows[96:96 + MH, TP:T], gb[:, TP:T]))
            dve.wait_ge(s["turned_g"].sem, 1)
            for n, dst in enumerate((ml["utok"], ml["wtok"])):
                V.link(dve, dve.tensor_copy(dst[:, 0:4, :], shaped(ps[:, 4, 32 * n:32 * n + 16], 4, MH)))
                s["tok_ready"].link(dve, dve.tensor_copy(dst[0:64, 4, :], ps[0:64, 4, 32 * n + 16:32 * n + 20]))

            ub = USES["b"]
            n0 = col("n0", MT, NB)
            bdq = ml["W"].rearrange("p a b -> p (a b)")
            for h in range(MH):
                hb = ub + N_HEADB * h
                if h == 0:
                    dve.wait_ge(out_done, 32)
                for u in range(2):
                    dve.wait_ge(cp_out[u], 8 * HT * h)
                for w in range(2):
                    for i in range(HT):
                        ins = block_diagonal(bdq[:, (HT * w + i) * P:(HT * w + i + 1) * P], w, HT * h + i)
                s["bd_ready"].on(ins)
                dve.wait_ge(s["kt_full"].sem, h + 1)
                for j in range(4):
                    ts(ml["ktok"][:, j, :], ps[:, 4 + j, :], ml["wtok"][:, j, h:h + 1], KS, ALU.mult, ALU.mult)
                p = (hb + 12) % 2
                pair_free[p].on(ts(ml["ktok"][0:64, 4, :], ps[0:64, 2 * p, :], ml["wtok"][0:64, 4, h:h + 1], KS,
                                   ALU.mult, ALU.mult))
                dve.wait_ge(pair_free[p].sem, (hb + 12) // 2 + 1)
                for pp in range(2):
                    dve.wait_ge(pair_free[pp].sem, (hb + 12) // 2)
                for i in range(HT):
                    tmp = mx["rs"]
                    V.link(dve, tt(tmp, ml["kz"][:, i, :], mx["mu"], ALU.mult))
                    no = ml["nout"][:, HT * h + i, :]
                    V.link(dve, dve.tensor_reduce(no[:, 0:1], tmp[:, 0:TP], AX.X, ALU.add))
                    V.link(dve, dve.tensor_reduce(no[:, 1:NV], by_seq(tmp[:, TP:T]), AX.X, ALU.add))
                wl = by_seq(mx["wcb"])[:, :, TS - 1]
                nh = n0[:, HT * h:HT * (h + 1), :]
                V.link(dve, tt(shaped(mx["rs"][:, 0:HT * NB], HT, NB), nh, wl.unsqueeze(1).broadcast_to([P, HT, NB]), ALU.mult))
                no = ml["nout"][:, HT * h:HT * (h + 1), 1:NV]
                s["n_ready"].link(dve, tt(no, no, shaped(mx["rs"][:, 0:HT * NB], HT, NB), ALU.add))
                qs = ml["q"][:, :, TP:T]
                V.link(dve, tt(mx["qw"], qs, mx["wcb"].unsqueeze(1).broadcast_to([P, HT, 64]), ALU.mult))
                qn = mx["kb"][:, 0:256].rearrange("p (i b t) -> p i b t", i=HT, b=NB)
                s["qw_ready"].link(dve, tt(qn, mx["qw"].rearrange("p i (b t) -> p i b t", b=NB), over_t(nh), ALU.mult))
                dve.wait_ge(s["s_full"].sem, h + 1)

                def weight(j):
                    n = TP - P * j if j < 4 else 64
                    m = P if j < 4 else 64
                    w = ml["W"][0:m, j % 2, 0:n]
                    src = mx["nM"][0:m, P * j:P * j + n]
                    s["w_ready"].link(dve, ts(w, src, ml["utok"][0:m, j, h:h + 1], 0.0, ALU.add, ALU.min))

                weight(0)
                for j in range(TJ):
                    if j + 1 < TJ:
                        weight(j + 1)
                    dve.wait_ge(s["w_exp"].sem, 5 * h + j + 1)
                    if j < 4:
                        n = TP - P * j
                        Pj = mx[f"P{j}"]
                        V.link(dve, tt(Pj, ps[:, 4 + j, 0:n], ml["W"][:, j % 2, 0:n], ALU.mult))
                        s["p_ready"].link(dve, tt(Pj[:, 0:P], Pj[:, 0:P], causal, ALU.mult))
                    else:
                        p = (hb + 13) % 2
                        pair_free[p].on(tt(mx["Ps"][0:64, :], ps[0:64, 2 * p, 0:64], ml["W"][0:64, 0, 0:64], ALU.mult))
                        dve.wait_ge(pair_free[p].sem, (hb + 13) // 2 + 1)
                        s["p_ready"].link(dve, tt(mx["Ps"][0:64, :], mx["Ps"][0:64, :], causal_s[0:64, :], ALU.mult))
                for b in range(NB):
                    n = NB * h + b
                    C = shaped(ml["C"][:, n % 2, :], HT, MD)
                    dve.wait_ge(s["num_s"].sem, 9 * h + b + 2)
                    for k in range(HT):
                        dve.wait_ge(s["upd_c"].sem, HT * n + k + 1)
                        s["c_done"].on(stt(C[:, k, :], C[:, k, :], mx["wcb"][:, TS * b + TS - 1:TS * (b + 1)],
                                           ps[:, 4 + k, :], ALU.mult, ALU.add))
                rd = mx["rs"]

                def guard_den(dst, den, emn):
                    V.link(dve, ts(dst, den, -1.0, None, ALU.mult))
                    V.link(dve, tt(dst, dst, den, ALU.max))
                    V.link(dve, tt(dst, dst, emn, ALU.max))
                    V.link(dve, dve.reciprocal(dst, dst))

                n = hb + 14
                p = n % 2
                dve.wait_ge(s["num_full"].sem, h + 1)
                guard_den(rd[:, TP:T], ps[:, 2 * p + 1, 0:64], mx["emn"][:, TP:T])
                ins = tt(ml["q"][:, :, TP:T], shaped(ps[:, 2 * p, 0:256], HT, 64),
                         rd[:, TP:T].unsqueeze(1).broadcast_to([P, HT, 64]), ALU.mult)
                pair_free[p].on(ins)
                fb = 17 * h + 12
                n += 1
                p = n % 2
                dve.wait_ge(s["b_full"].sem, fb + 1)
                V.link(dve, ts(rd[:, 0:TP], ps[:, 2 * p, :], -1.0, None, ALU.mult))
                pair_free[p].on(tt(rd[:, 0:TP], rd[:, 0:TP], ps[:, 2 * p, :], ALU.max))
                dve.wait_ge(pair_free[p].sem, n // 2 + 1)
                V.link(dve, tt(rd[:, 0:TP], rd[:, 0:TP], mx["emn"][:, 0:TP], ALU.max))
                V.link(dve, dve.reciprocal(rd[:, 0:TP], rd[:, 0:TP]))
                for i in range(HT):
                    n += 1
                    p = n % 2
                    dve.wait_ge(s["b_full"].sem, fb + 2 + i)
                    pair_free[p].on(tt(ml["q"][:, i, 0:TP], ps[:, 2 * p, :], rd[:, 0:TP], ALU.mult))
                n += 5
                p = n % 2
                dve.wait_ge(s["mu_full"].sem, h + 1)
                pair_free[p].on(ts(two(mx["mu"]), halves(p), 1.0 / MD, None, ALU.mult))
                dve.wait_ge(pair_free[p].sem, n // 2 + 1)
                q, z = ml["q"], ml["kz"]
                s["rs_h"].link(dve, tt(q, q, mx["mu"].unsqueeze(1).broadcast_to([P, HT, T]), ALU.subtract))
                dve.wait_ge(s["sqh_ready"].sem, h + 1)
                for i in range(HT):
                    V.link(dve, ts(q[:, i, :], q[:, i, :], col("mln")[:, HT * h + i:HT * h + i + 1], None, ALU.mult))
                dve.wait_ge(s["rsh_ready"].sem, h + 1)
                V.link(dve, tt(q, q, mx["rs"].unsqueeze(1).broadcast_to([P, HT, T]), ALU.mult))
                for i in range(HT):
                    xc = ml["xc"][:, HT * h + i, :]
                    V.link(dve, stt(q[:, i, :], xc, col("skip")[:, HT * h + i:HT * h + i + 1], q[:, i, :], ALU.mult, ALU.add))
                for p in range(2):
                    dve.wait_ge(pair_free[p].sem, (hb + 24) // 2)
                s["ho_ready"].link(dve, tt(ml["xc"][:, HT * h:HT * (h + 1), :], q, z, ALU.mult))

            dve.wait_ge(x_back, 16)
            gated("md", 2, 0, ml["W"][:, 0, 0:64])
            moe(1)
            norm(4)


def kernel(**inputs):
    import concourse.bacc as _bacc
    from concourse.bass_utils import run_bass_kernel_spmd as _run

    a = {k: np.asarray(v) for k, v in inputs.items()}
    f32 = np.float32

    def features(x):
        return np.moveaxis(x.reshape(x.shape[:-1] + (-1, P)), -1, 0)

    cols = np.zeros((P, NCOL), f32)

    def put(name, x):
        at, n = COLS[name]
        x = np.asarray(x, f32)
        x = x.reshape(x.shape[0], -1)
        assert x.shape[1] == n, (name, x.shape, n)
        cols[:x.shape[0], at:at + n] = x

    c = np.concatenate([a["c_prompt"], a["c_sample"]], 0)
    put("c", np.moveaxis(features(c), 1, 2))
    put("bada", features(a["b_ada"]))
    put("ng", features(a["norm_g"]))
    put("fg", features(a["final_g"]))
    put("hgn", a["hg_norm"][0][:, None])
    put("lb", features(a["hg_lb"]))
    put("cw", features(a["ml_conv_w"][0]))
    put("cb", features(a["ml_conv_b"][0]))
    put("wE", np.stack([a[n][0].transpose(0, 2, 1).reshape(MT, P, 4) for n in ("ml_wq", "ml_wk", "ml_wv")], 0).transpose(2, 0, 1, 3))
    put("mln", features(a["ml_norm"][0]))
    put("skip", features(a["ml_skip"][0]))
    wr = np.concatenate([a["moe_wrg"], a["moe_wre"].reshape(LAYERS, D, NE)], 2)
    put("wr", wr.reshape(LAYERS, DC, P, 20).transpose(2, 0, 1, 3))
    put("rb", np.concatenate([a["moe_brg"], a["moe_bre"].reshape(LAYERS, NE)], 1).T)
    put("n0", a["state_mlstm_n"][0].reshape(NB, MT, P).transpose(2, 1, 0))
    put("big", a["ml_big"].T)
    put("bfg", a["ml_bfg"].T)
    put("m0", a["state_mlstm_m"][0].T)
    t = np.arange(T)
    put("ident", np.eye(P))
    put("ones", np.ones((P, P)))
    put("causal", np.triu(np.ones((P, P))))
    r = np.arange(NB * TS)
    put("causal_s", (r[:, None] // TS == r[None] // TS) & (r[:, None] <= r[None]))
    put("own", r[:, None] // TS == np.arange(NB)[None])
    starts = np.where(t < TP, t % P == 0, (t - TP) % TS == 0)
    put("keep", np.tile(np.where(starts, 0.0, 1.0), (P, 1)))
    whole = np.where(t < TP, t == 0, (t - TP) % TS == 0)
    put("whole", np.tile(np.where(whole, 0.0, 1.0), (MH, 1)))
    put("rank", np.tile(np.arange(4, 0, -1), (P, 1)))
    put("bd", np.arange(P)[:, None] // 4 == np.arange(32)[None])
    put("eps", np.full((P, 1), EPS))

    def tiles(w):
        k, m = w.shape
        w = w.reshape(k // 1024, 8, P, m // P, P).transpose(3, 0, 2, 1, 4)
        return w.reshape(-1, P, SLOT)

    def ada_tiles(w):
        w = w.reshape(4, 2, P, 12, 512).transpose(3, 0, 2, 1, 4)
        return w.reshape(-1, P, SLOT)

    win = a["hg_win"][0].reshape(D, 4, H, P)[:, [1, 0, 3, 2]]
    parts = {
        "ada0": ada_tiles(a["w_ada"][0]), "ada1": ada_tiles(a["w_ada"][1]),
        "hg": tiles(win.transpose(0, 2, 1, 3).reshape(D, -1)),
        "wo": tiles(a["hg_wo"][0]),
        "xm": tiles(a["ml_wup"][0][:, :MI]), "z": tiles(a["ml_wup"][0][:, MI:]),
        "md": tiles(a["ml_wdown"][0])}
    for l in range(LAYERS):
        w13 = np.stack([a["moe_w1"][l].reshape(NE, D, FT, P), a["moe_w3"][l].reshape(NE, D, FT, P)], 3)
        parts[f"up{l}"] = tiles(w13.transpose(1, 0, 2, 3, 4).reshape(D, -1))
        parts[f"down{l}"] = tiles(a["moe_w2"][l].reshape(NE * FF, D))
    wstream = np.empty((NSLOT, P, SLOT), f32)
    for name, w in parts.items():
        wstream[SLOTS[name]:SLOTS[name] + len(w)] = w

    x = np.concatenate([a["x_prompt"].reshape(TP, D), a["x_sample"].reshape(NB * TS, D)], 0)
    wg = np.concatenate([a["ml_wig"][0], a["ml_wfg"][0]], 1).reshape(3, MT, 32, 4, 8)
    wg = np.broadcast_to(wg.transpose(0, 1, 2, 4, 3)[:, :, :, None], (3, MT, 32, 4, 8, 4))
    c0 = a["state_mlstm_c"][0].transpose(1, 0, 2, 3).reshape(MH * NB, HT, P, MD)
    arrays = {
        "cols": cols, "wstream": wstream,
        "xT": x.reshape(T, DC, P).transpose(2, 1, 0),
        "hg0": a["state_hgrn"][0].transpose(1, 2, 0, 3).reshape(H, P, NB * P),
        "wg": wg.reshape(3, MT, P, 32).transpose(2, 0, 1, 3).reshape(P, -1),
        "conv0": a["state_conv"][0].reshape(NB, 3, MT, P).transpose(3, 2, 0, 1).reshape(P, -1),
        "c0": c0.transpose(0, 2, 1, 3).reshape(MH * NB, P, HT * MD)}
    arrays = {k: np.ascontiguousarray(v, f32) for k, v in arrays.items()}
    outs = {"y": (P, DC, T), "hg_p": (H, P, P), "hg_s": (H, P, NB * P), "mc_p": (MH, HT, P, MD),
            "mc_s": (MH * NB, P, HT * MD), "mn": (P, MT * NV), "mm": (MH, NV), "conv": (P, MT * 3 * NV)}

    nc = _bacc.Bacc("TRN2", target_bir_lowering=False, num_devices=1)
    io = {k: nc.dram_tensor(f"in_{k}", list(v.shape), F32, kind="ExternalInput").ap() for k, v in arrays.items()}
    io["out"] = {k: nc.dram_tensor(f"out_{k}", list(v), F32, kind="ExternalOutput").ap() for k, v in outs.items()}
    io["x_dram"] = nc.dram_tensor("x_dram", [P, DC, T], F32, kind="Internal").ap()
    build(nc, io)
    res = _run(nc, [{f"in_{k}": v for k, v in arrays.items()}], core_ids=[0]).results[0]
    o = {k: np.asarray(res[f"out_{k}"]) for k in outs}

    y = o["y"].transpose(2, 1, 0).reshape(T, D)
    mn = o["mn"].reshape(P, MT, NV).transpose(2, 1, 0).reshape(NV, MH, MD)
    conv = o["conv"].reshape(P, MT, NV, 3).transpose(2, 3, 1, 0).reshape(NV, 3, MI)
    mm = o["mm"].T
    hg_s = o["hg_s"].reshape(H, P, NB, P).transpose(2, 0, 1, 3)
    mc_s = o["mc_s"].reshape(MH, NB, P, HT, MD).transpose(1, 0, 3, 2, 4).reshape(NB, MH, MD, MD)
    return (y[:TP].reshape(1, TP, D), y[TP:].reshape(NB, TS, D), o["hg_p"][None, None],
            o["mc_p"].reshape(1, 1, MH, MD, MD), mn[None, :1], mm[None, :1], conv[None, :1],
            hg_s[None], mc_s[None], mn[None, 1:], mm[None, 1:], conv[None, 1:])
```

```python
from contextlib import ExitStack, contextmanager

import numpy as np

import concourse.bass as bass
from concourse import mybir

F32 = mybir.dt.float32
ALU = mybir.AluOpType
ACT = mybir.ActivationFunctionType
AX = mybir.AxisListType

P = 128
D = 1024
DC = D // P
TP = 512
NB, TS = 8, 8
T = TP + NB * TS
TH = T // 2
TJ = 5
NV = NB + 1
H = 8
BLK = 32
MI = 2048
MT = MI // P
MH = 4
MD = MI // MH
HT = MD // P
G, E, NE, FF = 4, 4, 16, 256
FT = FF // P
KG = E * FT
W = 224
CH = (128, W - 128)
TW = T + W
MORE = T // W
X_PE, X_ACT, X_DVE = 6 + DC, E + 1, 5 * E + 2 + 4 * DC
EPS = 1e-6
BIG = 1e30
CLAMP = 60.0
LAYERS = 2

R = 8
SLOT = 1024
N_ADA = 6 * D // 512 * 4
N_HG, N_WO = 4 * H, DC
N_GROUP = E * FT * 2 + E * FT
N_XM, N_Z, N_MD = MT, MT, DC * MT // 8
SLOTS = {}
_at = 0
for _name, _n in (("ada0", N_ADA), ("hg", N_HG), ("wo", N_WO), ("moe0", G * N_GROUP),
                  ("ada1", N_ADA), ("xm", N_XM), ("z", N_Z), ("md", N_MD), ("moe1", G * N_GROUP)):
    SLOTS[_name] = _at
    _at += _n
NSLOT = _at
USES = {}
_at = 2
N_HEADB = 26
for _name, _n in (("ada0", 12), ("hg", 4 * H), ("wo", DC), ("moe0", 2 * DC + 4 * NE), ("ada1", 12),
                  ("xm", MT), ("b", N_HEADB * MH), ("md", DC), ("moe1", 2 * DC + 4 * NE)):
    USES[_name] = _at
    _at += _n


def offsets(spec):
    at, out = 0, {}
    for name, n in spec:
        out[name] = (at, n)
        at += n
    return out, at


COLS, NCOL = offsets([
    ("c", DC * NV), ("bada", LAYERS * 48), ("ng", LAYERS * 2 * DC), ("fg", DC), ("hgn", 1), ("lb", 3 * H),
    ("cw", 4 * MT), ("cb", MT), ("wE", 3 * MT * 4), ("mln", MT), ("skip", MT), ("wr", LAYERS * DC * 20),
    ("rb", LAYERS), ("n0", MT * NB), ("big", 1), ("bfg", 1), ("m0", NB),
    ("ident", P), ("ones", P), ("causal", P), ("causal_s", 64), ("own", NB), ("keep", T), ("whole", T),
    ("rank", 4), ("bd", 32), ("eps", 1), ("part", 1)])


class Signal:

    def __init__(self, sem):
        self.sem, self.base, self.n = sem, 0, 0

    def on(self, ins):
        ins.then_inc(self.sem, 1)
        self.n += 1

    def link(self, eng, ins):
        self.on(ins)
        eng.wait_ge(self.sem, self.base + self.n)


@contextmanager
def looped(eng, n, per):
    kept = {s: s.base + s.n for s in per}
    with eng.Fori(0, n) as i:
        for s, k in per.items():
            s.base, s.n = kept[s] + i * k, 0
        yield i
    for s, k in per.items():
        assert s.n == k, f"a signal is raised {s.n} times in a pass, not {k}"
        s.base, s.n = kept[s] + n * k, 0


def build(nc, io):
    with ExitStack() as ctx:
        def sb(name, *dims):
            return ctx.enter_context(nc.sbuf_tensor(name, [P, int(np.prod(dims))], F32))

        def sem(name):
            return ctx.enter_context(nc.semaphore(name))

        def shaped(ap, *dims):
            if len(dims) == 1:
                return ap
            names = "abcd"[:len(dims)]
            return ap.rearrange(f"p ({' '.join(names)}) -> p {' '.join(names)}", **dict(zip(names, dims)))

        ring = shaped(sb("ring", R * SLOT)[:, :], R, SLOT)
        xT = shaped(sb("xT", DC * T)[:, :], DC, T)
        hT = shaped(sb("hT", DC * T)[:, :], DC, T)
        cols = sb("cols", NCOL)
        modt = shaped(sb("modt", 48 * NV)[:, :], 48, NV)
        amod = shaped(sb("amod", 2 * DC * NV)[:, :], 2, DC, NV)
        ARENA = 32504
        arena = sb("arena", ARENA)
        ps = ctx.enter_context(nc.psum_tensor("ps", [P, 8, 512], F32))

        def col(name, *dims):
            at, n = COLS[name]
            return shaped(cols[:, at:at + n], *dims) if dims else cols[:, at:at + n]

        def carve(spec, start=0):
            at, out = start, {}
            for name, *dims in spec:
                n = int(np.prod(dims))
                out[name] = shaped(arena[:, at:at + n], *dims)
                at += n
            assert at <= ARENA, at
            return out, at

        ident, ones, keep = col("ident"), col("ones"), col("keep")
        causal, causal_s, own = col("causal"), col("causal_s"), col("own")
        eps = col("eps")

        ada, _ = carve([("modrow", 6 * D)])
        silc = col("c", DC, NV)
        rstd = arena[:, 24000:24000 + T]
        hg, _ = carve([
            ("og", H, T), ("S0", 2, NB * P), ("Vx", NB, P), ("th", 2, T), ("q", 2, T), ("zg", 2, T),
            ("v", 2, TJ * P), ("k", T), ("g", T), ("b", T), ("eq", T), ("K", 16, P), ("Ks", 64),
            ("qe", T), ("kw", T), ("at", TJ, P), ("ktw", TJ, P), ("S", 4, P), ("sq", T),
            ("rs", T), ("Sn", NB, P), ("half", H), ("low", H), ("t1", 3, H), ("t2", H)])
        mo, _ = carve([
            ("hs", DC, TW), ("P", TJ, TW), ("y", 2 * G, D), ("PT", 2 * G, T), ("hid", 2, KG, W),
            ("sil", W), ("tmp", W), ("ce", 2, W), ("cS", TW), ("lgT", T), ("gt", 64),
            ("lg", TJ, 20), ("r1", TJ, 4), ("r2", TJ, 4), ("r3", TJ, 4), ("oh1", TJ, 4), ("oh2", TJ, 4),
            ("s1", TJ), ("s2", TJ), ("s3", TJ), ("s4", TJ), ("ps", TJ), ("ohg", TJ, 4), ("sel", TJ, 4, 4),
            ("comb", TJ, 4, 4), ("rk", TJ, 4), ("tot", TJ, 4), ("pre", TJ, 4), ("off", 4), ("pos", TJ),
            ("at", 2 * G), ("w0", 4), ("w1", 4), ("w2", 4), ("w3", 4), ("more", 3, MORE), ("more_at", 2, MORE)])
        h_tok = shaped(mo["y"].rearrange("p a b -> p (a b)")[:, 0:TJ * D], TJ, D)
        pt_flat = mo["PT"].rearrange("p a b -> p (a b)")
        iota1, dg, strict = pt_flat[:, 0:TW], shaped(pt_flat[:, TW:TW + TJ * P], TJ, P), \
            pt_flat[:, TW + TJ * P:TW + TJ * P + P]
        pos_row = mo["lgT"]
        place = ctx.enter_context(nc.sbuf_tensor("place", [1, G + 3 * MORE], mybir.dt.int32))
        off_i, more_i = place[:, 0:G], shaped(place[:, G:], 3, MORE)
        ml, _ = carve([
            ("vtok", TJ, MI), ("xc", MT, T), ("q", HT, T), ("kz", HT, T), ("ktok", TJ, MD),
            ("C", 2, HT * MD), ("W", 2, 512), ("rows", T), ("nout", MT, NV), ("utok", TJ, MH),
            ("wtok", TJ, MH)])
        c_at = TJ * MI + MT * T + 2 * HT * T + TJ * MD
        first, first_end = carve([
            ("xpad", 2, 3 + TP + NB * 11), ("xs", 2, 64), ("acc", T), ("bdv", 2, P), ("gx", 2, 64),
            ("gm", 2, 64), ("wg", 3, MT, 8, 4), ("conv0", MT, 3 * NB), ("pr", 8, 4), ("pr2", 8, 4),
            ("convout", MT, 3 * NV)], c_at)
        assert first_end <= c_at + 2 * HT * MD + 1024
        gate, gate_end = carve([("ig", T), ("b", T), ("u", T), ("t1", T), ("t2", T), ("cut", T)], c_at)
        assert gate_end <= first_end - MT * 3 * NV
        x_flat = xT.rearrange("p a b -> p (a b)")
        mx, at = {}, 0
        for name, *dims in (("P0", 512), ("P1", 384), ("P2", 256), ("P3", 128), ("Ps", 64), ("kb", 512),
                            ("mu", T), ("rs", T), ("emn", T), ("nM", T), ("qw", HT, 64), ("wcb", 64)):
            n = int(np.prod(dims))
            mx[name] = shaped(x_flat[:, at:at + n], *dims)
            at += n
        assert at <= DC * T
        slot_full = [sem(f"slot_full{r}") for r in range(R)]
        pair_free = [Signal(sem(f"pair_free{p}")) for p in range(2)]
        small_in, x_in, conv_in, x_kept, x_back, out_done, sn_out = (
            sem(n) for n in ("small_in", "x_in", "conv_in", "x_kept", "x_back", "out_done", "sn_out"))
        s0_in, cp_out = ([sem(f"{n}{u}") for u in range(2)] for n in ("s0_in", "cp_out"))
        c_in, c_out = ([[sem(f"{n}{u}{half}") for half in range(2)] for u in range(2)] for n in ("c_in", "c_out"))
        names = (
            "dve act num_full lb_in lb_out conv_acc rsh_ready slot_used silc turned mod_ready sq_ready ss_ready rstd_ready h_ready x_tile y_ready "
            "zf_read heads_in decay f_ready diffs exps elem_ready scored scored_s at_ready upd upd_s vx_ready s_ready "
            "o_full o_read sq_head head_ss head_rs head_done sn_ready sn_kept "
            "lgT_full lg_ready lg_turned top_in top_out comb_ready ranked place_ready spread htok_full htok_ready "
            "cS_full cS_ready pos_full pos_ready gathered ce_ready cb_full y_full yg_ready scattered pt_ready "
            "hid_ready xm_ready bdv_ready xc_ready v_full v_read gates_full "
            "conv_done abs_ready soft_ready dec_ready dec_exp rows_ready turned_g tok_ready gates_read "
            "bd_ready b_full b_read kt_full kt_read s_full w_ready w_exp p_ready qw_ready kb_ready num_s "
            "upd_c c_done cp_full cp_ready n_ready hc_ready mu_full sqh_ready var_full ho_ready "
            "z_ready rs_h alone_ready raw_ready turned_s").split()
        s = {n: Signal(sem(n)) for n in names}
        x_w = [sem(f"x_w{l}") for l in range(LAYERS)]
        x_pe, x_act, x_dve = ([Signal(sem(f"{n}{l}")) for l in range(LAYERS)] for n in ("x_pe", "x_act", "x_dve"))
        wstream, out = io["wstream"], io["out"]

        qn = shaped(ml["W"][:, 0, 64:64 + HT * 64], HT, 64)
        alone = shaped(ml["W"][:, 1, :], 2, HT, 64)

        xw, xy, xhid = mo["y"][:, 4:8, :], mo["y"], mo["hid"][:, 0]

        @contextmanager
        def further(eng, steps):
            with looped(eng, MORE, steps) as k:
                there, group, start = (eng.value_load(more_i[0:1, n, bass.ds(k, 1)], min_val=0, max_val=hi)
                                       for n, hi in enumerate((1, G - 1, T)))
                with eng.If(there > 0):
                    yield k, group, start

        @contextmanager
        def further_one(eng, k):
            there, group, start = (eng.value_load(more_i[0:1, n, k:k + 1], min_val=0, max_val=hi)
                                   for n, hi in enumerate((1, G - 1, T)))
            with eng.If(there > 0):
                yield group, start

        block = ctx.enter_context(nc.Block())

        @block.sync
        def _(sp):
            sp.dma_start(cols[:, :], io["cols"]).then_inc(small_in, 16)
            for r in range(R):
                sp.dma_start(ring[:, r, :], wstream[r]).then_inc(slot_full[r], 16)
            sp.dma_start(xT, io["xT"]).then_inc(x_in, 16)
            with sp.Fori(1, NSLOT // R) as i:
                for r in range(R):
                    sp.wait_ge(s["slot_used"].sem, R * i + (r + 1 - R))
                    sp.dma_start(ring[:, r, :], wstream[bass.ds(R * i + r, 1)].rearrange("a p n -> p (a n)")
                                 ).then_inc(slot_full[r], 16)

        @block.gpsimd
        def _(pool):
            pool.sem_inc(s["sn_kept"].sem, 1)
            pool.wait_ge(s["turned"].sem, 1)
            for h in range(2):
                pool.dma_start(hg["S0"][:, h, :], io["hg0"][h]).then_inc(s0_in[h], 16)
            def states_out(h):
                pool.wait_ge(s["sn_ready"].sem, h + 1)
                pool.dma_start(out["hg_s"][bass.ds(h, 1)].rearrange("a p n -> p (a n)"),
                               hg["Sn"].rearrange("p a b -> p (a b)")).then_inc(sn_out, 16)
                pool.dma_start(out["hg_p"][bass.ds(h, 1)].rearrange("a p n -> p (a n)"),
                               hg["S"][:, 3, :]).then_inc(sn_out, 16)

            with pool.Fori(0, H // 2 - 1) as i:
                for u in range(2):
                    states_out(2 * i + u)
                    pool.wait_ge(s["head_done"].sem, 2 * i + u + 1)
                    pool.dma_start(hg["S0"][:, u, :], io["hg0"][bass.ds(2 * i + u + 2, 1)].rearrange(
                        "a p n -> p (a n)")).then_inc(s0_in[u], 16)
                    pool.wait_ge(sn_out, 64 * i + 32 * (u + 1))
                    pool.sem_inc(s["sn_kept"].sem, 1)
            for h in range(H - 2, H):
                states_out(h)
                pool.wait_ge(sn_out, 32 * (h + 1))
                pool.sem_inc(s["sn_kept"].sem, 1)
            def further_weights(layer):
                dma = pool.dma_start
                with further(pool, {}) as (k, group, start):
                    for b in range(6):
                        pool.wait_ge(x_pe[layer].sem, X_PE * k + (b + 1))
                        src = wstream[bass.ds(N_GROUP * group + (SLOTS[f"moe{layer}"] + 4 * b), 4)]
                        dma(xw, src.rearrange("a p n -> p a n")).then_inc(x_w[layer], 16)
                    pool.wait_ge(x_dve[layer].sem, X_DVE * (k + 1))

            pool.wait_ge(s["x_tile"].sem, 2 * DC)
            further_weights(0)
            pool.dma_start(first["wg"].rearrange("p a b c d -> p (a b c d)"), io["wg"]).then_inc(conv_in, 16)
            pool.dma_start(first["conv0"].rearrange("p a b -> p (a b)"), io["conv0"]).then_inc(conv_in, 16)
            pool.wait_ge(s["h_ready"].sem, 3)
            pool.dma_start(io["x_dram"], xT).then_inc(x_kept, 16)
            pool.wait_ge(s["conv_done"].sem, 1)
            pool.dma_start(out["conv"], first["convout"].rearrange("p a b -> p (a b)")).then_inc(out_done, 16)
            pool.wait_ge(s["rows_ready"].sem, 1)
            pool.dma_start(out["mm"], gate["t2"][0:MH, 0:NV]).then_inc(out_done, 16)
            pool.wait_ge(out_done, 32)
            pool.wait_ge(s["turned_g"].sem, 1)
            def half_of(state, half):
                return state[:, HT * MD // 2 * half:HT * MD // 2 * (half + 1)]

            for n in range(2):
                for half in range(2):
                    pool.dma_start(half_of(ml["C"][:, n, :], half), half_of(io["c0"][n], half)).then_inc(c_in[n][half], 16)
            for h in range(MH):
                for b in range(NB):
                    n = NB * h + b
                    for half in range(2):
                        pool.wait_ge(s["c_done"].sem, HT * n + HT // 2 * (half + 1))
                        pool.dma_start(half_of(out["mc_s"][n], half), half_of(ml["C"][:, n % 2, :], half)
                                       ).then_inc(c_out[n % 2][half], 16)
                    if n + 2 < NB * MH:
                        for half in range(2):
                            pool.wait_ge(c_out[n % 2][half], 16 * (n // 2 + 1))
                            pool.dma_start(half_of(ml["C"][:, n % 2, :], half), half_of(io["c0"][n + 2], half)
                                           ).then_inc(c_in[n % 2][half], 16)
                for kt in range(HT):
                    pool.wait_ge(s["cp_ready"].sem, HT * h + kt + 1)
                    pool.dma_start(out["mc_p"][h, kt], ml["W"][:, kt % 2, :]).then_inc(cp_out[kt % 2], 16)
            pool.wait_ge(s["n_ready"].sem, MH)
            pool.dma_start(out["mn"], ml["nout"].rearrange("p a b -> p (a b)")).then_inc(out_done, 16)
            pool.wait_ge(s["ho_ready"].sem, MH)
            pool.dma_start(xT, io["x_dram"]).then_inc(x_back, 16)
            pool.wait_ge(s["x_tile"].sem, 4 * DC)
            further_weights(1)
            pool.wait_ge(s["y_ready"].sem, 1)
            pool.dma_start(out["y"], hT).then_inc(out_done, 16)
            pool.wait_ge(out_done, 64)
            pool.wait_ge(sn_out, 32 * H)
            for u in range(2):
                for half in range(2):
                    pool.wait_ge(c_out[u][half], 16 * NB * MH // 2)
                pool.wait_ge(cp_out[u], 16 * MH * HT // 2)

        @block.tensor
        def _(pe):
            used = s["slot_used"]

            def feature_tile(phase, turn, rs, p, freed, rhs, nk):
                pe.wait_ge(pair_free[p].sem, freed)
                for si, r in enumerate(rs):
                    pe.wait_ge(slot_full[r], 16 * (turn + 1))
                    for c in range(8):
                        k = 8 * si + c
                        for half in range(2):
                            mm = pe.matmul(ps[:, 2 * p + half, 0:TH], ring[:, r, c * P:(c + 1) * P],
                                           rhs(k)[:, TH * half:TH * (half + 1)], start=(k == 0), stop=(k == nk - 1))
                    used.on(mm)

            def h_rhs(k):
                return hT[:, k, :]

            def wide(banks, lhs, rhs, last=True):
                n = len(lhs)
                for k in range(n):
                    for half in range(2):
                        mm = pe.matmul(ps[:, banks[half], 0:TH], lhs[k], rhs[k][:, TH * half:TH * (half + 1)],
                                       start=(k == 0), stop=(k == n - 1))
                return mm

            def ada_rows(layer):
                if layer == 0:
                    pe.wait_ge(small_in, 16)
                pe.wait_ge(s["silc"].sem, 1)
                base, ub = SLOTS[f"ada{layer}"] // R, USES[f"ada{layer}"] // 2
                with looped(pe, 6, {used: R}) as i:
                    for p in range(2):
                        pe.wait_ge(pair_free[p].sem, i + ub)
                        for si in range(4):
                            r = 4 * p + si
                            pe.wait_ge(slot_full[r], 16 * (i + base + 1))
                            for kk in range(2):
                                mm = pe.matmul(ps[0:NV, 2 * p, :], silc[:, 2 * si + kk, :],
                                               ring[:, r, kk * 512:(kk + 1) * 512],
                                               start=(si + kk == 0), stop=(si == 3 and kk == 1))
                            used.on(mm)
                for p in range(2):
                    pe.wait_ge(pair_free[p].sem, ub + 6)
                for j in range(48):
                    mm = pe.transpose(ps[:, 4, NV * j:NV * (j + 1)], ada["modrow"][0:NV, P * j:P * (j + 1)],
                                      ident[0:NV, 0:NV])
                s["turned"].on(mm)

            def norm_sums(n):
                for c in range(DC):
                    pe.wait_ge(s["sq_ready"].sem, DC * n + c + 1)
                    for half in range(2):
                        mm = pe.matmul(ps[:, 6 + half, 0:TH], ones, hT[:, c, TH * half:TH * (half + 1)],
                                       start=(c == 0), stop=(c == DC - 1))
                s["ss_ready"].on(mm)
                if n < 2 * LAYERS:
                    pe.wait_ge(s["h_ready"].sem, n + 1)

            pe.sem_inc(s["cb_full"].sem, 2)
            s["cb_full"].base = 2
            for x in x_pe:
                pe.sem_inc(x.sem, 1)
                x.base = 1
            ada_rows(0)
            pe.wait_ge(x_in, 16)
            norm_sums(0)

            sh, uh = SLOTS["hg"] // R, USES["hg"] // 2

            def project(u, i):
                for q in range(3):
                    feature_tile("hg", i + sh, [4 * u + q], q % 2, 4 * i + (uh + 2 * u + q // 2), h_rhs, DC)
                pe.wait_ge(pair_free[1].sem, 4 * i + (uh + 2 * u + 1))
                pe.wait_ge(slot_full[4 * u + 3], 16 * (i + sh + 1))
                for j in range(TJ):
                    m = P if j < 4 else 64
                    dst = ps[:, 2, P * j:P * (j + 1)] if j < 4 else ps[0:64, 3, 0:P]
                    for c in range(DC):
                        mm = pe.matmul(dst, hT[:, c, P * j:P * j + m], ring[:, 4 * u + 3, c * P:(c + 1) * P],
                                       start=(c == 0), stop=(c == DC - 1))
                used.on(mm)

            def scan(u, pair):
                h = 2 * pair + u
                v = shaped(hg["v"][:, u, :], TJ, P)
                pe.wait_ge(s["elem_ready"].sem, h + 1)
                pe.wait_ge(pair_free[1].sem, 2 * h + (uh + 2))
                pe.wait_ge(s["head_rs"].sem, h + 1)
                for c in range(4):
                    for i in range(4):
                        at = c * P + i * BLK
                        pe.matmul(ps[:, 4, at:at + BLK], hg["K"][:, 4 * c + i, :], hg["eq"][:, at:at + BLK],
                                  start=True, stop=True)
                for c in range(4):
                    mm = pe.transpose(ps[:, 6, c * P:(c + 1) * P], hg["kw"][:, c * P:(c + 1) * P], ident)
                s["scored"].on(mm)
                pe.matmul(ps[0:64, 5, 0:64], hg["Ks"], hg["eq"][:, TP:T], start=True, stop=True)
                s["scored_s"].on(pe.transpose(ps[0:64, 5, P:2 * P], hg["kw"][:, TP:T], ident))
                pe.wait_ge(s["at_ready"].sem, 2 * h + 2)
                for c in range(4):
                    mm = pe.matmul(ps[:, 7, c * P:(c + 1) * P], hg["ktw"][:, c, :], v[:, c, :], start=True, stop=True)
                s["upd"].on(mm)
                pe.wait_ge(s["vx_ready"].sem, h + 1)
                for half in range(2):
                    mm = pe.matmul(ps[:, 4 + 2 * half, :], hg["ktw"][0:64, 4, :],
                                   hg["Vx"].rearrange("p a b -> p (a b)")[0:64, 512 * half:512 * (half + 1)],
                                   start=True, stop=True)
                s["upd_s"].on(mm)
                for c in range(4):
                    mm = pe.matmul(ps[:, 5, c * P:(c + 1) * P], v[:, c, :], hg["at"][:, c, :], start=True,
                                   stop=(c == 0))
                    if c:
                        pe.wait_ge(s["s_ready"].sem, 4 * h + c)
                        mm = pe.matmul(ps[:, 5, c * P:(c + 1) * P], hg["S"][:, c - 1, :],
                                       hg["qe"][:, c * P:(c + 1) * P], start=False, stop=True)
                s["o_full"].on(mm)
                pe.wait_ge(s["s_ready"].sem, 4 * h + 4)
                pe.wait_ge(s0_in[u], 16 * (pair + 1))
                for b in range(NB):
                    pe.matmul(ps[:, 7, TS * b:TS * (b + 1)], hg["S0"][:, u, P * b:P * (b + 1)],
                              hg["qe"][:, TP + TS * b:TP + TS * (b + 1)], start=(b == 0), stop=False,
                              skip_group_check=True)
                mm = pe.matmul(ps[:, 7, 0:64], v[0:64, 4, :], hg["at"][0:64, 4, 0:64], start=False, stop=True,
                               skip_group_check=True)
                s["o_full"].on(mm)
                pe.wait_ge(s["sq_head"].sem, 2 * h + 2)
                pe.wait_ge(s["o_read"].sem, 2 * h + 2)
                s["head_ss"].on(wide((5, 7), [ones], [hg["sq"]]))

            project(0, 0)
            per = {used: 8, s["scored"]: 2, s["scored_s"]: 2, s["upd"]: 2, s["upd_s"]: 2, s["o_full"]: 4,
                   s["head_ss"]: 2}
            with looped(pe, H // 2 - 1, per) as i:
                project(1, i)
                scan(0, i)
                project(0, i + 1)
                scan(1, i)
            project(1, H // 2 - 1)
            scan(0, H // 2 - 1)
            scan(1, H // 2 - 1)

            def out_proj(phase, nslot, rhs, nk):
                base, ub = SLOTS[phase], USES[phase]
                for m in range(DC):
                    n = base + m * nslot
                    feature_tile(phase, n // R, [(n + k) % R for k in range(nslot)], m % 2, (ub + m) // 2, rhs, nk)

            pe.wait_ge(s["head_done"].sem, H)
            out_proj("wo", 1, lambda k: hg["og"][:, k, :], DC)

            def moe(layer):
                nr = 2 * layer + 1
                norm_sums(nr)
                wr = col("wr", LAYERS, DC, 20)
                for c in range(DC):
                    for half in range(2):
                        mm = pe.matmul(ps[0:20, 6 + half, 0:TH], wr[:, layer, c, :], hT[:, c, TH * half:TH * (half + 1)],
                                       start=(c == 0), stop=(c == DC - 1))
                s["lgT_full"].on(mm)
                pe.wait_ge(s["lg_ready"].sem, layer + 1)
                for j in range(TJ):
                    m = P if j < 4 else 64
                    mm = pe.transpose(ps[0:m, 3, 20 * j:20 * (j + 1)], mo["lgT"][0:20, P * j:P * j + m], ident[0:20, 0:20])
                s["lg_turned"].on(mm)
                for j in range(TJ):
                    m = P if j < 4 else 64
                    b0 = 4 + 2 * (j % 2)
                    pe.wait_ge(s["htok_ready"].sem, TJ * layer + max(j - 1, 0))
                    for c in range(DC):
                        mm = pe.transpose(ps[0:m, b0 + c // 4, P * (c % 4):P * (c % 4 + 1)],
                                          hT[:, c, P * j:P * j + m], ident)
                    s["htok_full"].on(mm)
                pe.wait_ge(s["comb_ready"].sem, layer + 1)
                ohg = mo["ohg"].rearrange("p a b -> p (a b)")
                pe.matmul(ps[:, 2, 0:20], strict, ohg, start=True, stop=True)
                s["ranked"].on(pe.matmul(ps[:, 2, 32:52], ones, ohg, start=True, stop=True))
                pe.wait_ge(s["place_ready"].sem, layer + 1)
                for j in range(TJ):
                    m = P if j < 4 else 64
                    dst = ps[:, 2, P * j:P * (j + 1)] if j < 4 else ps[:, 3, 0:64]
                    mm = pe.matmul(dst, ones[0:m, :], dg[0:m, j, 0:m], start=True, stop=True)
                s["pos_full"].on(mm)
                comb = mo["comb"].rearrange("p j a b -> p j (a b)")
                pe.wait_ge(s["spread"].sem, layer + 1)
                for half in range(2):
                    for j in range(TJ):
                        m = P if j < 4 else 64
                        mm = pe.matmul(ps[0:NE, half, 0:TW // 2], comb[0:m, j, :],
                                       mo["P"][0:m, j, TW // 2 * half:TW // 2 * (half + 1)],
                                       start=(j == 0), stop=(j == TJ - 1))
                s["cS_full"].on(mm)
                pe.wait_ge(s["cS_ready"].sem, layer + 1)
                pe.wait_ge(s["pos_ready"].sem, layer + 1)
                pe.wait_ge(s["htok_ready"].sem, TJ * (layer + 1))
                base, un = SLOTS[f"moe{layer}"] // R, USES[f"moe{layer}"]
                for c in range(DC):
                    p = c % 2
                    pe.wait_ge(pair_free[p].sem, (un + c) // 2)
                    for half in range(2):
                        for j in range(TJ):
                            m = P if j < 4 else 64
                            mm = pe.matmul(ps[:, 2 * p + half, 0:TH], h_tok[0:m, j, P * c:P * (c + 1)],
                                           mo["P"][0:m, j, TH * half:TH * (half + 1)], start=(j == 0), stop=(j == TJ - 1))
                    s["gathered"].on(mm)
                for p in range(2):
                    pe.wait_ge(pair_free[p].sem, (un + DC) // 2)
                ub = (un + DC) // 2
                with looped(pe, 2, {used: 2 * N_GROUP, s["cb_full"]: 2 * E, s["y_full"]: 2}) as i:
                    for gg in range(2):
                        g = 2 * i + gg
                        at_g = pe.value_load(off_i[0:1, bass.ds(g, 1)], min_val=0, max_val=T)
                        for e in range(E):
                            pe.wait_ge(s["ce_ready"].sem, E * g + (NE * layer + e + 1))
                            s["cb_full"].on(pe.matmul(ps[:, 2 * (e % 2) + 1, 0:W], ones[0:NE, :],
                                                      mo["ce"][0:NE, e % 2, :], start=True, stop=True))
                            for f in range(FT):
                                for p in range(2):
                                    r = (4 * e + 2 * f + p) % R
                                    pe.wait_ge(pair_free[p].sem, 16 * i + (ub + 8 * gg + 2 * e + f))
                                    pe.wait_ge(slot_full[r], 16 * (6 * i + (base + 3 * gg + e // 2 + 1)))
                                    for c in range(DC):
                                        mm = pe.matmul(ps[:, 2 * p, 0:W], ring[:, r, c * P:(c + 1) * P],
                                                       mo["hs"][:, c, bass.ds(at_g, W)], start=(c == 0), stop=(c == DC - 1))
                                    used.on(mm)
                        pe.wait_ge(s["yg_ready"].sem, 2 * g + (2 * G * layer + 1))
                        for k in range(KG):
                            pe.wait_ge(slot_full[k], 16 * (6 * i + (base + 3 * gg + 2 + 1)))
                            pe.wait_ge(s["hid_ready"].sem, KG * g + (KG * G * layer + k + 1))
                            for ch in range(2):
                                for half in range(2):
                                    mm = pe.matmul(ps[0:CH[ch], 4 + 2 * ch + half, :],
                                                   mo["hid"][:, gg, k, P * ch:P * ch + CH[ch]],
                                                   ring[:, k, 512 * half:512 * (half + 1)], start=(k == 0), stop=(k == KG - 1))
                                if k == KG - 1 and ch == 0:
                                    s["y_full"].on(mm)
                            used.on(mm)
                pe.wait_ge(s["yg_ready"].sem, 2 * G * (layer + 1) + 1)
                pe.wait_ge(s["pt_ready"].sem, 2 * G * (layer + 1))
                un += DC + 4 * NE
                for m in range(DC):
                    p = m % 2
                    pe.wait_ge(pair_free[p].sem, (un + m) // 2)
                    for half in range(2):
                        for q in range(2 * G):
                            n = CH[q % 2]
                            mm = pe.matmul(ps[:, 2 * p + half, 0:TH], mo["y"][0:n, q, P * m:P * (m + 1)],
                                           mo["PT"][0:n, q, TH * half:TH * (half + 1)], start=(q == 0), stop=(q == 2 * G - 1))
                    s["scattered"].on(mm)
                further_windows(layer)

            def further_windows(layer):
                pe.wait_ge(s["x_tile"].sem, DC * (2 * layer + 2))
                done, dve_done = x_pe[layer], x_dve[layer].sem
                with further(pe, {done: X_PE}) as (k, group, start):
                    for e in range(E):
                        pe.wait_ge(dve_done, X_DVE * k + (5 * e + 1))
                        pe.matmul(ps[:, 1, 0:W], ones[0:NE, :], mo["ce"][0:NE, 0, :], start=True, stop=True)
                        pe.wait_ge(x_w[layer], 96 * k + 16 * (e + 1))
                        for n, bank in enumerate((0, 2, 3, 4)):
                            for c in range(DC):
                                mm = pe.matmul(ps[:, bank, 0:W], xw[:, n, c * P:(c + 1) * P],
                                               mo["hs"][:, c, bass.ds(start, W)], start=(c == 0), stop=(c == DC - 1))
                        done.on(mm)
                    pe.wait_ge(dve_done, X_DVE * k + (5 * E + 2))
                    for b in range(2):
                        pe.wait_ge(x_w[layer], 96 * k + 16 * (E + b + 1))
                        for kk in range(4):
                            n = 4 * b + kk
                            for ch in range(2):
                                for half in range(2):
                                    mm = pe.matmul(ps[0:CH[ch], 4 + 2 * ch + half, :], xhid[:, n, P * ch:P * ch + CH[ch]],
                                                   xw[:, kk, 512 * half:512 * (half + 1)], start=(n == 0), stop=(n == KG - 1))
                        done.on(mm)
                    pe.wait_ge(x_act[layer].sem, X_ACT * k + X_ACT)
                    for m in range(DC):
                        p = m % 2
                        if m >= 2:
                            pe.wait_ge(dve_done, X_DVE * k + (5 * E + 2 + 4 * (m - 1)))
                        for half in range(2):
                            for q in range(2):
                                mm = pe.matmul(ps[:, 2 * p + half, 0:TH], xy[0:CH[q], q, P * m:P * (m + 1)],
                                               mo["PT"][0:CH[q], q, TH * half:TH * (half + 1)], start=(q == 0), stop=(q == 1))
                        done.on(mm)
                    pe.wait_ge(dve_done, X_DVE * (k + 1))

            moe(0)
            ada_rows(1)
            norm_sums(2)

            sx, ux = SLOTS["xm"] // R, USES["xm"] // 2

            def values_and_gates(j, k):
                u, i = k % 2, 8 * j + k
                pe.wait_ge(s["bdv_ready"].sem, i + 1)
                pe.wait_ge(s["xm_ready"].sem, 3 * i + 3)
                pe.wait_ge(pair_free[u].sem, ux + i // 2 + 1)
                pe.wait_ge(s["v_read"].sem, i)
                for t in range(4):
                    pe.matmul(ps[:, 4, P * t:P * (t + 1)], first["xpad"][:, u, 3 + P * t:3 + P * (t + 1)],
                              first["bdv"][:, u, :], start=True, stop=True)
                mm = pe.matmul(ps[0:64, 5, 0:P], first["xs"][:, u, :], first["bdv"][:, u, :], start=True, stop=True)
                s["v_full"].on(mm)
                pe.wait_ge(s["xc_ready"].sem, i + 1)
                return i, u, ml["xc"][:, i, :]

            def gates(j, k, start, stop):
                i, u, xc_i = values_and_gates(j, k)
                gm, gx = first["gm"][:, u, :], first["gx"][:, u, :]
                pe.matmul(ps[0:64, 6, 0:TP], gm, first["xpad"][:, u, 3:3 + TP], start=start, stop=False)
                pe.matmul(ps[0:64, 6, 0:TP], gx, xc_i[:, 0:TP], start=False, stop=stop)
                pe.matmul(ps[0:64, 7, 0:64], gm, first["xs"][:, u, :], start=start, stop=False)
                s["gates_full"].on(pe.matmul(ps[0:64, 7, 0:64], gx, xc_i[:, TP:T], start=False, stop=stop))

            for j in range(2):
                for k in range(8):
                    feature_tile("xm", sx + j, [k], k % 2, ux + 4 * j + k // 2, h_rhs, DC)
                    if k:
                        gates(j, k - 1, j == 0 and k == 1, False)
                gates(j, 7, False, j == 1)

            pe.wait_ge(s["rows_ready"].sem, 1)
            for n, src in enumerate((gate["u"], gate["t1"])):
                for j in range(TJ):
                    m = P if j < 4 else 64
                    mm = pe.transpose(ps[0:m, 4, 32 * n + MH * j:32 * n + MH * (j + 1)], src[0:MH, P * j:P * j + m],
                                      ident[0:MH, 0:MH])
            s["turned_g"].on(mm)
            pe.wait_ge(s["tok_ready"].sem, 2)

            ub = USES["b"]
            un = [ub]

            def use():
                n = un[0]
                un[0] += 1
                pe.wait_ge(pair_free[n % 2].sem, n // 2)
                return n % 2

            def gate_tile(h, i):
                n = SLOTS["z"] + HT * h + i
                m = un[0]
                un[0] += 1
                feature_tile("z", n // R, [n % R], m % 2, m // 2, h_rhs, DC)

            full = s["b_full"]
            weighted = [mx[f"P{j}"] for j in range(4)]
            bdq = ml["W"].rearrange("p a b -> p (a b)")
            for h in range(MH):
                hb = ub + N_HEADB * h
                for k in range(4):
                    p = use()
                    sel = ident[32 * k:32 * k + MH, 32 * k + h:32 * k + h + 1].broadcast_to([MH, P])
                    row = ml["rows"][32 * k:32 * k + MH, :]
                    if k < 3:
                        mm = wide((2 * p, 2 * p + 1), [sel], [row])
                    else:
                        mm = pe.matmul(ps[:, 2 * p, 0:64], sel, row[:, TP:T], start=True, stop=True)
                    full.on(mm)
                pe.wait_ge(s["bd_ready"].sem, h + 1)
                for w in range(2):
                    for i in range(HT):
                        p = use()
                        at = (HT * w + i) * P
                        full.on(wide((2 * p, 2 * p + 1), [bdq[:, at:at + P]], [ml["xc"][:, HT * h + i, :]]))
                pe.wait_ge(s["c_done"].sem, HT * NB * h)
                pe.wait_ge(s["cp_ready"].sem, HT * h)
                for j in range(TJ):
                    m = P if j < 4 else 64
                    bank = 4 + j if j < 4 else 2 * use()
                    for i in range(HT):
                        mm = pe.matmul(ps[0:m, bank, P * i:P * (i + 1)], ml["xc"][:, HT * h + i, P * j:P * j + m],
                                       bdq[:, (HT + i) * P:(HT + i + 1) * P], start=True, stop=True)
                s["kt_full"].on(mm)
                pe.wait_ge(pair_free[(hb + 12) % 2].sem, (hb + 12) // 2 + 1)
                for j in range(TJ):
                    m = P if j < 4 else 64
                    bank = 4 + j if j < 4 else 2 * use()
                    hi = TP if j < 4 else T
                    for p in range(2):
                        pe.wait_ge(pair_free[p].sem, (ub + N_HEADB * h + 12) // 2)
                    for i in range(HT):
                        mm = pe.matmul(ps[0:m, bank, 0:hi - P * j], ml["kz"][:, i, P * j:P * j + m],
                                       ml["q"][:, i, P * j:hi], start=(i == 0), stop=(i == HT - 1))
                s["s_full"].on(mm)
                gate_tile(h, 0)
                pe.wait_ge(s["p_ready"].sem, 5 * h + 5)
                pe.wait_ge(s["qw_ready"].sem, h + 1)
                p = use()
                samples = ps[0:64, 2 * p, :]
                dn = ps[:, 2 * p + 1, 0:64]
                pe.matmul(dn, ones[0:64, :], mx["Ps"][0:64, :], start=True, stop=False)
                for i in range(HT):
                    mm = pe.matmul(dn, ones, qn[:, i, :], start=False, stop=(i == HT - 1))
                s["num_s"].on(mm)
                for b in range(NB):
                    n = NB * h + b
                    C = shaped(ml["C"][:, n % 2, :], HT, MD)
                    pe.wait_ge(s["alone_ready"].sem, n + 1)
                    for k in range(HT):
                        if k % 2 == 0:
                            pe.wait_ge(c_in[n % 2][k // 2], 16 * (n // 2 + 1))
                        mm = pe.matmul(samples, alone[:, b % 2, k, :], C[:, k, :], start=(b + k == 0), stop=False,
                                       skip_group_check=True)
                    s["num_s"].on(mm)
                    pe.wait_ge(s["kb_ready"].sem, n + 1)
                    for k in range(HT):
                        if n:
                            pe.wait_ge(s["c_done"].sem, HT * (n - 1) + k + 1)
                        mm = pe.matmul(ps[:, 4 + k, :], mx["kb"][0:64, P * k:P * (k + 1)],
                                       ml["vtok"][0:64, 4, MD * h:MD * (h + 1)], start=True, stop=True)
                        s["upd_c"].on(mm)
                s["num_full"].on(pe.matmul(samples, mx["Ps"][0:64, :], ml["vtok"][0:64, 4, MD * h:MD * (h + 1)],
                                           start=False, stop=True, skip_group_check=True))
                pe.wait_ge(s["c_done"].sem, HT * NB * (h + 1))
                for k in range(HT):
                    for j in range(4):
                        mm = pe.matmul(ps[:, 4 + k, :], ml["ktok"][:, j, P * k:P * (k + 1)],
                                       ml["vtok"][:, j, MD * h:MD * (h + 1)], start=(j == 0), stop=(j == 3))
                    s["cp_full"].on(mm)
                pe.wait_ge(s["raw_ready"].sem, h + 1)
                for i in range(HT):
                    mm = pe.transpose(ps[:, 2 * p, 64 * i:64 * (i + 1)], mx["kb"][0:64, P * i:P * (i + 1)], ident[0:64, 0:64])
                s["turned_s"].on(mm)
                for i in range(HT + 1):
                    p = use()
                    for j in range(4):
                        lhs = ones if i == 0 else ml["vtok"][:, j, MD * h + P * (i - 1):MD * h + P * i]
                        mm = pe.matmul(ps[:, 2 * p, P * j:TP], lhs, weighted[j], start=(j == 0), stop=(j == 3),
                                       skip_group_check=True)
                    full.on(mm)
                gate_tile(h, 1)
                pe.wait_ge(pair_free[(hb + 20) % 2].sem, (hb + 20) // 2 + 1)
                p = use()
                s["mu_full"].on(wide((2 * p, 2 * p + 1), [ones] * HT, [ml["q"][:, i, :] for i in range(HT)]))
                gate_tile(h, 2)
                pe.wait_ge(s["sqh_ready"].sem, h + 1)
                p = use()
                sqh = shaped(ml["ktok"].rearrange("p a b -> p (a b)")[:, 0:HT * T], HT, T)
                s["var_full"].on(wide((2 * p, 2 * p + 1), [ones] * HT, [sqh[:, i, :] for i in range(HT)]))
                gate_tile(h, 3)
            assert un[0] == USES["md"], (un[0], USES["md"])
            pe.wait_ge(s["ho_ready"].sem, MH)
            out_proj("md", 2, lambda k: ml["xc"][:, k, :], MT)
            moe(1)
            norm_sums(4)

        def halves(p):
            return ps[:, 2 * p:2 * p + 2, 0:TH]

        def two(ap):
            return ap.rearrange("p (a n) -> p a n", a=2)

        def at(tensor, i):
            return tensor[:, i] if isinstance(i, int) else tensor[:, bass.ds(i, 1)].rearrange(
                "p a n -> p (a n)")

        KS = float(MD) ** -0.5

        @block.scalar
        def _(act):
            A = s["act"]
            used = s["slot_used"].sem

            def norm(n):
                for c in range(DC):
                    if n:
                        act.wait_ge(s["x_tile"].sem, DC * (n - 1) + c + 1)
                    s["sq_ready"].on(act.activation(hT[:, c, :], xT[:, c, :], ACT.Square))
                act.wait_ge(s["ss_ready"].sem, n + 1)
                A.link(act, act.activation(two(rstd), halves(3), ACT.Ln, bias=eps, scale=1.0 / D))
                s["rstd_ready"].on(act.activation(rstd, rstd, ACT.Exp, scale=-0.5))

            def ada_rows(layer):
                base, ub = SLOTS[f"ada{layer}"], USES[f"ada{layer}"] // 2
                with looped(act, 6, {}) as i:
                    for p in range(2):
                        act.wait_ge(used, R * i + (base + 4 * (p + 1)))
                        dst = ada["modrow"][0:NV, bass.ds((2 * i + p) * 512, 512)]
                        pair_free[p].on(act.copy(dst, ps[0:NV, 2 * p, :]))

            for p in range(2):
                act.sem_inc(pair_free[p].sem, 1)
            for n in ("head_rs", "yg_ready"):
                act.sem_inc(s[n].sem, 1)
                s[n].base = 1
            act.wait_ge(small_in, 16)
            s["silc"].on(act.activation(silc, silc, ACT.Silu))
            ada_rows(0)
            act.wait_ge(x_in, 16)
            norm(0)

            act.wait_ge(s["lb_in"].sem, 1)
            s["lb_out"].on(act.activation(hg["t1"], hg["t1"], ACT.Exp))
            base = SLOTS["hg"]

            def evict(u, h, guarded):
                if guarded:
                    act.wait_ge(s["head_done"].sem, h - 1)
                for q, (dst, f, k) in enumerate(((hg["th"], ACT.Tanh, 0.5), (hg["q"], ACT.Silu, 1.0),
                                                 (hg["zg"], ACT.Silu, 1.0))):
                    act.wait_ge(used, 4 * h + (base + q + 1))
                    pair_free[q % 2].on(act.activation(two(dst[:, u, :]), halves(q % 2), f, scale=k))
                act.wait_ge(used, 4 * h + (base + 4))
                act.copy(hg["v"][:, u, 0:512], ps[:, 2, :])
                pair_free[1].on(act.copy(hg["v"][0:64, u, 512:512 + P], ps[0:64, 3, 0:P]))

            def exponentials(h):
                act.wait_ge(s["decay"].sem, h + 1)
                s["f_ready"].on(act.activation(hg["g"], hg["g"], ACT.Ln))
                act.wait_ge(s["diffs"].sem, 3 * h + 1)
                A.link(act, act.activation(hg["Ks"], hg["eq"][:, TP:T], ACT.Exp, scale=-1.0))
                s["exps"].on(act.activation(hg["eq"], hg["eq"], ACT.Exp))
                act.wait_ge(s["diffs"].sem, 3 * h + 2)
                s["exps"].on(act.activation(hg["K"], hg["K"], ACT.Exp))
                act.wait_ge(s["diffs"].sem, 3 * h + 3)
                s["exps"].on(act.activation(hg["qe"], hg["b"], ACT.Exp))
                s["exps"].on(act.activation(hg["kw"], hg["kw"], ACT.Exp))

            def head_norm(h):
                act.wait_ge(s["o_read"].sem, 2 * h + 1)
                s["sq_head"].on(act.activation(hg["sq"][:, 0:TP], ps[:, 5, :], ACT.Square))
                act.wait_ge(s["o_read"].sem, 2 * h + 2)
                s["sq_head"].on(act.activation(hg["sq"][:, TP:T], ps[:, 7, 0:64], ACT.Square))
                act.wait_ge(s["head_ss"].sem, h + 1)
                act.activation(hg["rs"][:, 0:TH], ps[:, 5, 0:TH], ACT.Ln, bias=eps, scale=1.0 / P)
                A.link(act, act.activation(hg["rs"][:, TH:T], ps[:, 7, 0:TH], ACT.Ln, bias=eps, scale=1.0 / P))
                s["head_rs"].on(act.activation(hg["rs"], hg["rs"], ACT.Exp, scale=-0.5))

            evict(0, 0, False)
            exponentials(0)
            evict(1, 1, False)
            head_norm(0)
            per = {A: 4, s["f_ready"]: 2, s["exps"]: 8, s["sq_head"]: 4, s["head_rs"]: 2}
            with looped(act, H // 2 - 1, per) as i:
                for u in range(2):
                    h = 2 * i + (u + 1)
                    exponentials(h)
                    evict(u, h + 1, True)
                    head_norm(h)
            exponentials(H - 1)
            head_norm(H - 1)

            def moe(layer):
                norm(2 * layer + 1)
                act.wait_ge(s["lgT_full"].sem, layer + 1)
                act.wait_ge(sn_out, 32 * H)
                s["lg_ready"].on(act.activation(two(mo["lgT"][0:20, :]), ps[0:20, 6:8, 0:TH], ACT.Identity,
                                                bias=col("rb")[0:20, layer:layer + 1]))
                for j in range(TJ):
                    m = P if j < 4 else 64
                    act.wait_ge(s["htok_full"].sem, TJ * layer + j + 1)
                    b0 = 4 + 2 * (j % 2)
                    s["htok_ready"].on(act.copy(h_tok[0:m, j, :].rearrange("p (a n) -> p a n", a=2), ps[0:m, b0:b0 + 2, :]))
                act.wait_ge(s["top_in"].sem, layer + 1)
                A.link(act, act.activation(mo["r1"], mo["r1"], ACT.Exp))
                s["top_out"].on(act.activation(mo["s2"], mo["s2"], ACT.Exp))
                act.wait_ge(s["pos_full"].sem, layer + 1)
                A.link(act, act.copy(pos_row[:, 0:TP], ps[:, 2, :]))
                s["pos_ready"].on(act.copy(pos_row[:, TP:T], ps[:, 3, 0:64]))
                act.wait_ge(s["cS_full"].sem, layer + 1)
                s["cS_ready"].on(act.copy(mo["cS"][0:NE, :].rearrange("p (a n) -> p a n", a=2), ps[0:NE, 0:2, 0:TW // 2]))
                for c in range(DC):
                    act.wait_ge(s["gathered"].sem, DC * layer + c + 1)
                    pair_free[c % 2].on(act.copy(two(mo["hs"][:, c, 0:T]), halves(c % 2)))
                base, ub = SLOTS[f"moe{layer}"], (USES[f"moe{layer}"] + DC) // 2
                with looped(act, 2, {s["yg_ready"]: 2 * 2}) as i:
                    for gg in range(2):
                        for t in range(E * FT):
                            act.wait_ge(used, 2 * N_GROUP * i + (base + N_GROUP * gg + 2 * t + 1))
                            act.wait_ge(pair_free[1].sem, 16 * i + (ub + 8 * gg + t))
                            pair_free[0].on(act.activation(mo["sil"], ps[:, 0, 0:W], ACT.Silu))
                        y = mo["y"][:, bass.ds(4 * i + 2 * gg, 2), :]
                        act.wait_ge(s["y_full"].sem, 2 * i + (2 * 2 * layer + gg + 1))
                        s["yg_ready"].on(act.copy(y[:, 0, :].rearrange("p (a n) -> p a n", a=2), ps[:, 4:6, :]))
                        act.wait_ge(used, 2 * N_GROUP * i + (base + N_GROUP * (gg + 1)))
                        s["yg_ready"].on(act.copy(y[0:CH[1], 1, :].rearrange("p (a n) -> p a n", a=2), ps[0:CH[1], 6:8, :]))

            def further_windows(layer):
                done = x_act[layer]
                act.wait_ge(s["x_tile"].sem, DC * (2 * layer + 2))
                for k in range(MORE):
                    with further_one(act, k):
                        for e in range(E):
                            act.wait_ge(x_pe[layer].sem, X_PE * k + (e + 2))
                            act.activation(mo["sil"], ps[:, 0, 0:W], ACT.Silu)
                            done.on(act.activation(mo["hid"][:, 1, 0, :], ps[:, 3, 0:W], ACT.Silu))
                        act.wait_ge(x_pe[layer].sem, X_PE * k + 7)
                        act.copy(xy[:, 0, :].rearrange("p (a n) -> p a n", a=2), ps[:, 4:6, :])
                        done.on(act.copy(xy[0:CH[1], 1, :].rearrange("p (a n) -> p a n", a=2), ps[0:CH[1], 6:8, :]))
                        act.wait_ge(x_dve[layer].sem, X_DVE * (k + 1))

            moe(0)
            further_windows(0)
            ada_rows(1)
            norm(2)

            base = SLOTS["xm"]

            def inner(u, i, guarded):
                act.wait_ge(used, i + (base + 1))
                if guarded:
                    act.wait_ge(s["gates_full"].sem, i - 1)
                    act.wait_ge(s["conv_acc"].sem, i - 1)
                xp = first["xpad"][:, u, :]
                s["xm_ready"].on(act.copy(xp[:, 3:3 + TH], ps[:, 2 * u, 0:TH]))
                s["xm_ready"].on(act.copy(xp[:, 3 + TH:3 + TP], ps[:, 2 * u + 1, 0:TP - TH]))
                src = ps[:, 2 * u + 1, TP - TH:TH].rearrange("p (b t) -> p b t", b=NB)
                s["xm_ready"].on(act.copy(xp[:, 3 + TP:].rearrange("p (b t) -> p b t", b=NB)[:, :, 3:], src))
                pair_free[u].on(act.copy(first["xs"][:, u, :].rearrange("p (b t) -> p b t", b=NB), src))
                act.wait_ge(s["conv_acc"].sem, i + 1)
                s["xc_ready"].on(act.activation(at(ml["xc"], i), first["acc"], ACT.Silu))

            inner(0, 0, False)
            inner(1, 1, False)
            with looped(act, MT // 2 - 1, {s["xm_ready"]: 6, s["xc_ready"]: 2}) as i:
                for u in range(2):
                    inner(u, 2 * i + (u + 2), True)

            act.wait_ge(s["abs_ready"].sem, 1)
            t1, t2, gb = gate["t1"][0:MH, :], gate["t2"][0:MH, :], gate["b"][0:MH, :]
            A.link(act, act.activation(t2, t2, ACT.Exp, scale=-1.0))
            s["soft_ready"].on(act.activation(t2, t2, ACT.Ln, bias=ones[0:MH, 0:1]))
            act.wait_ge(s["dec_ready"].sem, 1)
            A.link(act, act.activation(t1, t1, ACT.Exp))
            s["dec_exp"].on(act.activation(gb[:, TP:T], gb[:, TP:T], ACT.Exp))

            act.wait_ge(x_kept, 16)
            un = [USES["b"]]

            def use(sem, value):
                n = un[0]
                un[0] += 1
                act.wait_ge(sem, value)
                return n % 2

            nf = [0]

            def read_full():
                nf[0] += 1
                return use(s["b_full"].sem, nf[0])

            def output_gate(h, i):
                p = use(used, SLOTS["z"] + HT * h + i + 1)
                pair_free[p].on(act.activation(two(ml["kz"][:, i, :]), halves(p), ACT.Silu))

            for h in range(MH):
                act.wait_ge(s["ho_ready"].sem, h)
                p = read_full()
                pair_free[p].on(act.copy(two(mx["nM"]), halves(p)))
                p = read_full()
                pair_free[p].on(act.activation(two(mx["emn"]), halves(p), ACT.Exp, scale=-1.0))
                p = read_full()
                pair_free[p].on(act.copy(two(mx["mu"]), halves(p)))
                p = read_full()
                pair_free[p].on(act.copy(mx["wcb"], ps[:, 2 * p, 0:64]))
                for i in range(HT):
                    p = read_full()
                    pair_free[p].on(act.copy(two(ml["q"][:, i, :]), halves(p)))
                for i in range(HT):
                    p = read_full()
                    pair_free[p].on(act.activation(two(ml["kz"][:, i, :]), halves(p), ACT.Identity, scale=KS))
                un[0] += 2
                for j in range(TJ):
                    act.wait_ge(s["w_ready"].sem, 5 * h + j + 1)
                    n = TP - P * j if j < 4 else 64
                    w = ml["W"][:, j % 2, 0:n] if j < 4 else ml["W"][0:64, 0, 0:64]
                    s["w_exp"].on(act.activation(w, w, ACT.Exp))
                act.wait_ge(s["n_ready"].sem, h + 1)
                act.wait_ge(s["s_full"].sem, h + 1)
                output_gate(h, 0)
                un[0] += 1
                for b in range(NB):
                    n = NB * h + b
                    act.wait_ge(s["upd_c"].sem, HT * n)
                    s["kb_ready"].on(act.activation(mx["kb"][0:64, :], ml["ktok"][0:64, 4, :], ACT.Identity,
                                                    scale=own[0:64, b:b + 1]))
                act.wait_ge(s["num_full"].sem, h + 1)
                s["raw_ready"].on(act.copy(mx["kb"][0:64, :], ps[0:64, 2 * ((un[0] - 1) % 2), :]))
                for k in range(HT):
                    n = HT * h + k
                    act.wait_ge(s["cp_full"].sem, n + 1)
                    if n >= 2:
                        act.wait_ge(cp_out[k % 2], 16 * (n // 2))
                    s["cp_ready"].on(act.copy(ml["W"][:, k % 2, :], ps[:, 4 + k, :]))
                un[0] += 5
                nf[0] += 5
                output_gate(h, 1)
                un[0] += 1
                act.wait_ge(s["rs_h"].sem, h + 1)
                sqh = shaped(ml["ktok"].rearrange("p a b -> p (a b)")[:, 0:HT * T], HT, T)
                s["sqh_ready"].on(act.activation(sqh, ml["q"], ACT.Square))
                output_gate(h, 2)
                n = un[0]
                p = use(s["var_full"].sem, h + 1)
                pair_free[p].on(act.activation(two(mx["rs"]), halves(p), ACT.Ln, bias=eps, scale=1.0 / MD))
                act.wait_ge(pair_free[p].sem, n // 2 + 1)
                s["rsh_ready"].on(act.activation(mx["rs"], mx["rs"], ACT.Exp, scale=-0.5))
                output_gate(h, 3)
            moe(1)
            further_windows(1)
            norm(4)

        @block.vector
        def _(dve):
            V = s["dve"]
            used = s["slot_used"].sem
            tt, ts, stt = dve.tensor_tensor, dve.tensor_scalar, dve.scalar_tensor_tensor

            def over_t(ap):
                return ap.unsqueeze(len(ap.shape)).broadcast_to(list(ap.shape) + [TS])

            def by_seq(ap):
                return ap.rearrange("p (b t) -> p b t", b=NB)

            def modulation(layer):
                dve.wait_ge(s["turned"].sem, layer + 1)
                V.link(dve, tt(modt, shaped(ps[:, 4, 0:48 * NV], 48, NV),
                               col("bada", LAYERS, 48)[:, layer, :].unsqueeze(2).broadcast_to([P, 48, NV]), ALU.add))
                for k in range(2):
                    g = col("ng", LAYERS, 2, DC)[:, layer, k, :].unsqueeze(2).broadcast_to([P, DC, NV])
                    V.link(dve, stt(amod[:, k], modt[:, 24 * k + 8:24 * k + 16, :], 1.0, g, ALU.add, ALU.mult))

            def norm(n):
                k = n % 2
                dve.wait_ge(s["rstd_ready"].sem, n + 1)
                V.link(dve, tt(hT, xT, rstd.unsqueeze(1).broadcast_to([P, DC, T]), ALU.mult))
                if n == 2 * LAYERS:
                    for c in range(DC):
                        ins = ts(hT[:, c, :], hT[:, c, :], col("fg")[:, c:c + 1], None, ALU.mult)
                    s["y_ready"].on(ins)
                    return
                for c in range(DC):
                    ts(hT[:, c, 0:TP], hT[:, c, 0:TP], amod[:, k, c, 0:1], modt[:, 24 * k + c, 0:1], ALU.mult, ALU.add)
                hs = hT[:, :, TP:T].rearrange("p c (b t) -> p c b t", b=NB)
                V.link(dve, tt(hs, hs, over_t(amod[:, k, :, 1:NV]), ALU.mult))
                s["h_ready"].link(dve, tt(hs, hs, over_t(modt[:, 24 * k:24 * k + DC, 1:NV]), ALU.add))

            def gated(full, base, nslot, use, k, tmp):
                for m in range(DC):
                    p = m % 2
                    dve.wait_ge(full, base + (m + 1) * nslot)
                    g = modt[:, 24 * k + 16 + m, :]
                    stt(xT[:, m, 0:TH], ps[:, 2 * p, 0:TH], g[:, 0:1], xT[:, m, 0:TH], ALU.mult, ALU.add)
                    stt(xT[:, m, TH:TP], ps[:, 2 * p + 1, 0:TP - TH], g[:, 0:1], xT[:, m, TH:TP], ALU.mult, ALU.add)
                    pair_free[p].on(tt(by_seq(tmp), by_seq(ps[:, 2 * p + 1, TP - TH:TH]), over_t(g[:, 1:NV]), ALU.mult))
                    dve.wait_ge(pair_free[p].sem, (use + m) // 2 + 1)
                    s["x_tile"].link(dve, tt(xT[:, m, TP:T], xT[:, m, TP:T], tmp, ALU.add))

            dve.wait_ge(small_in, 16)
            modulation(0)
            norm(0)
            lb = col("lb", 3, H)
            V.link(dve, tt(hg["t2"], lb[:, 0], lb[:, 1], ALU.max))
            V.link(dve, tt(hg["t2"], hg["t2"], lb[:, 2], ALU.max))
            s["lb_in"].on(tt(hg["t1"], lb, hg["t2"].unsqueeze(1).broadcast_to([P, 3, H]), ALU.subtract))
            dve.wait_ge(s["lb_out"].sem, 1)
            V.link(dve, tt(hg["t2"], hg["t1"][:, 0], hg["t1"][:, 1], ALU.add))
            V.link(dve, tt(hg["t2"], hg["t2"], hg["t1"][:, 2], ALU.add))
            V.link(dve, dve.reciprocal(hg["t2"], hg["t2"]))
            V.link(dve, tt(hg["t2"], hg["t1"][:, 0], hg["t2"], ALU.mult))
            V.link(dve, ts(hg["half"], hg["t2"], -0.5, 0.5, ALU.mult, ALU.add))
            V.link(dve, tt(hg["low"], hg["half"], hg["t2"], ALU.add))

            uh = USES["hg"] // 2

            def elementwise(u, h):
                th, q = hg["th"][:, u, :], hg["q"][:, u, :]
                k, g, b, eq, K, Ks, qe, kw = (hg[n] for n in ("k", "g", "b", "eq", "K", "Ks", "qe", "kw"))
                half = hg["half"][:, h:h + 1] if isinstance(h, int) else hg["half"][:, bass.ds(h, 1)]
                low = hg["low"][:, h:h + 1] if isinstance(h, int) else hg["low"][:, bass.ds(h, 1)]
                dve.wait_ge(pair_free[0].sem, 2 * h + (uh + 1))
                V.link(dve, ts(g, th, half, low, ALU.mult, ALU.add))
                s["decay"].link(dve, ts(k, g, -1.0, 1.0, ALU.mult, ALU.add))
                dve.wait_ge(s["f_ready"].sem, h + 1)
                V.link(dve, dve.tensor_tensor_scan(b, keep, g, 0.0, ALU.mult, ALU.add))
                b3 = b[:, 0:TP].rearrange("p (i t) -> p i t", t=BLK)
                mid = b3[:, :, BLK // 2]
                bs = by_seq(b[:, TP:T])
                tt(eq[:, 0:TP].rearrange("p (i t) -> p i t", t=BLK), b3,
                   mid.unsqueeze(2).broadcast_to([P, 16, BLK]), ALU.subtract)
                s["diffs"].on(tt(by_seq(eq[:, TP:T]), bs, over_t(bs[:, :, TS // 2]), ALU.subtract))
                V.link(dve, tt(K.rearrange("p (c i) t -> p c i t", c=4),
                               mid.rearrange("p (c i) -> p c i", c=4).unsqueeze(3).broadcast_to([P, 4, 4, P]),
                               b[:, 0:TP].rearrange("p (c t) -> p c t", c=4).unsqueeze(2).broadcast_to([P, 4, 4, P]),
                               ALU.subtract))
                s["diffs"].on(dve.tensor_scalar_min(K, K, CLAMP))
                bc = b[:, 0:TP].rearrange("p (c t) -> p c t", c=4)
                tt(kw[:, 0:TP].rearrange("p (c t) -> p c t", c=4),
                   bc[:, :, P - 1].unsqueeze(2).broadcast_to([P, 4, P]), bc, ALU.subtract)
                s["diffs"].on(tt(by_seq(kw[:, TP:T]), over_t(bs[:, :, TS - 1]), bs, ALU.subtract))
                dve.wait_ge(pair_free[1].sem, 2 * h + (uh + 1))
                dve.wait_ge(s["exps"].sem, 4 * h + 1)
                tt(eq, q, eq, ALU.mult)
                tt(Ks, k[:, TP:T], Ks, ALU.mult)
                dve.wait_ge(s["exps"].sem, 4 * h + 2)
                K4 = K.rearrange("p (c i) t -> p c i t", c=4)
                tt(K4, K4, k[:, 0:TP].rearrange("p (c t) -> p c t", c=4).unsqueeze(2).broadcast_to([P, 4, 4, P]),
                   ALU.mult)
                dve.wait_ge(s["exps"].sem, 4 * h + 4)
                el = hg["sq"][:, 0:12]
                tt(el[:, 0:4].unsqueeze(2), qe[:, 0:TP].rearrange("p (c t) -> p c t", c=4)[:, :, P - 1:P],
                   col("ones")[:, 0:4].unsqueeze(2), ALU.mult)
                V.link(dve, tt(el[:, 4:12].unsqueeze(2), by_seq(qe[:, TP:T])[:, :, TS - 1:TS],
                               col("ones")[:, 0:8].unsqueeze(2), ALU.mult))
                V.link(dve, dve.tensor_copy(hg["t1"].rearrange("p a b -> p (a b)")[:, 0:12], el))
                tt(qe, q, qe, ALU.mult)
                s["elem_ready"].on(tt(kw, k, kw, ALU.mult))

            def scan(u, pair):
                h = 2 * pair + u
                v = shaped(hg["v"][:, u, :], TJ, P)
                el = hg["t1"].rearrange("p a b -> p (a b)")
                dve.wait_ge(s["scored"].sem, h + 1)
                tt(hg["at"][:, 0:4, :], shaped(ps[:, 4, :], 4, P), causal.unsqueeze(1).broadcast_to([P, 4, P]), ALU.mult)
                s["at_ready"].on(dve.tensor_copy(hg["ktw"][:, 0:4, :], shaped(ps[:, 6, :], 4, P)))
                dve.wait_ge(s["scored_s"].sem, h + 1)
                tt(hg["at"][0:64, 4, 0:64], ps[0:64, 5, 0:64], causal_s[0:64, :], ALU.mult)
                s["at_ready"].on(dve.tensor_copy(hg["ktw"][0:64, 4, :], ps[0:64, 5, P:2 * P]))
                dve.wait_ge(pair_free[1].sem, 2 * h + (uh + 2))
                s["vx_ready"].on(tt(hg["Vx"][0:64], v[0:64, 4, :].unsqueeze(1).broadcast_to([64, NB, P]),
                                    own[0:64, :].unsqueeze(2).broadcast_to([64, NB, P]), ALU.mult))
                dve.wait_ge(s["upd"].sem, h + 1)
                dve.wait_ge(s["sn_kept"].sem, h + 1)
                s["s_ready"].link(dve, dve.tensor_copy(hg["S"][:, 0, :], ps[:, 7, 0:P]))
                for c in range(1, 4):
                    s["s_ready"].link(dve, stt(hg["S"][:, c, :], hg["S"][:, c - 1, :], el[:, c:c + 1],
                                               ps[:, 7, c * P:(c + 1) * P], ALU.mult, ALU.add))
                dve.wait_ge(s["upd_s"].sem, h + 1)
                dve.wait_ge(s0_in[u], 16 * (pair + 1))
                Sn = hg["Sn"]
                V.link(dve, tt(Sn, shaped(hg["S0"][:, u, :], NB, P), el[:, 4:12].unsqueeze(2).broadcast_to([P, NB, P]),
                               ALU.mult))
                Sn2 = Sn.rearrange("p (a b) n -> p a (b n)", a=2)
                tt(Sn2[:, 0], Sn2[:, 0], ps[:, 4, :], ALU.add)
                s["sn_ready"].on(tt(Sn2[:, 1], Sn2[:, 1], ps[:, 6, :], ALU.add))
                og = at(hg["og"], h)
                gn = col("hgn")
                dve.wait_ge(s["o_full"].sem, 2 * h + 1)
                s["o_read"].on(ts(og[:, 0:TP], ps[:, 5, :], gn, None, ALU.mult))
                dve.wait_ge(s["o_full"].sem, 2 * h + 2)
                s["o_read"].link(dve, ts(og[:, TP:T], ps[:, 7, 0:64], gn, None, ALU.mult))
                dve.wait_ge(s["head_rs"].sem, h + 2)
                V.link(dve, tt(og, og, hg["rs"], ALU.mult))
                dve.wait_ge(pair_free[0].sem, 2 * h + (uh + 2))
                s["head_done"].link(dve, tt(og, og, hg["zg"][:, u, :], ALU.mult))

            names = {"decay": 1, "diffs": 3, "elem_ready": 1, "at_ready": 2, "vx_ready": 1, "s_ready": 4,
                     "sn_ready": 1, "o_read": 2, "head_done": 1}
            per = {s[n]: 2 * k for n, k in names.items()} | {V: 2 * 7}
            with looped(dve, H // 2, per) as i:
                for u in range(2):
                    elementwise(u, 2 * i + u)
                    scan(u, i)
            gated(used, SLOTS["wo"], 1, USES["wo"], 0, hg["sq"][:, 0:64])

            def first_of(dst, eq, tmp, s1):
                rank = col("rank").unsqueeze(1).broadcast_to([P, TJ, 4])
                V.link(dve, tt(tmp, eq, rank, ALU.mult))
                V.link(dve, dve.tensor_reduce(s1, tmp, AX.X, ALU.max))
                V.link(dve, tt(dst, tmp, s1.unsqueeze(2).broadcast_to([P, TJ, 4]), ALU.is_equal))

            def moe(layer):
                norm(2 * layer + 1)
                lg, r1, r2, r3, s1, s2, s3, s4, pst = (mo[n] for n in "lg r1 r2 r3 s1 s2 s3 s4 ps".split())
                four = lambda ap: ap.unsqueeze(2).broadcast_to([P, TJ, 4])
                dve.wait_ge(sn_out, 32 * H)
                V.link(dve, dve.memset(lg, 0.0))
                dve.wait_ge(s["lg_turned"].sem, layer + 1)
                V.link(dve, dve.tensor_copy(lg[:, 0:4, :], shaped(ps[:, 3, 0:80], 4, 20)))
                V.link(dve, dve.tensor_copy(lg[0:64, 4, :], ps[0:64, 3, 80:100]))
                V.link(dve, dve.tensor_reduce(s1, lg[:, :, 0:4], AX.X, ALU.max))
                V.link(dve, tt(r1, lg[:, :, 0:4], four(s1), ALU.subtract))
                V.link(dve, ts(r2, r1, 0.0, None, ALU.is_equal))
                first_of(mo["ohg"], r2, r3, s3)
                el = lg[:, :, 4:20].rearrange("p j (g e) -> p j g e", g=G)
                for g in range(G):
                    oh = mo["ohg"][:, :, g:g + 1].broadcast_to([P, TJ, E])
                    V.link(dve, tt(mo["sel"][:, :, g, :], lg[:, :, 4 + E * g:4 + E * (g + 1)], oh, ALU.mult))
                V.link(dve, tt(r2, mo["sel"][:, :, 0, :], mo["sel"][:, :, 1, :], ALU.add))
                V.link(dve, tt(r2, r2, mo["sel"][:, :, 2, :], ALU.add))
                V.link(dve, tt(r2, r2, mo["sel"][:, :, 3, :], ALU.add))
                V.link(dve, dve.tensor_reduce(s1, r2, AX.X, ALU.max))
                V.link(dve, tt(r3, r2, four(s1), ALU.is_equal))
                first_of(mo["oh1"], r3, r3, s3)
                V.link(dve, stt(r2, mo["oh1"], -BIG, r2, ALU.mult, ALU.add))
                V.link(dve, dve.tensor_reduce(s4, r2, AX.X, ALU.max))
                V.link(dve, tt(r3, r2, four(s4), ALU.is_equal))
                first_of(mo["oh2"], r3, r3, s3)
                s["top_in"].on(tt(s2, s4, s1, ALU.subtract))
                dve.wait_ge(s["top_out"].sem, layer + 1)
                V.link(dve, dve.tensor_reduce(pst, r1, AX.X, ALU.add))
                V.link(dve, ts(s3, s2, 1.0, None, ALU.add))
                V.link(dve, tt(s3, s3, pst, ALU.mult))
                V.link(dve, dve.reciprocal(s3, s3))
                V.link(dve, tt(s2, s2, s3, ALU.mult))
                V.link(dve, tt(r1, mo["oh1"], four(s3), ALU.mult))
                V.link(dve, tt(r2, mo["oh2"], four(s2), ALU.mult))
                V.link(dve, tt(r1, r1, r2, ALU.add))
                for g in range(G):
                    ins = tt(mo["comb"][:, :, g, :], r1, mo["ohg"][:, :, g:g + 1].broadcast_to([P, TJ, E]), ALU.mult)
                V.link(dve, ins)
                V.link(dve, dve.memset(mo["ohg"][64:P, 4, :], 0.0))
                s["comb_ready"].link(dve, tt(strict, causal, ident, ALU.subtract))
                V.link(dve, dve.memset(mo["P"][:, 0, :], 1.0))
                V.link(dve, dve.tensor_tensor_scan(iota1, mo["P"][:, 0, :], mo["P"][:, 0, :], 0.0, ALU.mult, ALU.add))
                dve.memset(mo["hs"][:, :, T:TW], 0.0)
                rk, tot, pre, off, pos = (mo[n] for n in "rk tot pre off pos".split())
                dve.wait_ge(s["ranked"].sem, layer + 1)
                V.link(dve, dve.tensor_copy(rk, shaped(ps[:, 2, 0:20], TJ, 4)))
                V.link(dve, dve.tensor_copy(tot, shaped(ps[:, 2, 32:52], TJ, 4)))
                V.link(dve, dve.memset(pre[:, 0, :], 0.0))
                for j in range(1, TJ):
                    V.link(dve, tt(pre[:, j, :], pre[:, j - 1, :], tot[:, j - 1, :], ALU.add))
                V.link(dve, tt(tot[:, 0, :], pre[:, TJ - 1, :], tot[:, TJ - 1, :], ALU.add))
                V.link(dve, dve.memset(off[:, 0:1], 0.0))
                for g in range(1, G):
                    V.link(dve, tt(off[:, g:g + 1], off[:, g - 1:g], tot[:, 0, g - 1:g], ALU.add))
                V.link(dve, dve.tensor_copy(off_i[:, 0:G], off[0:1, :]))
                n, extra, cum, prev = tot[:, 0, :], mo["w0"], mo["w1"], mo["w2"]
                V.link(dve, ts(extra, n, float(W), None, ALU.is_gt))
                for k in range(2, MORE + 1):
                    V.link(dve, stt(extra, n, float(k * W), extra, ALU.is_gt, ALU.add))
                V.link(dve, dve.tensor_copy(cum[:, 0:1], extra[:, 0:1]))
                for g in range(1, G):
                    V.link(dve, tt(cum[:, g:g + 1], cum[:, g - 1:g], extra[:, g:g + 1], ALU.add))
                V.link(dve, tt(prev, cum, extra, ALU.subtract))
                oh, part, more = mo["w3"], mo["w0"], mo["more"]
                for k in range(MORE):
                    V.link(dve, ts(oh, prev, float(k), None, ALU.is_le))
                    V.link(dve, stt(oh, cum, float(k), oh, ALU.is_gt, ALU.mult))
                    V.link(dve, dve.tensor_reduce(more[:, 0, k:k + 1], oh, AX.X, ALU.add))
                    V.link(dve, ts(part, col("rank"), -1.0, float(G), ALU.mult, ALU.add))
                    V.link(dve, tt(part, part, oh, ALU.mult))
                    V.link(dve, dve.tensor_reduce(more[:, 1, k:k + 1], part, AX.X, ALU.add))
                    V.link(dve, ts(part, prev, -float(W), float(W * (k + 1)), ALU.mult, ALU.add))
                    V.link(dve, tt(part, part, off, ALU.add))
                    V.link(dve, tt(part, part, oh, ALU.mult))
                    V.link(dve, dve.tensor_reduce(more[:, 2, k:k + 1], part, AX.X, ALU.add))
                    for ch in range(2):
                        V.link(dve, stt(mo["more_at"][:, ch, k:k + 1], col("part"), P * ch + 1.0, more[:, 2, k:k + 1],
                                        ALU.add, ALU.add))
                V.link(dve, dve.tensor_copy(more_i, more[0:1, :, :]))
                V.link(dve, tt(rk, rk, pre, ALU.add))
                V.link(dve, tt(rk, rk, off.unsqueeze(1).broadcast_to([P, TJ, 4]), ALU.add))
                V.link(dve, tt(rk, rk, mo["ohg"], ALU.mult))
                V.link(dve, dve.tensor_reduce(pos, rk, AX.X, ALU.add))
                V.link(dve, ts(pos, pos, 1.0, None, ALU.add))
                for j in range(TJ):
                    ins = ts(dg[:, j, :], ident, pos[:, j:j + 1], None, ALU.mult)
                s["place_ready"].link(dve, ins)
                for j in range(TJ):
                    ins = ts(mo["P"][:, j, :], iota1, pos[:, j:j + 1], None, ALU.is_equal)
                s["spread"].link(dve, ins)
                for q in range(2 * G):
                    V.link(dve, stt(mo["at"][:, q:q + 1], col("part"), P * (q % 2) + 1.0, off[:, q // 2:q // 2 + 1],
                                    ALU.add, ALU.add))
                dve.wait_ge(s["cS_ready"].sem, layer + 1)
                ub = (USES[f"moe{layer}"] + DC) // 2
                base = SLOTS[f"moe{layer}"]
                with looped(dve, 2, {s["ce_ready"]: 2 * E, s["hid_ready"]: 2 * KG, s["pt_ready"]: 2 * 2}) as i:
                    for gg in range(2):
                        g = 2 * i + gg
                        off_g = dve.value_load(off_i[0:1, bass.ds(g, 1)], min_val=0, max_val=T)

                        def weights(e):
                            dve.wait_ge(s["cb_full"].sem, E * g + (NE * layer + e + 1))
                            s["ce_ready"].on(ts(mo["ce"][0:NE, e % 2, :], mo["cS"][0:NE, bass.ds(off_g, W)],
                                                ident[0:NE, bass.ds(E * g + e, 1)], None, ALU.mult))

                        weights(0)
                        weights(1)
                        for e in range(E):
                            for f in range(FT):
                                t = 2 * e + f
                                dve.wait_ge(used, 2 * N_GROUP * i + (base + N_GROUP * gg + 2 * t + 2))
                                dve.wait_ge(pair_free[0].sem, 16 * i + (ub + 8 * gg + t + 1))
                                pair_free[1].on(tt(mo["tmp"], ps[:, 2, 0:W], mo["sil"], ALU.mult))
                                dve.wait_ge(s["cb_full"].sem, E * g + (NE * layer + e + 3))
                                dve.wait_ge(pair_free[1].sem, 16 * i + (ub + 8 * gg + t + 1))
                                s["hid_ready"].link(dve, tt(mo["hid"][:, gg, t, :], mo["tmp"],
                                                            ps[:, 2 * (e % 2) + 1, 0:W], ALU.mult))
                                if f == 0 and 1 <= e < E - 1:
                                    weights(e + 1)
                        for ch in range(2):
                            s["pt_ready"].on(ts(at(mo["PT"], 2 * g + ch), pos_row, mo["at"][:, bass.ds(2 * g + ch, 1)], None,
                                           ALU.is_equal))
                gated(s["scattered"].sem, DC * layer, 1, USES[f"moe{layer}"] + DC + 4 * NE, 1, mo["tmp"][:, 0:64])

            def further_windows(layer):
                X = x_dve[layer]
                for k in range(MORE):
                    with further_one(dve, k) as (group, start):
                        for e in range(E):
                            X.link(dve, ts(mo["ce"][0:NE, 0, :], mo["cS"][0:NE, bass.ds(start, W)],
                                           ident[0:NE, bass.ds(E * group + e, 1)], None, ALU.mult))
                            dve.wait_ge(x_act[layer].sem, X_ACT * k + (e + 1))
                            X.link(dve, tt(xhid[:, 2 * e, :], ps[:, 2, 0:W], mo["sil"], ALU.mult))
                            X.link(dve, tt(xhid[:, 2 * e + 1, :], ps[:, 4, 0:W], mo["hid"][:, 1, 0, :], ALU.mult))
                            for f in range(FT):
                                t = FT * e + f
                                X.link(dve, tt(xhid[:, t, :], xhid[:, t, :], ps[:, 1, 0:W], ALU.mult))
                        for ch in range(2):
                            X.link(dve, ts(mo["PT"][:, ch, :], pos_row, mo["more_at"][:, ch, k:k + 1], None, ALU.is_equal))
                        for m in range(DC):
                            p = m % 2
                            dve.wait_ge(x_pe[layer].sem, X_PE * k + (6 + m + 2))
                            g = modt[:, 40 + m, :]
                            tmp = mo["tmp"][:, 0:64]
                            X.link(dve, stt(xT[:, m, 0:TH], ps[:, 2 * p, 0:TH], g[:, 0:1], xT[:, m, 0:TH], ALU.mult, ALU.add))
                            X.link(dve, stt(xT[:, m, TH:TP], ps[:, 2 * p + 1, 0:TP - TH], g[:, 0:1], xT[:, m, TH:TP],
                                            ALU.mult, ALU.add))
                            X.link(dve, tt(by_seq(tmp), by_seq(ps[:, 2 * p + 1, TP - TH:TH]), over_t(g[:, 1:NV]), ALU.mult))
                            X.link(dve, tt(xT[:, m, TP:T], xT[:, m, TP:T], tmp, ALU.add))

            moe(0)
            further_windows(0)
            modulation(1)
            norm(2)

            wE = col("wE", 3, MT, 4)
            V.link(dve, dve.memset(first["gx"], 0.0))
            V.link(dve, dve.memset(first["gm"], 0.0))
            V.link(dve, dve.memset(first["xpad"][:, :, 0:3], 0.0))
            dve.wait_ge(conv_in, 32)
            cw = col("cw", 4, MT)

            def weight_of(w, i):
                return wE[:, w, i, :] if isinstance(i, int) else wE[:, w, bass.ds(i, 1), :].rearrange("p a o -> p (a o)")

            def block_diagonal(dst, w, i):
                return tt(dst.rearrange("p (m o) -> p m o", o=4), col("bd").unsqueeze(2).broadcast_to([P, 32, 4]),
                          weight_of(w, i).unsqueeze(1).broadcast_to([P, 32, 4]), ALU.mult)

            def gate_weights(dst, w, i):
                g = first["wg"][:, w, bass.ds(i, 1)].rearrange("p a n o -> p (a n) o")
                return tt(dst, g, weight_of(w, i).unsqueeze(1).broadcast_to([P, 8, 4]), ALU.mult)

            def inner(u, i, guarded):
                if guarded:
                    dve.wait_ge(s["gates_full"].sem, i - 1)
                two4 = lambda ap: ap.rearrange("p (a b) -> p a b", a=2)[:, :, 0:4]
                V.link(dve, gate_weights(first["pr"], 0, i))
                V.link(dve, gate_weights(first["pr2"], 1, i))
                V.link(dve, tt(first["pr"], first["pr"], first["pr2"], ALU.add))
                V.link(dve, dve.tensor_reduce(two4(first["gx"][:, u, :]), first["pr"].rearrange(
                    "p (a b) o -> p a b o", a=2), AX.X, ALU.add))
                V.link(dve, gate_weights(first["pr"], 2, i))
                V.link(dve, dve.tensor_reduce(two4(first["gm"][:, u, :]), first["pr"].rearrange(
                    "p (a b) o -> p a b o", a=2), AX.X, ALU.add))
                s["bdv_ready"].on(block_diagonal(first["bdv"][:, u, :], 2, i))
                xp = first["xpad"][:, u, :]
                pads = xp[:, 3 + TP:].rearrange("p (b t) -> p b t", b=NB)
                c0 = first["conv0"][:, bass.ds(i, 1), :].rearrange("p a (b t) -> p (a b) t", t=3)
                V.link(dve, dve.tensor_copy(pads[:, :, 0:3], c0))
                dve.wait_ge(s["xm_ready"].sem, 3 * i + 3)
                dve.wait_ge(s["xc_ready"].sem, i)
                acc = first["acc"]
                for tap in range(4):
                    w = cw[:, tap, i:i + 1] if isinstance(i, int) else cw[:, tap, bass.ds(i, 1)]
                    cb = col("cb")[:, bass.ds(i, 1)]
                    for dst, src in ((acc[:, 0:TP], xp[:, tap:tap + TP]), (by_seq(acc[:, TP:T]), pads[:, :, tap:tap + TS])):
                        if tap == 0:
                            ins = ts(dst, src, w, cb, ALU.mult, ALU.add)
                        else:
                            ins = stt(dst, src, w, dst, ALU.mult, ALU.add)
                    if tap < 3:
                        V.link(dve, ins)
                co = at(first["convout"], i)
                s["conv_acc"].on(ins)
                dve.tensor_copy(co[:, 0:3], xp[:, TP:TP + 3])
                dve.tensor_copy(co[:, 3:].rearrange("p (b t) -> p b t", b=NB), pads[:, :, TS:TS + 3])
                dve.wait_ge(s["v_full"].sem, i + 1)
                vt = ml["vtok"][:, :, bass.ds(P * i, P)]
                dve.tensor_copy(vt[:, 0:4, :], shaped(ps[:, 4, :], 4, P))
                s["v_read"].link(dve, dve.tensor_copy(vt[0:64, 4, :], ps[0:64, 5, 0:P]))

            inner(0, 0, False)
            inner(1, 1, False)
            with looped(dve, MT // 2 - 1, {V: 2 * 10, s["bdv_ready"]: 2, s["conv_acc"]: 2, s["v_read"]: 2}) as i:
                for u in range(2):
                    inner(u, 2 * i + (u + 2), True)
            s["conv_done"].link(dve, dve.memset(first["pr"][:, 0, 0:1], 0.0))

            dve.wait_ge(s["gates_full"].sem, MT)
            dve.wait_ge(out_done, 16)
            ig, gb, gu, t1, t2 = (gate[n][0:MH, :] for n in ("ig", "b", "u", "t1", "t2"))
            for dst, r0 in ((ig, 0), (t1, 32)):
                V.link(dve, dve.tensor_copy(dst[:, 0:TP], ps[r0:r0 + MH, 6, :]))
                V.link(dve, dve.tensor_copy(dst[:, TP:T], ps[r0:r0 + MH, 7, 0:64]))
            V.link(dve, ts(ig, ig, col("big")[0:MH, :], None, ALU.add))
            V.link(dve, ts(t1, t1, col("bfg")[0:MH, :], None, ALU.add))
            s["abs_ready"].link(dve, stt(t2, t1, -1.0, t1, ALU.mult, ALU.max))
            V.link(dve, ts(t1, t1, 0.0, None, ALU.min))
            dve.wait_ge(s["soft_ready"].sem, 1)
            V.link(dve, tt(t1, t1, t2, ALU.subtract))
            V.link(dve, dve.tensor_tensor_scan(gb, col("whole")[0:MH, :], t1, 0.0, ALU.mult, ALU.add))
            V.link(dve, tt(gu, ig, gb, ALU.subtract))
            V.link(dve, dve.tensor_copy(t2, gu))
            V.link(dve, ts(t2[:, 0:1], gu[:, 0:1], 0.0, None, ALU.max))
            m0 = col("m0")[0:MH, :]
            V.link(dve, tt(by_seq(t2[:, TP:T])[:, :, 0:1], by_seq(gu[:, TP:T])[:, :, 0:1], m0.unsqueeze(2), ALU.max))
            cut = gate["cut"][0:MH, :]
            V.link(dve, ts(cut, col("whole")[0:MH, :], -1.0, BIG, ALU.add, ALU.mult))
            V.link(dve, dve.tensor_tensor_scan(ig, cut, t2, 0.0, ALU.add, ALU.max))
            V.link(dve, tt(gb, gb, ig, ALU.add))
            rows = ml["rows"]
            V.link(dve, ts(rows[0:MH, :], ig, -1.0, None, ALU.mult))
            V.link(dve, dve.tensor_copy(rows[32:32 + MH, :], gb))
            V.link(dve, dve.tensor_copy(t2[:, 0:1], gb[:, TP - 1:TP]))
            V.link(dve, dve.tensor_copy(t2[:, 1:NV].unsqueeze(2), by_seq(gb[:, TP:T])[:, :, TS - 1:TS]))
            V.link(dve, ts(t1[:, 0:TP], gu[:, 0:TP], ig[:, TP - 1:TP], None, ALU.subtract))
            V.link(dve, tt(by_seq(t1[:, TP:T]), by_seq(gu[:, TP:T]), over_t(by_seq(ig[:, TP:T])[:, :, TS - 1]), ALU.subtract))
            s["dec_ready"].on(tt(by_seq(gb[:, TP:T]), over_t(m0), by_seq(ig[:, TP:T]), ALU.subtract))
            dve.wait_ge(s["dec_exp"].sem, 1)
            V.link(dve, dve.tensor_copy(rows[64:64 + MH, :], t1))
            s["rows_ready"].link(dve, dve.tensor_copy(rows[96:96 + MH, TP:T], gb[:, TP:T]))
            dve.wait_ge(s["turned_g"].sem, 1)
            for n, dst in enumerate((ml["utok"], ml["wtok"])):
                V.link(dve, dve.tensor_copy(dst[:, 0:4, :], shaped(ps[:, 4, 32 * n:32 * n + 16], 4, MH)))
                s["tok_ready"].link(dve, dve.tensor_copy(dst[0:64, 4, :], ps[0:64, 4, 32 * n + 16:32 * n + 20]))

            ub = USES["b"]
            n0 = col("n0", MT, NB)
            bdq = ml["W"].rearrange("p a b -> p (a b)")
            for h in range(MH):
                hb = ub + N_HEADB * h
                if h == 0:
                    dve.wait_ge(out_done, 32)
                for u in range(2):
                    dve.wait_ge(cp_out[u], 8 * HT * h)
                for w in range(2):
                    for i in range(HT):
                        ins = block_diagonal(bdq[:, (HT * w + i) * P:(HT * w + i + 1) * P], w, HT * h + i)
                s["bd_ready"].on(ins)
                dve.wait_ge(s["kt_full"].sem, h + 1)
                for j in range(4):
                    ts(ml["ktok"][:, j, :], ps[:, 4 + j, :], ml["wtok"][:, j, h:h + 1], KS, ALU.mult, ALU.mult)
                p = (hb + 12) % 2
                pair_free[p].on(ts(ml["ktok"][0:64, 4, :], ps[0:64, 2 * p, :], ml["wtok"][0:64, 4, h:h + 1], KS,
                                   ALU.mult, ALU.mult))
                dve.wait_ge(pair_free[p].sem, (hb + 12) // 2 + 1)
                for pp in range(2):
                    dve.wait_ge(pair_free[pp].sem, (hb + 12) // 2)
                for i in range(HT):
                    tmp = mx["rs"]
                    V.link(dve, tt(tmp, ml["kz"][:, i, :], mx["mu"], ALU.mult))
                    no = ml["nout"][:, HT * h + i, :]
                    V.link(dve, dve.tensor_reduce(no[:, 0:1], tmp[:, 0:TP], AX.X, ALU.add))
                    V.link(dve, dve.tensor_reduce(no[:, 1:NV], by_seq(tmp[:, TP:T]), AX.X, ALU.add))
                wl = by_seq(mx["wcb"])[:, :, TS - 1]
                nh = n0[:, HT * h:HT * (h + 1), :]
                V.link(dve, tt(shaped(mx["rs"][:, 0:HT * NB], HT, NB), nh, wl.unsqueeze(1).broadcast_to([P, HT, NB]), ALU.mult))
                no = ml["nout"][:, HT * h:HT * (h + 1), 1:NV]
                s["n_ready"].link(dve, tt(no, no, shaped(mx["rs"][:, 0:HT * NB], HT, NB), ALU.add))
                qs = ml["q"][:, :, TP:T]
                V.link(dve, tt(mx["qw"], qs, mx["wcb"].unsqueeze(1).broadcast_to([P, HT, 64]), ALU.mult))
                dve.wait_ge(s["s_full"].sem, h + 1)

                def weight(j):
                    n = TP - P * j if j < 4 else 64
                    m = P if j < 4 else 64
                    w = ml["W"][0:m, j % 2, 0:n]
                    src = mx["nM"][0:m, P * j:P * j + n]
                    s["w_ready"].link(dve, ts(w, src, ml["utok"][0:m, j, h:h + 1], 0.0, ALU.add, ALU.min))

                weight(0)
                for j in range(TJ):
                    if j + 1 < TJ:
                        weight(j + 1)
                    dve.wait_ge(s["w_exp"].sem, 5 * h + j + 1)
                    if j < 4:
                        n = TP - P * j
                        Pj = mx[f"P{j}"]
                        V.link(dve, tt(Pj, ps[:, 4 + j, 0:n], ml["W"][:, j % 2, 0:n], ALU.mult))
                        s["p_ready"].link(dve, tt(Pj[:, 0:P], Pj[:, 0:P], causal, ALU.mult))
                    else:
                        p = (hb + 13) % 2
                        pair_free[p].on(tt(mx["Ps"][0:64, :], ps[0:64, 2 * p, 0:64], ml["W"][0:64, 0, 0:64], ALU.mult))
                        dve.wait_ge(pair_free[p].sem, (hb + 13) // 2 + 1)
                        s["p_ready"].link(dve, tt(mx["Ps"][0:64, :], mx["Ps"][0:64, :], causal_s[0:64, :], ALU.mult))
                s["qw_ready"].on(tt(qn.rearrange("p i (b t) -> p i b t", b=NB),
                                    mx["qw"].rearrange("p i (b t) -> p i b t", b=NB), over_t(nh), ALU.mult))
                V.link(dve, dve.memset(alone, 0.0))

                def one_sequence(b):
                    if b >= 2:
                        dve.memset(alone[:, b % 2, :, TS * (b - 2):TS * (b - 1)], 0.0)
                    of_b = slice(TS * b, TS * (b + 1))
                    s["alone_ready"].on(dve.tensor_copy(alone[:, b % 2, :, of_b], mx["qw"][:, :, of_b]))

                one_sequence(0)
                one_sequence(1)
                for b in range(NB):
                    n = NB * h + b
                    C = shaped(ml["C"][:, n % 2, :], HT, MD)
                    dve.wait_ge(s["num_s"].sem, 9 * h + b + 2)
                    if b + 2 < NB:
                        one_sequence(b + 2)
                    for k in range(HT):
                        dve.wait_ge(s["upd_c"].sem, HT * n + k + 1)
                        s["c_done"].on(stt(C[:, k, :], C[:, k, :], mx["wcb"][:, TS * b + TS - 1:TS * (b + 1)],
                                           ps[:, 4 + k, :], ALU.mult, ALU.add))
                rd = mx["rs"]

                def guard_den(dst, den, emn):
                    V.link(dve, ts(dst, den, -1.0, None, ALU.mult))
                    V.link(dve, tt(dst, dst, den, ALU.max))
                    V.link(dve, tt(dst, dst, emn, ALU.max))
                    V.link(dve, dve.reciprocal(dst, dst))

                n = hb + 15
                p = n % 2
                dve.wait_ge(s["num_full"].sem, h + 1)
                guard_den(rd[:, TP:T], ps[:, 2 * p + 1, 0:64], mx["emn"][:, TP:T])
                dve.wait_ge(s["turned_s"].sem, h + 1)
                ins = tt(ml["q"][:, :, TP:T], shaped(ps[:, 2 * p, 0:256], HT, 64),
                         rd[:, TP:T].unsqueeze(1).broadcast_to([P, HT, 64]), ALU.mult)
                pair_free[p].on(ins)
                fb = 17 * h + 12
                n += 1
                p = n % 2
                dve.wait_ge(s["b_full"].sem, fb + 1)
                V.link(dve, ts(rd[:, 0:TP], ps[:, 2 * p, :], -1.0, None, ALU.mult))
                pair_free[p].on(tt(rd[:, 0:TP], rd[:, 0:TP], ps[:, 2 * p, :], ALU.max))
                dve.wait_ge(pair_free[p].sem, n // 2 + 1)
                V.link(dve, tt(rd[:, 0:TP], rd[:, 0:TP], mx["emn"][:, 0:TP], ALU.max))
                V.link(dve, dve.reciprocal(rd[:, 0:TP], rd[:, 0:TP]))
                for i in range(HT):
                    n += 1
                    p = n % 2
                    dve.wait_ge(s["b_full"].sem, fb + 2 + i)
                    pair_free[p].on(tt(ml["q"][:, i, 0:TP], ps[:, 2 * p, :], rd[:, 0:TP], ALU.mult))
                n += 2
                p = n % 2
                dve.wait_ge(s["mu_full"].sem, h + 1)
                pair_free[p].on(ts(two(mx["mu"]), halves(p), 1.0 / MD, None, ALU.mult))
                dve.wait_ge(pair_free[p].sem, n // 2 + 1)
                q, z = ml["q"], ml["kz"]
                s["rs_h"].link(dve, tt(q, q, mx["mu"].unsqueeze(1).broadcast_to([P, HT, T]), ALU.subtract))
                dve.wait_ge(s["sqh_ready"].sem, h + 1)
                for i in range(HT):
                    V.link(dve, ts(q[:, i, :], q[:, i, :], col("mln")[:, HT * h + i:HT * h + i + 1], None, ALU.mult))
                dve.wait_ge(s["rsh_ready"].sem, h + 1)
                V.link(dve, tt(q, q, mx["rs"].unsqueeze(1).broadcast_to([P, HT, T]), ALU.mult))
                for i in range(HT):
                    xc = ml["xc"][:, HT * h + i, :]
                    V.link(dve, stt(q[:, i, :], xc, col("skip")[:, HT * h + i:HT * h + i + 1], q[:, i, :], ALU.mult, ALU.add))
                for p in range(2):
                    dve.wait_ge(pair_free[p].sem, (hb + N_HEADB) // 2)
                s["ho_ready"].link(dve, tt(ml["xc"][:, HT * h:HT * (h + 1), :], q, z, ALU.mult))

            dve.wait_ge(x_back, 16)
            gated(used, SLOTS["md"], 2, USES["md"], 0, ml["W"][:, 0, 0:64])
            moe(1)
            further_windows(1)
            norm(4)


def kernel(**inputs):
    import concourse.bacc as _bacc
    from concourse.bass_utils import run_bass_kernel_spmd as _run

    a = {k: np.asarray(v) for k, v in inputs.items()}
    f32 = np.float32

    def features(x):
        return np.moveaxis(x.reshape(x.shape[:-1] + (-1, P)), -1, 0)

    cols = np.zeros((P, NCOL), f32)

    def put(name, x):
        at, n = COLS[name]
        x = np.asarray(x, f32)
        x = x.reshape(x.shape[0], -1)
        assert x.shape[1] == n, (name, x.shape, n)
        cols[:x.shape[0], at:at + n] = x

    c = np.concatenate([a["c_prompt"], a["c_sample"]], 0)
    put("c", np.moveaxis(features(c), 1, 2))
    put("bada", features(a["b_ada"]))
    put("ng", features(a["norm_g"]))
    put("fg", features(a["final_g"]))
    put("hgn", a["hg_norm"][0][:, None])
    put("lb", features(a["hg_lb"]))
    put("cw", features(a["ml_conv_w"][0]))
    put("cb", features(a["ml_conv_b"][0]))
    put("wE", np.stack([a[n][0].transpose(0, 2, 1).reshape(MT, P, 4) for n in ("ml_wq", "ml_wk", "ml_wv")], 0).transpose(2, 0, 1, 3))
    put("mln", features(a["ml_norm"][0]))
    put("skip", features(a["ml_skip"][0]))
    wr = np.concatenate([a["moe_wrg"], a["moe_wre"].reshape(LAYERS, D, NE)], 2)
    put("wr", wr.reshape(LAYERS, DC, P, 20).transpose(2, 0, 1, 3))
    put("rb", np.concatenate([a["moe_brg"], a["moe_bre"].reshape(LAYERS, NE)], 1).T)
    put("n0", a["state_mlstm_n"][0].reshape(NB, MT, P).transpose(2, 1, 0))
    put("big", a["ml_big"].T)
    put("bfg", a["ml_bfg"].T)
    put("m0", a["state_mlstm_m"][0].T)
    t = np.arange(T)
    put("ident", np.eye(P))
    put("ones", np.ones((P, P)))
    put("causal", np.triu(np.ones((P, P))))
    r = np.arange(NB * TS)
    put("causal_s", (r[:, None] // TS == r[None] // TS) & (r[:, None] <= r[None]))
    put("own", r[:, None] // TS == np.arange(NB)[None])
    starts = np.where(t < TP, t % P == 0, (t - TP) % TS == 0)
    put("keep", np.tile(np.where(starts, 0.0, 1.0), (P, 1)))
    whole = np.where(t < TP, t == 0, (t - TP) % TS == 0)
    put("whole", np.tile(np.where(whole, 0.0, 1.0), (MH, 1)))
    put("rank", np.tile(np.arange(4, 0, -1), (P, 1)))
    put("bd", np.arange(P)[:, None] // 4 == np.arange(32)[None])
    put("eps", np.full((P, 1), EPS))
    put("part", np.arange(P)[:, None])

    def tiles(w):
        k, m = w.shape
        w = w.reshape(k // 1024, 8, P, m // P, P).transpose(3, 0, 2, 1, 4)
        return w.reshape(-1, P, SLOT)

    def ada_tiles(w):
        w = w.reshape(4, 2, P, 12, 512).transpose(3, 0, 2, 1, 4)
        return w.reshape(-1, P, SLOT)

    win = a["hg_win"][0].reshape(D, 4, H, P)[:, [1, 0, 3, 2]]
    parts = {
        "ada0": ada_tiles(a["w_ada"][0]), "ada1": ada_tiles(a["w_ada"][1]),
        "hg": tiles(win.transpose(0, 2, 1, 3).reshape(D, -1)),
        "wo": tiles(a["hg_wo"][0]),
        "xm": tiles(a["ml_wup"][0][:, :MI]), "z": tiles(a["ml_wup"][0][:, MI:]),
        "md": tiles(a["ml_wdown"][0])}
    for l in range(LAYERS):
        w13 = np.stack([a["moe_w1"][l].reshape(NE, D, FT, P), a["moe_w3"][l].reshape(NE, D, FT, P)], 3)
        w13 = tiles(w13.transpose(1, 0, 2, 3, 4).reshape(D, -1)).reshape(G, 2 * KG, P, SLOT)
        w2 = a["moe_w2"][l].reshape(G, KG, P, D)
        parts[f"moe{l}"] = np.concatenate([w13, w2], 1).reshape(-1, P, SLOT)
    wstream = np.empty((NSLOT, P, SLOT), f32)
    for name, w in parts.items():
        wstream[SLOTS[name]:SLOTS[name] + len(w)] = w

    x = np.concatenate([a["x_prompt"].reshape(TP, D), a["x_sample"].reshape(NB * TS, D)], 0)
    wg = np.concatenate([a["ml_wig"][0], a["ml_wfg"][0]], 1).reshape(3, MT, 32, 4, 8)
    wg = np.broadcast_to(wg.transpose(0, 1, 2, 4, 3)[:, :, :, None], (3, MT, 32, 4, 8, 4))
    c0 = a["state_mlstm_c"][0].transpose(1, 0, 2, 3).reshape(MH * NB, HT, P, MD)
    arrays = {
        "cols": cols, "wstream": wstream,
        "xT": x.reshape(T, DC, P).transpose(2, 1, 0),
        "hg0": a["state_hgrn"][0].transpose(1, 2, 0, 3).reshape(H, P, NB * P),
        "wg": wg.reshape(3, MT, P, 32).transpose(2, 0, 1, 3).reshape(P, -1),
        "conv0": a["state_conv"][0].reshape(NB, 3, MT, P).transpose(3, 2, 0, 1).reshape(P, -1),
        "c0": c0.transpose(0, 2, 1, 3).reshape(MH * NB, P, HT * MD)}
    arrays = {k: np.ascontiguousarray(v, f32) for k, v in arrays.items()}
    outs = {"y": (P, DC, T), "hg_p": (H, P, P), "hg_s": (H, P, NB * P), "mc_p": (MH, HT, P, MD),
            "mc_s": (MH * NB, P, HT * MD), "mn": (P, MT * NV), "mm": (MH, NV), "conv": (P, MT * 3 * NV)}

    nc = _bacc.Bacc("TRN2", target_bir_lowering=False, num_devices=1)
    io = {k: nc.dram_tensor(f"in_{k}", list(v.shape), F32, kind="ExternalInput").ap() for k, v in arrays.items()}
    io["out"] = {k: nc.dram_tensor(f"out_{k}", list(v), F32, kind="ExternalOutput").ap() for k, v in outs.items()}
    io["x_dram"] = nc.dram_tensor("x_dram", [P, DC, T], F32, kind="Internal").ap()
    build(nc, io)
    res = _run(nc, [{f"in_{k}": v for k, v in arrays.items()}], core_ids=[0]).results[0]
    o = {k: np.asarray(res[f"out_{k}"]) for k in outs}

    y = o["y"].transpose(2, 1, 0).reshape(T, D)
    mn = o["mn"].reshape(P, MT, NV).transpose(2, 1, 0).reshape(NV, MH, MD)
    conv = o["conv"].reshape(P, MT, NV, 3).transpose(2, 3, 1, 0).reshape(NV, 3, MI)
    mm = o["mm"].T
    hg_s = o["hg_s"].reshape(H, P, NB, P).transpose(2, 0, 1, 3)
    mc_s = o["mc_s"].reshape(MH, NB, P, HT, MD).transpose(1, 0, 3, 2, 4).reshape(NB, MH, MD, MD)
    return (y[:TP].reshape(1, TP, D), y[TP:].reshape(NB, TS, D), o["hg_p"][None, None],
            o["mc_p"].reshape(1, 1, MH, MD, MD), mn[None, :1], mm[None, :1], conv[None, :1],
            hg_s[None], mc_s[None], mn[None, 1:], mm[None, 1:], conv[None, 1:])
```

```python
from contextlib import ExitStack, contextmanager

import numpy as np

import concourse.bass as bass
from concourse import mybir

F32 = mybir.dt.float32
F32R = mybir.dt.float32r
ALU = mybir.AluOpType
ACT = mybir.ActivationFunctionType
AX = mybir.AxisListType

P = 128
D = 1024
DC = D // P
TP = 512
NB, TS = 8, 8
T = TP + NB * TS
TH = T // 2
TJ = 5
NV = NB + 1
H = 8
BLK = 32
MI = 2048
MT = MI // P
MH = 4
MD = MI // MH
HT = MD // P
G, E, NE, FF = 4, 4, 16, 256
FT = FF // P
KG = E * FT
W = 224
CH = (128, W - 128)
TW = T + W
MORE = T // W
X_PE, X_ACT, X_DVE = 6 + DC, E + 2, 5 * E + 2 + 4 * DC
EPS = 1e-6
BIG = 1e30
CLAMP = 60.0
LAYERS = 2

R = 8
SLOT = 1024
N_ADA = 6 * D // 512 * 4
N_HG, N_WO = 4 * H, DC
N_GROUP = E * FT * 2 + E * FT
N_XM, N_Z, N_MD = MT, MT, DC * MT // 8
SLOTS = {}
_at = 0
for _name, _n in (("ada0", N_ADA), ("hg", N_HG), ("ada1", N_ADA), ("wo", N_WO), ("moe0", G * N_GROUP),
                  ("xm", N_XM), ("z", N_Z), ("md", N_MD), ("moe1", G * N_GROUP)):
    SLOTS[_name] = _at
    _at += _n
NSLOT = _at
USES = {}
_at = 2
N_HEADB = 26
for _name, _n in (("ada0", 12), ("hg", 4 * H), ("ada1", 12), ("wo", DC), ("moe0", 2 * DC + 4 * NE),
                  ("xm", MT), ("b", N_HEADB * MH), ("md", DC), ("moe1", 2 * DC + 4 * NE)):
    USES[_name] = _at
    _at += _n


def offsets(spec):
    at, out = 0, {}
    for name, n in spec:
        out[name] = (at, n)
        at += n
    return out, at


COLS, NCOL = offsets([
    ("c", DC * NV), ("bada", LAYERS * 48), ("ng", LAYERS * 2 * DC), ("fg", DC), ("hgn", 1), ("lb", 3 * H),
    ("cw", 4 * MT), ("cb", MT), ("wE", 3 * MT * 4), ("mln", MT), ("skip", MT), ("wr", LAYERS * DC * 20),
    ("rb", LAYERS), ("n0", MT * NB), ("big", 1), ("bfg", 1), ("m0", NB),
    ("ident", P), ("ones", P), ("causal", P), ("causal_s", 64), ("own", NB), ("whole", T),
    ("rank", 4), ("bd", 32), ("eps", 1), ("part", 1)])


class Signal:

    def __init__(self, sem):
        self.sem, self.base, self.n = sem, 0, 0

    def on(self, ins):
        ins.then_inc(self.sem, 1)
        self.n += 1

    def link(self, eng, ins):
        self.on(ins)
        eng.wait_ge(self.sem, self.base + self.n)


@contextmanager
def looped(eng, n, per):
    kept = {s: s.base + s.n for s in per}
    with eng.Fori(0, n) as i:
        for s, k in per.items():
            s.base, s.n = kept[s] + i * k, 0
        yield i
    for s, k in per.items():
        assert s.n == k, f"a signal is raised {s.n} times in a pass, not {k}"
        s.base, s.n = kept[s] + n * k, 0


def build(nc, io):
    with ExitStack() as ctx:
        def sb(name, *dims):
            return ctx.enter_context(nc.sbuf_tensor(name, [P, int(np.prod(dims))], F32))

        def sem(name):
            return ctx.enter_context(nc.semaphore(name))

        def shaped(ap, *dims):
            if len(dims) == 1:
                return ap
            names = "abcd"[:len(dims)]
            return ap.rearrange(f"p ({' '.join(names)}) -> p {' '.join(names)}", **dict(zip(names, dims)))

        ring = shaped(sb("ring", R * SLOT)[:, :], R, SLOT)
        xT = shaped(sb("xT", DC * T)[:, :], DC, T)
        hT = shaped(sb("hT", DC * T)[:, :], DC, T)
        cols = sb("cols", NCOL)
        modt = shaped(sb("modt", LAYERS * 48 * NV)[:, :], LAYERS, 48, NV)
        amod = shaped(sb("amod", LAYERS * 2 * DC * NV)[:, :], LAYERS, 2, DC, NV)
        ARENA = 32504
        R_AT, R_SIZE = DC * TW, 2 * G * (2 * D + T)
        with nc.sbuf_tensor("before_r", [P, R_AT], F32), nc.sbuf_tensor("arena_r", [P, R_SIZE], F32R) as arena_r:
            pass
        arena = sb("arena", ARENA)
        ps = ctx.enter_context(nc.psum_tensor("ps", [P, 8, 512], F32))

        def col(name, *dims):
            at, n = COLS[name]
            return shaped(cols[:, at:at + n], *dims) if dims else cols[:, at:at + n]

        def carve(spec, start=0):
            at, out = start, {}
            for name, *dims in spec:
                n = int(np.prod(dims))
                out[name] = shaped(arena[:, at:at + n], *dims)
                at += n
            assert at <= ARENA, at
            return out, at

        ident, ones = col("ident"), col("ones")
        causal, causal_s, own = col("causal"), col("causal_s"), col("own")
        eps = col("eps")

        silc = col("c", DC, NV)
        rstd = arena[:, 24000:24000 + T]
        hg, hg_end = carve([
            ("og", H, T), ("S0", 2, NB * P), ("Vx", NB, P), ("th", 2, T), ("q", 2, T), ("zg", 2, T),
            ("v", 2, TJ * P), ("k", T), ("g", T), ("b", T), ("eq", T), ("K", 16, P), ("Ks", 64),
            ("qe", T), ("kw", T), ("at", TJ, P), ("ktw", TJ, P), ("S", 4, P), ("sq", T),
            ("rs", T), ("Sn", NB, P), ("half", H), ("low", H), ("t1", 3, H), ("t2", H),
            ("keep", T)])
        modrow = [carve([("rows", 6 * D)], start)[0]["rows"] for start in (0, hg_end)]
        mo, _ = carve([
            ("hs", DC, TW), ("P", TJ, TW), ("more_y", 2 * G * D - TJ * TW), ("y", 2 * G, D), ("PT", 2 * G, T), ("hid", KG, W),
            ("sil", W), ("tmp", W), ("ce", 2, W), ("cS", TW), ("lgT", T), ("gt", 64),
            ("lg", TJ, 20), ("r1", TJ, 4), ("r2", TJ, 4), ("r3", TJ, 4), ("oh1", TJ, 4), ("oh2", TJ, 4),
            ("s1", TJ), ("s2", TJ), ("s3", TJ), ("s4", TJ), ("ps", TJ), ("ohg", TJ, 4), ("sel", TJ, 4, 4),
            ("comb", TJ, 4, 4), ("rk", TJ, 4), ("tot", TJ, 4), ("pre", TJ, 4), ("off", 4), ("pos", TJ),
            ("at", 2 * G), ("w0", 4), ("w1", 4), ("w2", 4), ("w3", 4), ("more", 3, MORE), ("more_at", 2, MORE)])
        y_at = 2 * G * D
        y_lo, y_hi = (shaped(arena_r[:, at:at + 2 * G * D], 2 * G, D) for at in (y_at - 2 * G * D, y_at))
        PT_r = shaped(arena_r[:, y_at + 2 * G * D:y_at + 2 * G * (D + T)], 2 * G, T)
        h_hi, h_lo = (shaped(arena_r[:, at:at + TJ * D], TJ, D) for at in (y_at, y_at + TJ * D))
        h_tok = shaped(mo["more_y"][:, 0:2 * D], 2, D)
        P_r = shaped(arena_r[:, 0:TJ * TW], TJ, TW)
        pt_flat = mo["PT"].rearrange("p a b -> p (a b)")[:, 2 * TJ * D - 2 * G * D:]
        iota1, dg, strict = pt_flat[:, 0:TW], shaped(pt_flat[:, TW:TW + TJ * P], TJ, P), \
            pt_flat[:, TW + TJ * P:TW + TJ * P + P]
        pos_row = mo["lgT"]
        place = ctx.enter_context(nc.sbuf_tensor("place", [1, G + 1 + 3 * MORE], mybir.dt.int32))
        off_i, more_i = place[:, 0:G + 1], shaped(place[:, G + 1:], 3, MORE)
        ml, _ = carve([
            ("vtok", TJ, MI), ("xc", MT, T), ("q", HT, T), ("kz", HT, T), ("ktok", TJ, MD),
            ("C", 2, HT * MD), ("W", 2, 512), ("rows", T), ("nout", MT, NV), ("utok", TJ, MH),
            ("wtok", TJ, MH)])
        c_at = TJ * MI + MT * T + 2 * HT * T + TJ * MD
        first, first_end = carve([
            ("xpad", 2, 3 + TP + NB * 11), ("xs", 2, 64), ("acc", T), ("bdv", 2, P), ("gx", 2, 64),
            ("gm", 2, 64), ("wg", 3, MT, 8, 4), ("conv0", MT, 3 * NB), ("pr", 8, 4), ("pr2", 8, 4),
            ("convout", MT, 3 * NV)], c_at)
        assert first_end <= c_at + 2 * HT * MD + 1024
        gate, gate_end = carve([("ig", T), ("b", T), ("u", T), ("t1", T), ("t2", T), ("cut", T)], c_at)
        assert gate_end <= first_end - MT * 3 * NV
        x_flat = xT.rearrange("p a b -> p (a b)")
        mx, at = {}, 0
        for name, *dims in (("P0", 512), ("P1", 384), ("P2", 256), ("P3", 128), ("Ps", 64), ("kb", 512),
                            ("mu", T), ("rs", T), ("emn", T), ("nM", T), ("qw", HT, 64), ("wcb", 64)):
            n = int(np.prod(dims))
            mx[name] = shaped(x_flat[:, at:at + n], *dims)
            at += n
        assert at <= DC * T
        slot_full = [sem(f"slot_full{r}") for r in range(R)]
        pair_free = [Signal(sem(f"pair_free{p}")) for p in range(2)]
        small_in, x_in, conv_in, x_kept, x_back, out_done, sn_out, keep_in = (
            sem(n) for n in ("small_in", "x_in", "conv_in", "x_kept", "x_back", "out_done", "sn_out", "keep_in"))
        s0_in, cp_out = ([sem(f"{n}{u}") for u in range(2)] for n in ("s0_in", "cp_out"))
        c_in, c_out = ([[sem(f"{n}{u}{half}") for half in range(2)] for u in range(2)] for n in ("c_in", "c_out"))
        names = (
            "dve act num_full lb_in lb_out conv_acc rsh_ready slot_used silc turned sq_ready ss_ready "
            "rstd_ready h_ready x_tile y_ready decay f_ready diffs exps elem_ready scored scored_s "
            "at_ready upd upd_s vx_ready s_ready o_full o_read sq_head head_ss head_rs head_done sn_ready "
            "sn_kept lgT_full lg_ready lg_turned top_in top_out comb_ready ranked place_ready spread "
            "htok_full htok_ready cS_full cS_ready pos_full pos_ready gathered ce_ready cb_full y_full "
            "yg_ready scattered scaled pt_ready y_hi_ready hlo_ready ohg_ready hid_ready xm_ready "
            "bdv_ready xc_ready v_full v_read gates_full abs_ready soft_ready dec_ready dec_exp "
            "rows_ready turned_g tok_ready bd_ready b_full kt_full kt_read s_full w_ready w_exp p_ready "
            "qw_ready kb_ready num_s upd_c c_done cp_full cp_ready n_ready mu_full sqh_ready var_full "
            "ho_ready rs_h alone_ready raw_ready turned_s").split()
        s = {n: Signal(sem(n)) for n in names}
        x_w = [sem(f"x_w{l}") for l in range(LAYERS)]
        x_pe, x_act, x_dve = ([Signal(sem(f"{n}{l}")) for l in range(LAYERS)] for n in ("x_pe", "x_act", "x_dve"))
        wstream, out = io["wstream"], io["out"]

        qn = shaped(ml["W"][:, 0, 64:64 + HT * 64], HT, 64)
        alone = shaped(ml["W"][:, 1, :], 2, HT, 64)

        xw, xy, xhid, xsil = mo["y"][:, 4:8, :], mo["y"], mo["hid"], mo["ce"][:, 1, :]

        @contextmanager
        def further(eng, steps):
            with looped(eng, MORE, steps) as k:
                there, group, start = (eng.value_load(more_i[0:1, n, bass.ds(k, 1)], min_val=0, max_val=hi)
                                       for n, hi in enumerate((1, G - 1, T)))
                with eng.If(there > 0):
                    yield k, group, start

        @contextmanager
        def further_one(eng, k):
            there, group, start = (eng.value_load(more_i[0:1, n, k:k + 1], min_val=0, max_val=hi)
                                   for n, hi in enumerate((1, G - 1, T)))
            with eng.If(there > 0):
                yield group, start

        block = ctx.enter_context(nc.Block())

        @block.sync
        def _(sp):
            sp.dma_start(cols[:, :], io["cols"]).then_inc(small_in, 16)
            for r in range(R):
                sp.dma_start(ring[:, r, :], wstream[r]).then_inc(slot_full[r], 16)
            sp.dma_start(xT, io["xT"]).then_inc(x_in, 16)
            with sp.Fori(1, NSLOT // R) as i:
                for r in range(R):
                    sp.wait_ge(s["slot_used"].sem, R * i + (r + 1 - R))
                    sp.dma_start(ring[:, r, :], wstream[bass.ds(R * i + r, 1)].rearrange("a p n -> p (a n)")
                                 ).then_inc(slot_full[r], 16)

        @block.gpsimd
        def _(pool):
            pool.sem_inc(s["sn_kept"].sem, 1)
            pool.dma_start(hg["keep"], io["keep"]).then_inc(keep_in, 16)
            pool.wait_ge(s["turned"].sem, 1)
            for h in range(2):
                pool.dma_start(hg["S0"][:, h, :], io["hg0"][h]).then_inc(s0_in[h], 16)
            def states_out(h):
                pool.wait_ge(s["sn_ready"].sem, h + 1)
                pool.dma_start(out["hg_s"][bass.ds(h, 1)].rearrange("a p n -> p (a n)"),
                               hg["Sn"].rearrange("p a b -> p (a b)")).then_inc(sn_out, 16)
                pool.dma_start(out["hg_p"][bass.ds(h, 1)].rearrange("a p n -> p (a n)"),
                               hg["S"][:, 3, :]).then_inc(sn_out, 16)

            with pool.Fori(0, H // 2 - 1) as i:
                for u in range(2):
                    states_out(2 * i + u)
                    pool.wait_ge(s["head_done"].sem, 2 * i + u + 1)
                    pool.dma_start(hg["S0"][:, u, :], io["hg0"][bass.ds(2 * i + u + 2, 1)].rearrange(
                        "a p n -> p (a n)")).then_inc(s0_in[u], 16)
                    pool.wait_ge(sn_out, 64 * i + 32 * (u + 1))
                    pool.sem_inc(s["sn_kept"].sem, 1)
            for h in range(H - 2, H):
                states_out(h)
                pool.wait_ge(sn_out, 32 * (h + 1))
                pool.sem_inc(s["sn_kept"].sem, 1)
            def h_remainder(layer):
                for j in range(TJ):
                    m = P if j < 4 else 64
                    pool.wait_ge(s["htok_ready"].sem, TJ * layer + j + 1)
                    s["hlo_ready"].on(pool.tensor_tensor(h_lo[0:m, j, :], h_tok[0:m, j % 2, :], h_hi[0:m, j, :],
                                                         ALU.subtract))

            def further_weights(layer):
                dma = pool.dma_start
                with further(pool, {}) as (k, group, start):
                    for b in range(6):
                        pool.wait_ge(x_pe[layer].sem, X_PE * k + (b + 1))
                        src = wstream[bass.ds(N_GROUP * group + (SLOTS[f"moe{layer}"] + 4 * b), 4)]
                        dma(xw, src.rearrange("a p n -> p a n")).then_inc(x_w[layer], 16)
                    pool.wait_ge(x_dve[layer].sem, X_DVE * (k + 1))

            h_remainder(0)
            pool.wait_ge(s["x_tile"].sem, 2 * DC)
            further_weights(0)
            pool.dma_start(first["wg"].rearrange("p a b c d -> p (a b c d)"), io["wg"]).then_inc(conv_in, 16)
            pool.dma_start(first["conv0"].rearrange("p a b -> p (a b)"), io["conv0"]).then_inc(conv_in, 16)
            pool.wait_ge(s["h_ready"].sem, 3 * DC)
            pool.dma_start(io["x_dram"], xT).then_inc(x_kept, 16)
            pool.wait_ge(s["v_read"].sem, MT)
            pool.dma_start(out["conv"], first["convout"].rearrange("p a b -> p (a b)")).then_inc(out_done, 16)
            pool.wait_ge(s["rows_ready"].sem, 1)
            pool.dma_start(out["mm"], gate["t2"][0:MH, 0:NV]).then_inc(out_done, 16)
            pool.wait_ge(out_done, 32)
            pool.wait_ge(s["turned_g"].sem, 1)
            def half_of(state, half):
                return state[:, HT * MD // 2 * half:HT * MD // 2 * (half + 1)]

            for n in range(2):
                for half in range(2):
                    pool.dma_start(half_of(ml["C"][:, n, :], half), half_of(io["c0"][n], half)).then_inc(c_in[n][half], 16)
            for h in range(MH):
                for b in range(NB):
                    n = NB * h + b
                    for half in range(2):
                        pool.wait_ge(s["c_done"].sem, HT * n + HT // 2 * (half + 1))
                        pool.dma_start(half_of(out["mc_s"][n], half), half_of(ml["C"][:, n % 2, :], half)
                                       ).then_inc(c_out[n % 2][half], 16)
                    if n + 2 < NB * MH:
                        for half in range(2):
                            pool.wait_ge(c_out[n % 2][half], 16 * (n // 2 + 1))
                            pool.dma_start(half_of(ml["C"][:, n % 2, :], half), half_of(io["c0"][n + 2], half)
                                           ).then_inc(c_in[n % 2][half], 16)
                for kt in range(HT):
                    pool.wait_ge(s["cp_ready"].sem, HT * h + kt + 1)
                    pool.dma_start(out["mc_p"][h, kt], ml["W"][:, kt % 2, :]).then_inc(cp_out[kt % 2], 16)
            pool.wait_ge(s["n_ready"].sem, MH)
            pool.dma_start(out["mn"], ml["nout"].rearrange("p a b -> p (a b)")).then_inc(out_done, 16)
            pool.wait_ge(s["ho_ready"].sem, MH)
            pool.dma_start(xT, io["x_dram"]).then_inc(x_back, 16)
            h_remainder(1)
            pool.wait_ge(s["x_tile"].sem, 4 * DC)
            further_weights(1)
            for half in range(2):
                pool.wait_ge(s["y_ready"].sem, DC // 2 * (half + 1))
                of_half = slice(DC // 2 * half, DC // 2 * (half + 1))
                pool.dma_start(out["y"][:, of_half, :], hT[:, of_half, :]).then_inc(out_done, 16)
            pool.wait_ge(out_done, 80)
            pool.wait_ge(sn_out, 32 * H)
            for u in range(2):
                for half in range(2):
                    pool.wait_ge(c_out[u][half], 16 * NB * MH // 2)
                pool.wait_ge(cp_out[u], 16 * MH * HT // 2)

        @block.tensor
        def _(pe):
            used = s["slot_used"]

            def feature_tile(phase, turn, rs, p, freed, rhs, nk, norm=None):
                pe.wait_ge(pair_free[p].sem, freed)
                for si, r in enumerate(rs):
                    pe.wait_ge(slot_full[r], 16 * (turn + 1))
                    for c in range(8):
                        k = 8 * si + c
                        if norm is not None:
                            h_tile(norm, k)
                        for half in range(2):
                            mm = pe.matmul(ps[:, 2 * p + half, 0:TH], ring[:, r, c * P:(c + 1) * P],
                                           rhs(k)[:, TH * half:TH * (half + 1)], start=(k == 0), stop=(k == nk - 1))
                    used.on(mm)

            def h_rhs(k):
                return hT[:, k, :]

            def wide(banks, lhs, rhs):
                n = len(lhs)
                for k in range(n):
                    for half in range(2):
                        mm = pe.matmul(ps[:, banks[half], 0:TH], lhs[k], rhs[k][:, TH * half:TH * (half + 1)],
                                       start=(k == 0), stop=(k == n - 1))
                return mm

            def ada_rows(layer):
                if layer == 0:
                    pe.wait_ge(small_in, 16)
                pe.wait_ge(s["silc"].sem, 1)
                base, ub = SLOTS[f"ada{layer}"] // R, USES[f"ada{layer}"] // 2
                with looped(pe, 6, {used: R}) as i:
                    for p in range(2):
                        pe.wait_ge(pair_free[p].sem, i + ub)
                        for si in range(4):
                            r = 4 * p + si
                            pe.wait_ge(slot_full[r], 16 * (i + base + 1))
                            for kk in range(2):
                                mm = pe.matmul(ps[0:NV, 2 * p, :], silc[:, 2 * si + kk, :],
                                               ring[:, r, kk * 512:(kk + 1) * 512],
                                               start=(si + kk == 0), stop=(si == 3 and kk == 1))
                            used.on(mm)
                for p in range(2):
                    pe.wait_ge(pair_free[p].sem, ub + 6)

            def turn_ada_rows(layer):
                for j in range(48):
                    mm = pe.transpose(ps[:, 4, NV * j:NV * (j + 1)], modrow[layer][0:NV, P * j:P * (j + 1)],
                                      ident[0:NV, 0:NV])
                s["turned"].on(mm)

            def norm_sums(n):
                for c in range(DC):
                    pe.wait_ge(s["sq_ready"].sem, DC * n + c + 1)
                    for half in range(2):
                        mm = pe.matmul(ps[:, 6 + half, 0:TH], ones, hT[:, c, TH * half:TH * (half + 1)],
                                       start=(c == 0), stop=(c == DC - 1))
                s["ss_ready"].on(mm)

            def h_tile(n, c):
                pe.wait_ge(s["h_ready"].sem, DC * n + c + 1)

            pe.sem_inc(s["cb_full"].sem, 2)
            s["cb_full"].base = 2
            for x in x_pe:
                pe.sem_inc(x.sem, 1)
                x.base = 1
            ada_rows(0)
            norm_sums(0)
            turn_ada_rows(0)

            sh, uh = SLOTS["hg"] // R, USES["hg"] // 2

            def project(u, i, norm=None):
                for q in range(3):
                    feature_tile("hg", i + sh, [4 * u + q], q % 2, 4 * i + (uh + 2 * u + q // 2), h_rhs, DC,
                                 norm if q == 0 else None)

            def values(u, i):
                pe.wait_ge(pair_free[1].sem, 4 * i + (uh + 2 * u + 1))
                pe.wait_ge(slot_full[4 * u + 3], 16 * (i + sh + 1))
                for j in range(TJ):
                    m = P if j < 4 else 64
                    dst = ps[:, 2, P * j:P * (j + 1)] if j < 4 else ps[0:64, 3, 0:P]
                    for c in range(DC):
                        mm = pe.matmul(dst, hT[:, c, P * j:P * j + m], ring[:, 4 * u + 3, c * P:(c + 1) * P],
                                       start=(c == 0), stop=(c == DC - 1))
                used.on(mm)

            def scores(u, pair):
                h = 2 * pair + u
                pe.wait_ge(s["elem_ready"].sem, h + 1)
                pe.wait_ge(s["head_rs"].sem, h + 1)
                for c in range(4):
                    for i in range(4):
                        at = c * P + i * BLK
                        pe.matmul(ps[:, 4, at:at + BLK], hg["K"][:, 4 * c + i, :], hg["eq"][:, at:at + BLK],
                                  start=True, stop=True)
                for c in range(4):
                    mm = pe.transpose(ps[:, 6, c * P:(c + 1) * P], hg["kw"][:, c * P:(c + 1) * P], ident)
                s["scored"].on(mm)
                pe.matmul(ps[0:64, 5, 0:64], hg["Ks"], hg["eq"][:, TP:T], start=True, stop=True)
                s["scored_s"].on(pe.transpose(ps[0:64, 5, P:2 * P], hg["kw"][:, TP:T], ident))

            def scan(u, pair):
                h = 2 * pair + u
                v = shaped(hg["v"][:, u, :], TJ, P)
                pe.wait_ge(pair_free[1].sem, 2 * h + (uh + 2))
                pe.wait_ge(s["at_ready"].sem, 2 * h + 2)
                for c in range(4):
                    mm = pe.matmul(ps[:, 7, c * P:(c + 1) * P], hg["ktw"][:, c, :], v[:, c, :], start=True, stop=True)
                s["upd"].on(mm)
                pe.wait_ge(s["vx_ready"].sem, h + 1)
                for half in range(2):
                    mm = pe.matmul(ps[:, 4 + 2 * half, :], hg["ktw"][0:64, 4, :],
                                   hg["Vx"].rearrange("p a b -> p (a b)")[0:64, 512 * half:512 * (half + 1)],
                                   start=True, stop=True)
                s["upd_s"].on(mm)
                for c in range(4):
                    mm = pe.matmul(ps[:, 5, c * P:(c + 1) * P], v[:, c, :], hg["at"][:, c, :], start=True,
                                   stop=(c == 0))
                    if c:
                        pe.wait_ge(s["s_ready"].sem, 4 * h + c)
                        mm = pe.matmul(ps[:, 5, c * P:(c + 1) * P], hg["S"][:, c - 1, :],
                                       hg["qe"][:, c * P:(c + 1) * P], start=False, stop=True)
                s["o_full"].on(mm)
                pe.wait_ge(s["s_ready"].sem, 4 * h + 4)
                pe.wait_ge(s0_in[u], 16 * (pair + 1))
                for b in range(NB):
                    pe.matmul(ps[:, 7, TS * b:TS * (b + 1)], hg["S0"][:, u, P * b:P * (b + 1)],
                              hg["qe"][:, TP + TS * b:TP + TS * (b + 1)], start=(b == 0), stop=False,
                              skip_group_check=True)
                mm = pe.matmul(ps[:, 7, 0:64], v[0:64, 4, :], hg["at"][0:64, 4, 0:64], start=False, stop=True,
                               skip_group_check=True)
                s["o_full"].on(mm)
                pe.wait_ge(s["sq_head"].sem, 2 * h + 2)
                pe.wait_ge(s["o_read"].sem, 2 * h + 2)
                s["head_ss"].on(wide((5, 7), [ones], [hg["sq"]]))

            project(0, 0, norm=0)
            values(0, 0)
            per = {used: 8, s["scored"]: 2, s["scored_s"]: 2, s["upd"]: 2, s["upd_s"]: 2, s["o_full"]: 4,
                   s["head_ss"]: 2}
            with looped(pe, H // 2 - 1, per) as i:
                for u in range(2):
                    project(1 - u, i + u)
                    scores(u, i)
                    values(1 - u, i + u)
                    scan(u, i)
            last = H // 2 - 1
            project(1, last)
            scores(0, last)
            values(1, last)
            scan(0, last)
            ada_rows(1)
            scores(1, last)
            scan(1, last)
            pe.wait_ge(s["s_ready"].sem, 4 * H)
            turn_ada_rows(1)

            def out_proj(phase, nslot, rhs, nk):
                base, ub = SLOTS[phase], USES[phase]
                for m in range(DC):
                    n = base + m * nslot
                    feature_tile(phase, n // R, [(n + k) % R for k in range(nslot)], m % 2, (ub + m) // 2, rhs, nk)

            pe.wait_ge(s["head_done"].sem, H)
            out_proj("wo", 1, lambda k: hg["og"][:, k, :], DC)

            def moe(layer):
                nr = 2 * layer + 1
                norm_sums(nr)
                wr = col("wr", LAYERS, DC, 20)
                for c in range(DC):
                    h_tile(nr, c)
                    for half in range(2):
                        mm = pe.matmul(ps[0:20, 6 + half, 0:TH], wr[:, layer, c, :], hT[:, c, TH * half:TH * (half + 1)],
                                       start=(c == 0), stop=(c == DC - 1))
                s["lgT_full"].on(mm)
                pe.wait_ge(s["lg_ready"].sem, layer + 1)
                for j in range(TJ):
                    m = P if j < 4 else 64
                    mm = pe.transpose(ps[0:m, 3, 20 * j:20 * (j + 1)], mo["lgT"][0:20, P * j:P * j + m], ident[0:20, 0:20])
                s["lg_turned"].on(mm)
                for j in range(TJ):
                    m = P if j < 4 else 64
                    b0 = 4 + 2 * (j % 2)
                    pe.wait_ge(s["htok_ready"].sem, TJ * layer + max(j - 1, 0))
                    for c in range(DC):
                        mm = pe.transpose(ps[0:m, b0 + c // 4, P * (c % 4):P * (c % 4 + 1)],
                                          hT[:, c, P * j:P * j + m], ident)
                    s["htok_full"].on(mm)
                pe.wait_ge(s["ohg_ready"].sem, layer + 1)
                ohg = mo["ohg"].rearrange("p a b -> p (a b)")
                pe.matmul(ps[:, 2, 0:20], strict, ohg, start=True, stop=True)
                s["ranked"].on(pe.matmul(ps[:, 2, 32:52], ones, ohg, start=True, stop=True))
                pe.wait_ge(s["place_ready"].sem, layer + 1)
                for j in range(TJ):
                    m = P if j < 4 else 64
                    dst = ps[:, 2, P * j:P * (j + 1)] if j < 4 else ps[:, 3, 0:64]
                    mm = pe.matmul(dst, ones[0:m, :], dg[0:m, j, 0:m], start=True, stop=True)
                s["pos_full"].on(mm)
                comb = mo["comb"].rearrange("p j a b -> p j (a b)")
                pe.wait_ge(s["spread"].sem, layer + 1)
                pe.wait_ge(s["pos_ready"].sem, layer + 1)
                pe.wait_ge(s["hlo_ready"].sem, TJ * (layer + 1))
                base, un = SLOTS[f"moe{layer}"] // R, USES[f"moe{layer}"]
                for c in range(DC):
                    p = c % 2
                    pe.wait_ge(pair_free[p].sem, (un + c) // 2)
                    for half in range(2):
                        for part in (h_lo, h_hi):
                            for j in range(TJ):
                                m = P if j < 4 else 64
                                mm = pe.matmul(ps[:, 2 * p + half, 0:TH], part[0:m, j, P * c:P * (c + 1)],
                                               P_r[0:m, j, TH * half:TH * (half + 1)],
                                               start=(part is h_lo and j == 0), stop=(part is h_hi and j == TJ - 1))
                    s["gathered"].on(mm)
                    if c == DC - 3:
                        pe.wait_ge(s["comb_ready"].sem, layer + 1)
                        for half in range(2):
                            for j in range(TJ):
                                m = P if j < 4 else 64
                                mm = pe.matmul(ps[0:NE, 4 + half, 0:TW // 2], comb[0:m, j, :],
                                               P_r[0:m, j, TW // 2 * half:TW // 2 * (half + 1)].bitcast(F32),
                                               start=(j == 0), stop=(j == TJ - 1))
                        s["cS_full"].on(mm)
                for p in range(2):
                    pe.wait_ge(pair_free[p].sem, (un + DC) // 2)
                ub = (un + DC) // 2
                with looped(pe, 2, {used: 2 * N_GROUP, s["cb_full"]: 2 * E, s["y_full"]: 2}) as i:
                    for gg in range(2):
                        g = 2 * i + gg
                        at_g = pe.value_load(off_i[0:1, bass.ds(g, 1)], min_val=0, max_val=T)
                        for e in range(E):
                            pe.wait_ge(s["ce_ready"].sem, E * g + ((NE + 2) * layer + e + 1))
                            s["cb_full"].on(pe.matmul(ps[:, 2 * (e % 2) + 1, 0:W], ones[0:NE, :],
                                                      mo["ce"][0:NE, e % 2, :], start=True, stop=True))
                            for f in range(FT):
                                for p in range(2):
                                    r = (4 * e + 2 * f + p) % R
                                    pe.wait_ge(pair_free[p].sem, 16 * i + (ub + 8 * gg + 2 * e + f))
                                    pe.wait_ge(slot_full[r], 16 * (6 * i + (base + 3 * gg + e // 2 + 1)))
                                    for c in range(DC):
                                        mm = pe.matmul(ps[:, 2 * p, 0:W], ring[:, r, c * P:(c + 1) * P],
                                                       mo["hs"][:, c, bass.ds(at_g, W)], start=(c == 0), stop=(c == DC - 1))
                                    used.on(mm)
                        pe.wait_ge(s["yg_ready"].sem, 2 * g + (2 * G * layer + 1))
                        for k in range(KG):
                            pe.wait_ge(slot_full[k], 16 * (6 * i + (base + 3 * gg + 2 + 1)))
                            pe.wait_ge(s["hid_ready"].sem, KG * g + (KG * G * layer + k + 1))
                            for ch in range(2):
                                for half in range(2):
                                    mm = pe.matmul(ps[0:CH[ch], 4 + 2 * ch + half, :],
                                                   mo["hid"][:, k, P * ch:P * ch + CH[ch]],
                                                   ring[:, k, 512 * half:512 * (half + 1)], start=(k == 0), stop=(k == KG - 1))
                                if k == KG - 1 and ch == 0:
                                    s["y_full"].on(mm)
                            used.on(mm)
                pe.wait_ge(s["yg_ready"].sem, 2 * G * (layer + 1) + 1)
                pe.wait_ge(s["pt_ready"].sem, 2 * G * (layer + 1))
                un += DC + 4 * NE
                for m in range(DC):
                    p = m % 2
                    pe.wait_ge(pair_free[p].sem, (un + m) // 2)
                    for half in range(2):
                        for part in (y_lo, y_hi):
                            for q in range(2 * G):
                                n = CH[q % 2]
                                mm = pe.matmul(ps[:, 2 * p + half, 0:TH], part[0:n, q, P * m:P * (m + 1)],
                                               PT_r[0:n, q, TH * half:TH * (half + 1)],
                                               start=(part is y_lo and q == 0), stop=(part is y_hi and q == 2 * G - 1))
                    s["scattered"].on(mm)
                further_windows(layer)

            def further_windows(layer):
                done, dve_done = x_pe[layer], x_dve[layer].sem
                with further(pe, {done: X_PE}) as (k, group, start):
                    for e in range(E):
                        pe.wait_ge(dve_done, X_DVE * k + (5 * e + 1))
                        pe.matmul(ps[:, 1, 0:W], ones[0:NE, :], mo["ce"][0:NE, 0, :], start=True, stop=True)
                        pe.wait_ge(x_w[layer], 96 * k + 16 * (e + 1))
                        for n, bank in enumerate((0, 2, 3, 4)):
                            for c in range(DC):
                                mm = pe.matmul(ps[:, bank, 0:W], xw[:, n, c * P:(c + 1) * P],
                                               mo["hs"][:, c, bass.ds(start, W)], start=(c == 0), stop=(c == DC - 1))
                        done.on(mm)
                    pe.wait_ge(dve_done, X_DVE * k + (5 * E + 2))
                    for b in range(2):
                        pe.wait_ge(x_w[layer], 96 * k + 16 * (E + b + 1))
                        for kk in range(4):
                            n = 4 * b + kk
                            for ch in range(2):
                                for half in range(2):
                                    mm = pe.matmul(ps[0:CH[ch], 4 + 2 * ch + half, :], xhid[:, n, P * ch:P * ch + CH[ch]],
                                                   xw[:, kk, 512 * half:512 * (half + 1)], start=(n == 0), stop=(n == KG - 1))
                        done.on(mm)
                    pe.wait_ge(x_act[layer].sem, X_ACT * k + (E + 1))
                    for m in range(DC):
                        p = m % 2
                        if m >= 2:
                            pe.wait_ge(dve_done, X_DVE * k + (5 * E + 2 + 4 * (m - 1)))
                        for half in range(2):
                            for q in range(2):
                                mm = pe.matmul(ps[:, 2 * p + half, 0:TH], xy[0:CH[q], q, P * m:P * (m + 1)],
                                               mo["PT"][0:CH[q], q, TH * half:TH * (half + 1)], start=(q == 0), stop=(q == 1))
                        done.on(mm)
                    pe.wait_ge(dve_done, X_DVE * (k + 1))
                    pe.wait_ge(x_act[layer].sem, X_ACT * (k + 1))

            moe(0)
            norm_sums(2)

            sx, ux = SLOTS["xm"] // R, USES["xm"] // 2

            def values_and_gates(j, k):
                u, i = k % 2, 8 * j + k
                pe.wait_ge(s["bdv_ready"].sem, i + 1)
                pe.wait_ge(s["xm_ready"].sem, 3 * i + 3)
                pe.wait_ge(pair_free[u].sem, ux + i // 2 + 1)
                pe.wait_ge(s["v_read"].sem, i)
                for t in range(4):
                    pe.matmul(ps[:, 4, P * t:P * (t + 1)], first["xpad"][:, u, 3 + P * t:3 + P * (t + 1)],
                              first["bdv"][:, u, :], start=True, stop=True)
                mm = pe.matmul(ps[0:64, 5, 0:P], first["xs"][:, u, :], first["bdv"][:, u, :], start=True, stop=True)
                s["v_full"].on(mm)
                pe.wait_ge(s["xc_ready"].sem, i + 1)
                return i, u, ml["xc"][:, i, :]

            def gates(j, k, start, stop):
                i, u, xc_i = values_and_gates(j, k)
                gm, gx = first["gm"][:, u, :], first["gx"][:, u, :]
                pe.matmul(ps[0:64, 6, 0:TP], gm, first["xpad"][:, u, 3:3 + TP], start=start, stop=False)
                pe.matmul(ps[0:64, 6, 0:TP], gx, xc_i[:, 0:TP], start=False, stop=stop)
                pe.matmul(ps[0:64, 7, 0:64], gm, first["xs"][:, u, :], start=start, stop=False)
                s["gates_full"].on(pe.matmul(ps[0:64, 7, 0:64], gx, xc_i[:, TP:T], start=False, stop=stop))

            for j in range(2):
                for k in range(8):
                    feature_tile("xm", sx + j, [k], k % 2, ux + 4 * j + k // 2, h_rhs, DC,
                                 2 if j + k == 0 else None)
                    if k:
                        gates(j, k - 1, j == 0 and k == 1, False)
                gates(j, 7, False, j == 1)

            ub = USES["b"]
            un = [ub]

            def use():
                n = un[0]
                un[0] += 1
                pe.wait_ge(pair_free[n % 2].sem, n // 2)
                return n % 2

            def gate_tile(h, i):
                n = SLOTS["z"] + HT * h + i
                m = un[0]
                un[0] += 1
                feature_tile("z", n // R, [n % R], m % 2, m // 2, h_rhs, DC)

            full = s["b_full"]
            weighted = [mx[f"P{j}"] for j in range(4)]
            bdq = ml["W"].rearrange("p a b -> p (a b)")
            def queries_and_keys(h):
                pe.wait_ge(s["bd_ready"].sem, h + 1)
                for w in range(2):
                    for i in range(HT):
                        p = use()
                        at = (HT * w + i) * P
                        full.on(wide((2 * p, 2 * p + 1), [bdq[:, at:at + P]], [ml["xc"][:, HT * h + i, :]]))

            queries_and_keys(0)
            pe.wait_ge(s["rows_ready"].sem, 1)
            for n, src in enumerate((gate["u"], gate["t1"])):
                for j in range(TJ):
                    m = P if j < 4 else 64
                    mm = pe.transpose(ps[0:m, 4, 32 * n + MH * j:32 * n + MH * (j + 1)], src[0:MH, P * j:P * j + m],
                                      ident[0:MH, 0:MH])
            s["turned_g"].on(mm)
            pe.wait_ge(s["tok_ready"].sem, 2)

            for h in range(MH):
                hb = ub + N_HEADB * h
                if h:
                    queries_and_keys(h)
                pe.wait_ge(s["c_done"].sem, HT * NB * h)
                pe.wait_ge(s["cp_ready"].sem, HT * h)
                for j in range(TJ):
                    m = P if j < 4 else 64
                    bank = 4 + j if j < 4 else 2 * use()
                    for i in range(HT):
                        mm = pe.matmul(ps[0:m, bank, P * i:P * (i + 1)], ml["xc"][:, HT * h + i, P * j:P * j + m],
                                       bdq[:, (HT + i) * P:(HT + i + 1) * P], start=True, stop=True)
                s["kt_full"].on(mm)
                for k in range(4):
                    p = use()
                    sel = ident[32 * k:32 * k + MH, 32 * k + h:32 * k + h + 1].broadcast_to([MH, P])
                    row = ml["rows"][32 * k:32 * k + MH, :]
                    if k < 3:
                        mm = wide((2 * p, 2 * p + 1), [sel], [row])
                    else:
                        mm = pe.matmul(ps[:, 2 * p, 0:64], sel, row[:, TP:T], start=True, stop=True)
                    full.on(mm)
                pe.wait_ge(s["kt_read"].sem, h + 1)
                for j in range(TJ):
                    m = P if j < 4 else 64
                    bank = 4 + j if j < 4 else 2 * use()
                    hi = TP if j < 4 else T
                    for p in range(2):
                        pe.wait_ge(pair_free[p].sem, (hb + 8) // 2)
                    for i in range(HT):
                        mm = pe.matmul(ps[0:m, bank, 0:hi - P * j], ml["kz"][:, i, P * j:P * j + m],
                                       ml["q"][:, i, P * j:hi], start=(i == 0), stop=(i == HT - 1))
                s["s_full"].on(mm)
                gate_tile(h, 0)
                pe.wait_ge(s["p_ready"].sem, 5 * h + 5)
                pe.wait_ge(s["qw_ready"].sem, h + 1)
                p = use()
                samples = ps[0:64, 2 * p, :]
                dn = ps[:, 2 * p + 1, 0:64]
                pe.matmul(dn, ones[0:64, :], mx["Ps"][0:64, :], start=True, stop=False)
                for i in range(HT):
                    mm = pe.matmul(dn, ones, qn[:, i, :], start=False, stop=(i == HT - 1))
                s["num_s"].on(mm)
                for b in range(NB):
                    n = NB * h + b
                    C = shaped(ml["C"][:, n % 2, :], HT, MD)
                    pe.wait_ge(s["alone_ready"].sem, n + 1)
                    for k in range(HT):
                        if k % 2 == 0:
                            pe.wait_ge(c_in[n % 2][k // 2], 16 * (n // 2 + 1))
                        mm = pe.matmul(samples, alone[:, b % 2, k, :], C[:, k, :], start=(b + k == 0), stop=False,
                                       skip_group_check=True)
                    s["num_s"].on(mm)
                    pe.wait_ge(s["kb_ready"].sem, n + 1)
                    for k in range(HT):
                        if n:
                            pe.wait_ge(s["c_done"].sem, HT * (n - 1) + k + 1)
                        mm = pe.matmul(ps[:, 4 + k, :], mx["kb"][0:64, P * k:P * (k + 1)],
                                       ml["vtok"][0:64, 4, MD * h:MD * (h + 1)], start=True, stop=True)
                        s["upd_c"].on(mm)
                s["num_full"].on(pe.matmul(samples, mx["Ps"][0:64, :], ml["vtok"][0:64, 4, MD * h:MD * (h + 1)],
                                           start=False, stop=True, skip_group_check=True))
                pe.wait_ge(s["c_done"].sem, HT * NB * (h + 1))
                for k in range(HT):
                    for j in range(4):
                        mm = pe.matmul(ps[:, 4 + k, :], ml["ktok"][:, j, P * k:P * (k + 1)],
                                       ml["vtok"][:, j, MD * h:MD * (h + 1)], start=(j == 0), stop=(j == 3))
                    s["cp_full"].on(mm)
                pe.wait_ge(s["raw_ready"].sem, h + 1)
                for i in range(HT):
                    mm = pe.transpose(ps[:, 2 * p, 64 * i:64 * (i + 1)], mx["kb"][0:64, P * i:P * (i + 1)], ident[0:64, 0:64])
                s["turned_s"].on(mm)
                for i in range(HT + 1):
                    p = use()
                    for j in range(4):
                        lhs = ones if i == 0 else ml["vtok"][:, j, MD * h + P * (i - 1):MD * h + P * i]
                        mm = pe.matmul(ps[:, 2 * p, P * j:TP], lhs, weighted[j], start=(j == 0), stop=(j == 3),
                                       skip_group_check=True)
                    full.on(mm)
                gate_tile(h, 1)
                pe.wait_ge(pair_free[(hb + 20) % 2].sem, (hb + 20) // 2 + 1)
                p = use()
                s["mu_full"].on(wide((2 * p, 2 * p + 1), [ones] * HT, [ml["q"][:, i, :] for i in range(HT)]))
                gate_tile(h, 2)
                pe.wait_ge(s["sqh_ready"].sem, h + 1)
                p = use()
                sqh = shaped(ml["ktok"].rearrange("p a b -> p (a b)")[:, 0:HT * T], HT, T)
                s["var_full"].on(wide((2 * p, 2 * p + 1), [ones] * HT, [sqh[:, i, :] for i in range(HT)]))
                gate_tile(h, 3)
            assert un[0] == USES["md"], (un[0], USES["md"])
            pe.wait_ge(s["ho_ready"].sem, MH)
            out_proj("md", 2, lambda k: ml["xc"][:, k, :], MT)
            moe(1)
            norm_sums(4)

        def halves(p):
            return ps[:, 2 * p:2 * p + 2, 0:TH]

        def two(ap):
            return ap.rearrange("p (a n) -> p a n", a=2)

        def at(tensor, i):
            return tensor[:, i] if isinstance(i, int) else tensor[:, bass.ds(i, 1)].rearrange(
                "p a n -> p (a n)")

        KS = float(MD) ** -0.5

        @block.scalar
        def _(act):
            A = s["act"]
            used = s["slot_used"].sem

            def squares(n):
                for c in range(DC):
                    if n:
                        act.wait_ge(s["x_tile"].sem, DC * (n - 1) + c + 1)
                    s["sq_ready"].on(act.activation(hT[:, c, :], xT[:, c, :], ACT.Square))

            def norm(n):
                act.wait_ge(s["ss_ready"].sem, n + 1)
                A.link(act, act.activation(two(rstd), halves(3), ACT.Ln, bias=eps, scale=1.0 / D))
                s["rstd_ready"].on(act.activation(rstd, rstd, ACT.Exp, scale=-0.5))
                if n < 2 * LAYERS:
                    for c in range(DC):
                        act.wait_ge(s["scaled"].sem, DC * n + c + 1)
                        s["h_ready"].on(act.activation(hT[:, c, 0:TP], hT[:, c, 0:TP], ACT.Identity,
                                                       bias=modt[:, n // 2, 24 * (n % 2) + c, 0:1]))

            def ada_rows(layer):
                base, ub = SLOTS[f"ada{layer}"], USES[f"ada{layer}"] // 2
                with looped(act, 6, {}) as i:
                    for p in range(2):
                        act.wait_ge(used, R * i + (base + 4 * (p + 1)))
                        dst = modrow[layer][0:NV, bass.ds((2 * i + p) * 512, 512)]
                        pair_free[p].on(act.copy(dst, ps[0:NV, 2 * p, :]))

            for p in range(2):
                act.sem_inc(pair_free[p].sem, 1)
            act.sem_inc(s["head_rs"].sem, 1)
            s["head_rs"].base = 1
            act.wait_ge(small_in, 16)
            s["silc"].on(act.activation(silc, silc, ACT.Silu))
            ada_rows(0)
            act.wait_ge(x_in, 16)
            squares(0)
            norm(0)

            act.wait_ge(s["lb_in"].sem, 1)
            s["lb_out"].on(act.activation(hg["t1"], hg["t1"], ACT.Exp))
            base = SLOTS["hg"]

            def evict(u, h, guarded):
                if guarded:
                    act.wait_ge(s["head_done"].sem, h - 1)
                for q, (dst, f, k) in enumerate(((hg["th"], ACT.Tanh, 0.5), (hg["q"], ACT.Silu, 1.0),
                                                 (hg["zg"], ACT.Silu, 1.0))):
                    act.wait_ge(used, 4 * h + (base + q + 1))
                    pair_free[q % 2].on(act.activation(two(dst[:, u, :]), halves(q % 2), f, scale=k))
                act.wait_ge(used, 4 * h + (base + 4))
                act.copy(hg["v"][:, u, 0:512], ps[:, 2, :])
                pair_free[1].on(act.copy(hg["v"][0:64, u, 512:512 + P], ps[0:64, 3, 0:P]))

            def exponentials(h):
                act.wait_ge(s["decay"].sem, h + 1)
                s["f_ready"].on(act.activation(hg["g"], hg["g"], ACT.Ln))
                act.wait_ge(s["diffs"].sem, 3 * h + 1)
                A.link(act, act.activation(hg["Ks"], hg["eq"][:, TP:T], ACT.Exp, scale=-1.0))
                s["exps"].on(act.activation(hg["eq"], hg["eq"], ACT.Exp))
                act.wait_ge(s["diffs"].sem, 3 * h + 2)
                s["exps"].on(act.activation(hg["K"], hg["K"], ACT.Exp))
                act.wait_ge(s["diffs"].sem, 3 * h + 3)
                s["exps"].on(act.activation(hg["qe"], hg["b"], ACT.Exp))
                s["exps"].on(act.activation(hg["kw"], hg["kw"], ACT.Exp))

            def head_norm(h):
                act.wait_ge(s["o_read"].sem, 2 * h + 1)
                s["sq_head"].on(act.activation(hg["sq"][:, 0:TP], ps[:, 5, :], ACT.Square))
                act.wait_ge(s["o_read"].sem, 2 * h + 2)
                s["sq_head"].on(act.activation(hg["sq"][:, TP:T], ps[:, 7, 0:64], ACT.Square))
                act.wait_ge(s["head_ss"].sem, h + 1)
                act.activation(hg["rs"][:, 0:TH], ps[:, 5, 0:TH], ACT.Ln, bias=eps, scale=1.0 / P)
                A.link(act, act.activation(hg["rs"][:, TH:T], ps[:, 7, 0:TH], ACT.Ln, bias=eps, scale=1.0 / P))
                s["head_rs"].on(act.activation(hg["rs"], hg["rs"], ACT.Exp, scale=-0.5))

            evict(0, 0, False)
            exponentials(0)
            evict(1, 1, False)
            head_norm(0)
            per = {A: 4, s["f_ready"]: 2, s["exps"]: 8, s["sq_head"]: 4, s["head_rs"]: 2}
            with looped(act, H // 2 - 1, per) as i:
                for u in range(2):
                    h = 2 * i + (u + 1)
                    exponentials(h)
                    evict(u, h + 1, True)
                    head_norm(h)
            exponentials(H - 1)
            ada_rows(1)
            head_norm(H - 1)

            def moe(layer):
                squares(2 * layer + 1)
                norm(2 * layer + 1)
                act.wait_ge(s["lgT_full"].sem, layer + 1)
                act.wait_ge(sn_out, 32 * H)
                s["lg_ready"].on(act.activation(two(mo["lgT"][0:20, :]), ps[0:20, 6:8, 0:TH], ACT.Identity,
                                                bias=col("rb")[0:20, layer:layer + 1]))
                for j in range(TJ):
                    m = P if j < 4 else 64
                    act.wait_ge(s["htok_full"].sem, TJ * layer + j + 1)
                    b0 = 4 + 2 * (j % 2)
                    act.copy(h_hi[0:m, j, :].rearrange("p (a n) -> p a n", a=2), ps[0:m, b0:b0 + 2, :])
                    if j >= 2:
                        act.wait_ge(s["hlo_ready"].sem, TJ * layer + j - 1)
                    s["htok_ready"].on(act.copy(h_tok[0:m, j % 2, :].rearrange("p (a n) -> p a n", a=2), ps[0:m, b0:b0 + 2, :]))
                act.wait_ge(s["pos_full"].sem, layer + 1)
                A.link(act, act.copy(pos_row[:, 0:TP], ps[:, 2, :]))
                s["pos_ready"].on(act.copy(pos_row[:, TP:T], ps[:, 3, 0:64]))
                for c in range(DC):
                    act.wait_ge(s["gathered"].sem, DC * layer + c + 1)
                    pair_free[c % 2].on(act.copy(two(mo["hs"][:, c, 0:T]), halves(c % 2)))
                    if c == 1:
                        act.wait_ge(s["top_in"].sem, layer + 1)
                        A.link(act, act.activation(mo["r1"], mo["r1"], ACT.Exp))
                        s["top_out"].on(act.activation(mo["s2"], mo["s2"], ACT.Exp))
                    if c == DC - 3:
                        act.wait_ge(s["cS_full"].sem, layer + 1)
                        s["cS_ready"].on(act.copy(mo["cS"][0:NE, :].rearrange("p (a n) -> p a n", a=2),
                                                  ps[0:NE, 4:6, 0:TW // 2]))
                base, ub = SLOTS[f"moe{layer}"], (USES[f"moe{layer}"] + DC) // 2
                with looped(act, 2, {s["y_hi_ready"]: 2 * 2}) as i:
                    for gg in range(2):
                        for t in range(E * FT):
                            act.wait_ge(used, 2 * N_GROUP * i + (base + N_GROUP * gg + 2 * t + 1))
                            act.wait_ge(pair_free[1].sem, 16 * i + (ub + 8 * gg + t))
                            pair_free[0].on(act.activation(mo["sil"], ps[:, 0, 0:W], ACT.Silu))
                        y = y_hi[:, bass.ds(4 * i + 2 * gg, 2), :]
                        act.wait_ge(s["y_full"].sem, 2 * i + (2 * 2 * layer + gg + 1))
                        s["y_hi_ready"].on(act.copy(y[:, 0, :].rearrange("p (a n) -> p a n", a=2), ps[:, 4:6, :]))
                        act.wait_ge(used, 2 * N_GROUP * i + (base + N_GROUP * (gg + 1)))
                        s["y_hi_ready"].on(act.copy(y[0:CH[1], 1, :].rearrange("p (a n) -> p a n", a=2), ps[0:CH[1], 6:8, :]))

            def further_windows(layer):
                done = x_act[layer]
                for k in range(MORE):
                    with further_one(act, k):
                        for e in range(E):
                            act.wait_ge(x_pe[layer].sem, X_PE * k + (e + 2))
                            act.activation(mo["sil"], ps[:, 0, 0:W], ACT.Silu)
                            done.on(act.activation(xsil, ps[:, 3, 0:W], ACT.Silu))
                        act.wait_ge(x_pe[layer].sem, X_PE * k + 7)
                        act.copy(xy[:, 0, :].rearrange("p (a n) -> p a n", a=2), ps[:, 4:6, :])
                        done.on(act.copy(xy[0:CH[1], 1, :].rearrange("p (a n) -> p a n", a=2), ps[0:CH[1], 6:8, :]))
                        act.wait_ge(x_dve[layer].sem, X_DVE * (k + 1))
                        for c in range(DC):
                            ins = act.activation(hT[:, c, :], xT[:, c, :], ACT.Square)
                        done.on(ins)

            moe(0)
            squares(2)
            further_windows(0)
            norm(2)

            base = SLOTS["xm"]

            def inner(u, i, guarded):
                act.wait_ge(used, i + (base + 1))
                if guarded:
                    act.wait_ge(s["gates_full"].sem, i - 1)
                    act.wait_ge(s["conv_acc"].sem, i - 1)
                xp = first["xpad"][:, u, :]
                s["xm_ready"].on(act.copy(xp[:, 3:3 + TH], ps[:, 2 * u, 0:TH]))
                s["xm_ready"].on(act.copy(xp[:, 3 + TH:3 + TP], ps[:, 2 * u + 1, 0:TP - TH]))
                src = ps[:, 2 * u + 1, TP - TH:TH].rearrange("p (b t) -> p b t", b=NB)
                s["xm_ready"].on(act.copy(xp[:, 3 + TP:].rearrange("p (b t) -> p b t", b=NB)[:, :, 3:], src))
                pair_free[u].on(act.copy(first["xs"][:, u, :].rearrange("p (b t) -> p b t", b=NB), src))
                act.wait_ge(s["conv_acc"].sem, i + 1)
                s["xc_ready"].on(act.activation(at(ml["xc"], i), first["acc"], ACT.Silu))

            inner(0, 0, False)
            inner(1, 1, False)
            with looped(act, MT // 2 - 1, {s["xm_ready"]: 6, s["xc_ready"]: 2}) as i:
                for u in range(2):
                    inner(u, 2 * i + (u + 2), True)

            un = [USES["b"]]

            def use(sem, value):
                n = un[0]
                un[0] += 1
                act.wait_ge(sem, value)
                return n % 2

            nf = [0]

            def read_full():
                nf[0] += 1
                return use(s["b_full"].sem, nf[0])

            def query_or_key(i):
                p = read_full()
                if i < HT:
                    pair_free[p].on(act.copy(two(ml["q"][:, i, :]), halves(p)))
                else:
                    pair_free[p].on(act.activation(two(ml["kz"][:, i - HT, :]), halves(p), ACT.Identity, scale=KS))

            query_or_key(0)
            act.wait_ge(s["abs_ready"].sem, 1)
            t1, t2, gb = gate["t1"][0:MH, :], gate["t2"][0:MH, :], gate["b"][0:MH, :]
            A.link(act, act.activation(t2, t2, ACT.Exp, scale=-1.0))
            s["soft_ready"].on(act.activation(t2, t2, ACT.Ln, bias=ones[0:MH, 0:1]))
            for i in range(1, 6):
                query_or_key(i)
            act.wait_ge(s["dec_ready"].sem, 1)
            A.link(act, act.activation(t1, t1, ACT.Exp))
            s["dec_exp"].on(act.activation(gb[:, TP:T], gb[:, TP:T], ACT.Exp))
            for i in range(6, 8):
                query_or_key(i)

            act.wait_ge(x_kept, 16)

            def output_gate(h, i):
                p = use(used, SLOTS["z"] + HT * h + i + 1)
                pair_free[p].on(act.activation(two(ml["kz"][:, i, :]), halves(p), ACT.Silu))

            for h in range(MH):
                if h:
                    act.wait_ge(s["ho_ready"].sem, h)
                    for i in range(2 * HT):
                        query_or_key(i)
                un[0] += 1
                p = read_full()
                pair_free[p].on(act.copy(two(mx["nM"]), halves(p)))
                p = read_full()
                pair_free[p].on(act.activation(two(mx["emn"]), halves(p), ACT.Exp, scale=-1.0))
                p = read_full()
                pair_free[p].on(act.copy(two(mx["mu"]), halves(p)))
                p = read_full()
                pair_free[p].on(act.copy(mx["wcb"], ps[:, 2 * p, 0:64]))
                un[0] += 1
                for j in range(TJ):
                    act.wait_ge(s["w_ready"].sem, 5 * h + j + 1)
                    n = TP - P * j if j < 4 else 64
                    w = ml["W"][:, j % 2, 0:n] if j < 4 else ml["W"][0:64, 0, 0:64]
                    s["w_exp"].on(act.activation(w, w, ACT.Exp))
                act.wait_ge(s["n_ready"].sem, h + 1)
                act.wait_ge(s["s_full"].sem, h + 1)
                output_gate(h, 0)
                un[0] += 1
                for b in range(NB):
                    n = NB * h + b
                    act.wait_ge(s["upd_c"].sem, HT * n)
                    s["kb_ready"].on(act.activation(mx["kb"][0:64, :], ml["ktok"][0:64, 4, :], ACT.Identity,
                                                    scale=own[0:64, b:b + 1]))
                act.wait_ge(s["num_full"].sem, h + 1)
                s["raw_ready"].on(act.copy(mx["kb"][0:64, :], ps[0:64, 2 * ((un[0] - 1) % 2), :]))
                for k in range(HT):
                    n = HT * h + k
                    act.wait_ge(s["cp_full"].sem, n + 1)
                    if n >= 2:
                        act.wait_ge(cp_out[k % 2], 16 * (n // 2))
                    s["cp_ready"].on(act.copy(ml["W"][:, k % 2, :], ps[:, 4 + k, :]))
                un[0] += 5
                nf[0] += 5
                output_gate(h, 1)
                un[0] += 1
                act.wait_ge(s["rs_h"].sem, h + 1)
                sqh = shaped(ml["ktok"].rearrange("p a b -> p (a b)")[:, 0:HT * T], HT, T)
                s["sqh_ready"].on(act.activation(sqh, ml["q"], ACT.Square))
                output_gate(h, 2)
                n = un[0]
                p = use(s["var_full"].sem, h + 1)
                pair_free[p].on(act.activation(two(mx["rs"]), halves(p), ACT.Ln, bias=eps, scale=1.0 / MD))
                act.wait_ge(pair_free[p].sem, n // 2 + 1)
                s["rsh_ready"].on(act.activation(mx["rs"], mx["rs"], ACT.Exp, scale=-0.5))
                output_gate(h, 3)
            moe(1)
            squares(4)
            further_windows(1)
            norm(4)

        @block.vector
        def _(dve):
            V = s["dve"]
            used = s["slot_used"].sem
            tt, ts, stt = dve.tensor_tensor, dve.tensor_scalar, dve.scalar_tensor_tensor

            def over_t(ap):
                return ap.unsqueeze(len(ap.shape)).broadcast_to(list(ap.shape) + [TS])

            def by_seq(ap):
                return ap.rearrange("p (b t) -> p b t", b=NB)

            def modulation(layer):
                dve.wait_ge(s["turned"].sem, layer + 1)
                V.link(dve, tt(modt[:, layer], shaped(ps[:, 4, 0:48 * NV], 48, NV),
                               col("bada", LAYERS, 48)[:, layer, :].unsqueeze(2).broadcast_to([P, 48, NV]), ALU.add))
                for k in range(2):
                    g = col("ng", LAYERS, 2, DC)[:, layer, k, :].unsqueeze(2).broadcast_to([P, DC, NV])
                    V.link(dve, stt(amod[:, layer, k], modt[:, layer, 24 * k + 8:24 * k + 16, :], 1.0, g, ALU.add, ALU.mult))

            def norm(n):
                layer, k = n // 2, n % 2
                dve.wait_ge(s["rstd_ready"].sem, n + 1)
                if n == 2 * LAYERS:
                    for c in range(DC):
                        s["y_ready"].on(stt(hT[:, c, :], xT[:, c, :], col("fg")[:, c:c + 1], rstd, ALU.mult, ALU.mult))
                    return
                by_token = lambda ap: ap.rearrange("p c (b t) -> p c b t", b=NB)
                hs = by_token(hT[:, :, TP:T])
                V.link(dve, tt(hT[:, :, TP:T], xT[:, :, TP:T], rstd[:, TP:T].unsqueeze(1).broadcast_to([P, DC, T - TP]),
                               ALU.mult))
                V.link(dve, tt(hs, hs, over_t(amod[:, layer, k, :, 1:NV]), ALU.mult))
                tt(hs, hs, over_t(modt[:, layer, 24 * k:24 * k + DC, 1:NV]), ALU.add)
                for c in range(DC):
                    s["scaled"].on(stt(hT[:, c, 0:TP], xT[:, c, 0:TP], amod[:, layer, k, c, 0:1], rstd[:, 0:TP],
                                       ALU.mult, ALU.mult))

            def gated(full, base, nslot, use, layer, k, tmp):
                for m in range(DC):
                    p = m % 2
                    dve.wait_ge(full, base + (m + 1) * nslot)
                    g = modt[:, layer, 24 * k + 16 + m, :]
                    stt(xT[:, m, 0:TH], ps[:, 2 * p, 0:TH], g[:, 0:1], xT[:, m, 0:TH], ALU.mult, ALU.add)
                    stt(xT[:, m, TH:TP], ps[:, 2 * p + 1, 0:TP - TH], g[:, 0:1], xT[:, m, TH:TP], ALU.mult, ALU.add)
                    pair_free[p].on(tt(by_seq(tmp), by_seq(ps[:, 2 * p + 1, TP - TH:TH]), over_t(g[:, 1:NV]), ALU.mult))
                    dve.wait_ge(pair_free[p].sem, (use + m) // 2 + 1)
                    s["x_tile"].link(dve, tt(xT[:, m, TP:T], xT[:, m, TP:T], tmp, ALU.add))

            dve.sem_inc(s["yg_ready"].sem, 1)
            s["yg_ready"].base = 1
            dve.wait_ge(small_in, 16)
            modulation(0)
            norm(0)
            lb = col("lb", 3, H)
            V.link(dve, tt(hg["t2"], lb[:, 0], lb[:, 1], ALU.max))
            V.link(dve, tt(hg["t2"], hg["t2"], lb[:, 2], ALU.max))
            s["lb_in"].on(tt(hg["t1"], lb, hg["t2"].unsqueeze(1).broadcast_to([P, 3, H]), ALU.subtract))
            dve.wait_ge(s["lb_out"].sem, 1)
            V.link(dve, tt(hg["t2"], hg["t1"][:, 0], hg["t1"][:, 1], ALU.add))
            V.link(dve, tt(hg["t2"], hg["t2"], hg["t1"][:, 2], ALU.add))
            V.link(dve, dve.reciprocal(hg["t2"], hg["t2"]))
            V.link(dve, tt(hg["t2"], hg["t1"][:, 0], hg["t2"], ALU.mult))
            V.link(dve, ts(hg["half"], hg["t2"], -0.5, 0.5, ALU.mult, ALU.add))
            V.link(dve, tt(hg["low"], hg["half"], hg["t2"], ALU.add))

            dve.wait_ge(keep_in, 16)
            uh = USES["hg"] // 2

            def elementwise(u, h):
                th, q = hg["th"][:, u, :], hg["q"][:, u, :]
                k, g, b, eq, K, Ks, qe, kw = (hg[n] for n in ("k", "g", "b", "eq", "K", "Ks", "qe", "kw"))
                half = hg["half"][:, h:h + 1] if isinstance(h, int) else hg["half"][:, bass.ds(h, 1)]
                low = hg["low"][:, h:h + 1] if isinstance(h, int) else hg["low"][:, bass.ds(h, 1)]
                dve.wait_ge(pair_free[0].sem, 2 * h + (uh + 1))
                V.link(dve, ts(g, th, half, low, ALU.mult, ALU.add))
                s["decay"].link(dve, ts(k, g, -1.0, 1.0, ALU.mult, ALU.add))
                dve.wait_ge(s["f_ready"].sem, h + 1)
                V.link(dve, dve.tensor_tensor_scan(b, hg["keep"], g, 0.0, ALU.mult, ALU.add))
                b3 = b[:, 0:TP].rearrange("p (i t) -> p i t", t=BLK)
                mid = b3[:, :, BLK // 2]
                bs = by_seq(b[:, TP:T])
                tt(eq[:, 0:TP].rearrange("p (i t) -> p i t", t=BLK), b3,
                   mid.unsqueeze(2).broadcast_to([P, 16, BLK]), ALU.subtract)
                s["diffs"].on(tt(by_seq(eq[:, TP:T]), bs, over_t(bs[:, :, TS // 2]), ALU.subtract))
                V.link(dve, tt(K.rearrange("p (c i) t -> p c i t", c=4),
                               mid.rearrange("p (c i) -> p c i", c=4).unsqueeze(3).broadcast_to([P, 4, 4, P]),
                               b[:, 0:TP].rearrange("p (c t) -> p c t", c=4).unsqueeze(2).broadcast_to([P, 4, 4, P]),
                               ALU.subtract))
                s["diffs"].on(dve.tensor_scalar_min(K, K, CLAMP))
                bc = b[:, 0:TP].rearrange("p (c t) -> p c t", c=4)
                tt(kw[:, 0:TP].rearrange("p (c t) -> p c t", c=4),
                   bc[:, :, P - 1].unsqueeze(2).broadcast_to([P, 4, P]), bc, ALU.subtract)
                s["diffs"].on(tt(by_seq(kw[:, TP:T]), over_t(bs[:, :, TS - 1]), bs, ALU.subtract))
                dve.wait_ge(pair_free[1].sem, 2 * h + (uh + 1))
                dve.wait_ge(s["exps"].sem, 4 * h + 1)
                tt(eq, q, eq, ALU.mult)
                tt(Ks, k[:, TP:T], Ks, ALU.mult)
                dve.wait_ge(s["exps"].sem, 4 * h + 2)
                K4 = K.rearrange("p (c i) t -> p c i t", c=4)
                tt(K4, K4, k[:, 0:TP].rearrange("p (c t) -> p c t", c=4).unsqueeze(2).broadcast_to([P, 4, 4, P]),
                   ALU.mult)
                dve.wait_ge(s["exps"].sem, 4 * h + 4)
                el = hg["sq"][:, 0:12]
                tt(el[:, 0:4].unsqueeze(2), qe[:, 0:TP].rearrange("p (c t) -> p c t", c=4)[:, :, P - 1:P],
                   col("ones")[:, 0:4].unsqueeze(2), ALU.mult)
                V.link(dve, tt(el[:, 4:12].unsqueeze(2), by_seq(qe[:, TP:T])[:, :, TS - 1:TS],
                               col("ones")[:, 0:8].unsqueeze(2), ALU.mult))
                V.link(dve, dve.tensor_copy(hg["t1"].rearrange("p a b -> p (a b)")[:, 0:12], el))
                tt(qe, q, qe, ALU.mult)
                s["elem_ready"].on(tt(kw, k, kw, ALU.mult))

            def scan(u, pair):
                h = 2 * pair + u
                v = shaped(hg["v"][:, u, :], TJ, P)
                el = hg["t1"].rearrange("p a b -> p (a b)")
                dve.wait_ge(s["scored"].sem, h + 1)
                tt(hg["at"][:, 0:4, :], shaped(ps[:, 4, :], 4, P), causal.unsqueeze(1).broadcast_to([P, 4, P]), ALU.mult)
                s["at_ready"].on(dve.tensor_copy(hg["ktw"][:, 0:4, :], shaped(ps[:, 6, :], 4, P)))
                dve.wait_ge(s["scored_s"].sem, h + 1)
                tt(hg["at"][0:64, 4, 0:64], ps[0:64, 5, 0:64], causal_s[0:64, :], ALU.mult)
                s["at_ready"].on(dve.tensor_copy(hg["ktw"][0:64, 4, :], ps[0:64, 5, P:2 * P]))
                dve.wait_ge(pair_free[1].sem, 2 * h + (uh + 2))
                s["vx_ready"].on(tt(hg["Vx"][0:64], v[0:64, 4, :].unsqueeze(1).broadcast_to([64, NB, P]),
                                    own[0:64, :].unsqueeze(2).broadcast_to([64, NB, P]), ALU.mult))
                dve.wait_ge(s["upd"].sem, h + 1)
                dve.wait_ge(s["sn_kept"].sem, h + 1)
                s["s_ready"].link(dve, dve.tensor_copy(hg["S"][:, 0, :], ps[:, 7, 0:P]))
                for c in range(1, 4):
                    s["s_ready"].link(dve, stt(hg["S"][:, c, :], hg["S"][:, c - 1, :], el[:, c:c + 1],
                                               ps[:, 7, c * P:(c + 1) * P], ALU.mult, ALU.add))
                dve.wait_ge(s["upd_s"].sem, h + 1)
                dve.wait_ge(s0_in[u], 16 * (pair + 1))
                Sn = hg["Sn"]
                V.link(dve, tt(Sn, shaped(hg["S0"][:, u, :], NB, P), el[:, 4:12].unsqueeze(2).broadcast_to([P, NB, P]),
                               ALU.mult))
                Sn2 = Sn.rearrange("p (a b) n -> p a (b n)", a=2)
                tt(Sn2[:, 0], Sn2[:, 0], ps[:, 4, :], ALU.add)
                s["sn_ready"].on(tt(Sn2[:, 1], Sn2[:, 1], ps[:, 6, :], ALU.add))
                og = at(hg["og"], h)
                gn = col("hgn")
                dve.wait_ge(s["o_full"].sem, 2 * h + 1)
                s["o_read"].on(ts(og[:, 0:TP], ps[:, 5, :], gn, None, ALU.mult))
                dve.wait_ge(s["o_full"].sem, 2 * h + 2)
                s["o_read"].link(dve, ts(og[:, TP:T], ps[:, 7, 0:64], gn, None, ALU.mult))
                dve.wait_ge(s["head_rs"].sem, h + 2)
                V.link(dve, tt(og, og, hg["rs"], ALU.mult))
                dve.wait_ge(pair_free[0].sem, 2 * h + (uh + 2))
                s["head_done"].link(dve, tt(og, og, hg["zg"][:, u, :], ALU.mult))

            names = {"decay": 1, "diffs": 3, "elem_ready": 1, "at_ready": 2, "vx_ready": 1, "s_ready": 4,
                     "sn_ready": 1, "o_read": 2, "head_done": 1}
            per = {s[n]: 2 * k for n, k in names.items()} | {V: 2 * 7}
            with looped(dve, H // 2, per) as i:
                for u in range(2):
                    elementwise(u, 2 * i + u)
                    scan(u, i)
            modulation(1)
            gated(used, SLOTS["wo"], 1, USES["wo"], 0, 0, hg["sq"][:, 0:64])

            def first_of(dst, eq, tmp, s1):
                rank = col("rank").unsqueeze(1).broadcast_to([P, TJ, 4])
                V.link(dve, tt(tmp, eq, rank, ALU.mult))
                V.link(dve, dve.tensor_reduce(s1, tmp, AX.X, ALU.max))
                V.link(dve, tt(dst, tmp, s1.unsqueeze(2).broadcast_to([P, TJ, 4]), ALU.is_equal))

            def moe(layer):
                norm(2 * layer + 1)
                lg, r1, r2, r3, s1, s2, s3, s4, pst = (mo[n] for n in "lg r1 r2 r3 s1 s2 s3 s4 ps".split())
                four = lambda ap: ap.unsqueeze(2).broadcast_to([P, TJ, 4])
                dve.wait_ge(sn_out, 32 * H)
                V.link(dve, dve.memset(lg, 0.0))
                V.link(dve, dve.memset(mo["P"][:, 0, :], 1.0))
                V.link(dve, dve.tensor_tensor_scan(iota1, mo["P"][:, 0, :], mo["P"][:, 0, :], 0.0, ALU.mult, ALU.add))
                dve.memset(mo["hs"][:, :, T:TW], 0.0)
                V.link(dve, tt(strict, causal, ident, ALU.subtract))
                dve.wait_ge(s["lg_turned"].sem, layer + 1)
                V.link(dve, dve.tensor_copy(lg[:, 0:4, :], shaped(ps[:, 3, 0:80], 4, 20)))
                V.link(dve, dve.tensor_copy(lg[0:64, 4, :], ps[0:64, 3, 80:100]))
                V.link(dve, dve.tensor_reduce(s1, lg[:, :, 0:4], AX.X, ALU.max))
                V.link(dve, tt(r1, lg[:, :, 0:4], four(s1), ALU.subtract))
                V.link(dve, ts(r2, r1, 0.0, None, ALU.is_equal))
                first_of(mo["ohg"], r2, r3, s3)
                s["ohg_ready"].link(dve, dve.memset(mo["ohg"][64:P, 4, :], 0.0))
                el = lg[:, :, 4:20].rearrange("p j (g e) -> p j g e", g=G)
                for g in range(G):
                    oh = mo["ohg"][:, :, g:g + 1].broadcast_to([P, TJ, E])
                    V.link(dve, tt(mo["sel"][:, :, g, :], lg[:, :, 4 + E * g:4 + E * (g + 1)], oh, ALU.mult))
                V.link(dve, tt(r2, mo["sel"][:, :, 0, :], mo["sel"][:, :, 1, :], ALU.add))
                V.link(dve, tt(r2, r2, mo["sel"][:, :, 2, :], ALU.add))
                V.link(dve, tt(r2, r2, mo["sel"][:, :, 3, :], ALU.add))
                rk, tot, pre, off, pos = (mo[n] for n in "rk tot pre off pos".split())
                dve.wait_ge(s["ranked"].sem, layer + 1)
                V.link(dve, dve.tensor_copy(rk, shaped(ps[:, 2, 0:20], TJ, 4)))
                V.link(dve, dve.tensor_copy(tot, shaped(ps[:, 2, 32:52], TJ, 4)))
                V.link(dve, dve.memset(pre[:, 0, :], 0.0))
                for j in range(1, TJ):
                    V.link(dve, tt(pre[:, j, :], pre[:, j - 1, :], tot[:, j - 1, :], ALU.add))
                V.link(dve, tt(tot[:, 0, :], pre[:, TJ - 1, :], tot[:, TJ - 1, :], ALU.add))
                V.link(dve, dve.memset(off[:, 0:1], 0.0))
                for g in range(1, G):
                    V.link(dve, tt(off[:, g:g + 1], off[:, g - 1:g], tot[:, 0, g - 1:g], ALU.add))
                V.link(dve, dve.tensor_copy(off_i[:, 0:G], off[0:1, :]))
                V.link(dve, dve.tensor_copy(off_i[:, G:G + 1], off[0:1, 0:1]))
                V.link(dve, tt(rk, rk, pre, ALU.add))
                V.link(dve, tt(rk, rk, off.unsqueeze(1).broadcast_to([P, TJ, 4]), ALU.add))
                V.link(dve, tt(rk, rk, mo["ohg"], ALU.mult))
                V.link(dve, dve.tensor_reduce(pos, rk, AX.X, ALU.add))
                V.link(dve, ts(pos, pos, 1.0, None, ALU.add))
                for j in range(TJ):
                    ins = ts(dg[:, j, :], ident, pos[:, j:j + 1], None, ALU.mult)
                s["place_ready"].link(dve, ins)
                for j in range(TJ):
                    ins = ts(P_r[:, j, :], iota1, pos[:, j:j + 1], None, ALU.is_equal)
                s["spread"].link(dve, ins)
                V.link(dve, dve.tensor_reduce(s1, r2, AX.X, ALU.max))
                V.link(dve, tt(r3, r2, four(s1), ALU.is_equal))
                first_of(mo["oh1"], r3, r3, s3)
                V.link(dve, stt(r2, mo["oh1"], -BIG, r2, ALU.mult, ALU.add))
                V.link(dve, dve.tensor_reduce(s4, r2, AX.X, ALU.max))
                V.link(dve, tt(r3, r2, four(s4), ALU.is_equal))
                first_of(mo["oh2"], r3, r3, s3)
                s["top_in"].on(tt(s2, s4, s1, ALU.subtract))
                dve.wait_ge(s["top_out"].sem, layer + 1)
                V.link(dve, dve.tensor_reduce(pst, r1, AX.X, ALU.add))
                V.link(dve, ts(s3, s2, 1.0, None, ALU.add))
                V.link(dve, tt(s3, s3, pst, ALU.mult))
                V.link(dve, dve.reciprocal(s3, s3))
                V.link(dve, tt(s2, s2, s3, ALU.mult))
                V.link(dve, tt(r1, mo["oh1"], four(s3), ALU.mult))
                V.link(dve, tt(r2, mo["oh2"], four(s2), ALU.mult))
                V.link(dve, tt(r1, r1, r2, ALU.add))
                for g in range(G):
                    ins = tt(mo["comb"][:, :, g, :], r1, mo["ohg"][:, :, g:g + 1].broadcast_to([P, TJ, E]), ALU.mult)
                s["comb_ready"].on(ins)
                n, extra, cum, prev = tot[:, 0, :], mo["w0"], mo["w1"], mo["w2"]
                V.link(dve, ts(extra, n, float(W), None, ALU.is_gt))
                for k in range(2, MORE + 1):
                    V.link(dve, stt(extra, n, float(k * W), extra, ALU.is_gt, ALU.add))
                V.link(dve, dve.tensor_copy(cum[:, 0:1], extra[:, 0:1]))
                for g in range(1, G):
                    V.link(dve, tt(cum[:, g:g + 1], cum[:, g - 1:g], extra[:, g:g + 1], ALU.add))
                V.link(dve, tt(prev, cum, extra, ALU.subtract))
                oh, part, more = mo["w3"], mo["w0"], mo["more"]
                for k in range(MORE):
                    V.link(dve, ts(oh, prev, float(k), None, ALU.is_le))
                    V.link(dve, stt(oh, cum, float(k), oh, ALU.is_gt, ALU.mult))
                    V.link(dve, dve.tensor_reduce(more[:, 0, k:k + 1], oh, AX.X, ALU.add))
                    V.link(dve, ts(part, col("rank"), -1.0, float(G), ALU.mult, ALU.add))
                    V.link(dve, tt(part, part, oh, ALU.mult))
                    V.link(dve, dve.tensor_reduce(more[:, 1, k:k + 1], part, AX.X, ALU.add))
                    V.link(dve, ts(part, prev, -float(W), float(W * (k + 1)), ALU.mult, ALU.add))
                    V.link(dve, tt(part, part, off, ALU.add))
                    V.link(dve, tt(part, part, oh, ALU.mult))
                    V.link(dve, dve.tensor_reduce(more[:, 2, k:k + 1], part, AX.X, ALU.add))
                    for ch in range(2):
                        V.link(dve, stt(mo["more_at"][:, ch, k:k + 1], col("part"), P * ch + 1.0, more[:, 2, k:k + 1],
                                        ALU.add, ALU.add))
                V.link(dve, dve.tensor_copy(more_i, more[0:1, :, :]))
                for q in range(2 * G):
                    V.link(dve, stt(mo["at"][:, q:q + 1], col("part"), P * (q % 2) + 1.0, off[:, q // 2:q // 2 + 1],
                                    ALU.add, ALU.add))
                dve.wait_ge(s["cS_ready"].sem, layer + 1)
                ub = (USES[f"moe{layer}"] + DC) // 2
                base = SLOTS[f"moe{layer}"]

                def weights(g, off_g, e):
                    dve.wait_ge(s["cb_full"].sem, E * g + (NE * layer + e + 1))
                    s["ce_ready"].on(ts(mo["ce"][0:NE, e % 2, :], mo["cS"][0:NE, bass.ds(off_g, W)],
                                        ident[0:NE, bass.ds(E * g + e, 1)], None, ALU.mult))

                def start_of(g):
                    return dve.value_load(off_i[0:1, bass.ds(g, 1)], min_val=0, max_val=T)

                off_g = dve.value_load(off_i[0:1, 0:1], min_val=0, max_val=T)
                weights(0, off_g, 0)
                weights(0, off_g, 1)
                per = {s["ce_ready"]: 2 * E, s["hid_ready"]: 2 * KG, s["pt_ready"]: 2 * 2, s["yg_ready"]: 2 * 2}
                with looped(dve, 2, per) as i:
                    for gg in range(2):
                        g = 2 * i + gg
                        off_g = start_of(g)
                        for e in range(E):
                            for f in range(FT):
                                t = 2 * e + f
                                dve.wait_ge(used, 2 * N_GROUP * i + (base + N_GROUP * gg + 2 * t + 2))
                                dve.wait_ge(pair_free[0].sem, 16 * i + (ub + 8 * gg + t + 1))
                                pair_free[1].on(tt(mo["tmp"], ps[:, 2, 0:W], mo["sil"], ALU.mult))
                                dve.wait_ge(s["cb_full"].sem, E * g + (NE * layer + e + 3))
                                dve.wait_ge(pair_free[1].sem, 16 * i + (ub + 8 * gg + t + 1))
                                s["hid_ready"].link(dve, tt(mo["hid"][:, t, :], mo["tmp"],
                                                            ps[:, 2 * (e % 2) + 1, 0:W], ALU.mult))
                                if f == 0 and 1 <= e < E - 1:
                                    weights(g, off_g, e + 1)
                        off_n = start_of(g + 1)
                        weights(g + 1, off_n, 0)
                        weights(g + 1, off_n, 1)
                        for ch in range(2):
                            s["pt_ready"].on(ts(at(PT_r, 2 * g + ch), pos_row, mo["at"][:, bass.ds(2 * g + ch, 1)], None,
                                                ALU.is_equal))
                        for ch in range(2):
                            dve.wait_ge(s["y_hi_ready"].sem, 2 * g + (2 * G * layer + ch + 1))
                            rows = slice(0, CH[ch])
                            halved = lambda ap: ap.rearrange("p (a n) -> p a n", a=2)
                            s["yg_ready"].on(tt(halved(at(y_lo, 2 * g + ch)[rows]), ps[rows, 4 + 2 * ch:6 + 2 * ch, :],
                                                halved(at(y_hi, 2 * g + ch)[rows]), ALU.subtract))
                gated(s["scattered"].sem, DC * layer, 1, USES[f"moe{layer}"] + DC + 4 * NE, layer, 1, mo["tmp"][:, 0:64])

            def further_windows(layer):
                X = x_dve[layer]
                for k in range(MORE):
                    with further_one(dve, k) as (group, start):
                        for e in range(E):
                            X.link(dve, ts(mo["ce"][0:NE, 0, :], mo["cS"][0:NE, bass.ds(start, W)],
                                           ident[0:NE, bass.ds(E * group + e, 1)], None, ALU.mult))
                            dve.wait_ge(x_act[layer].sem, X_ACT * k + (e + 1))
                            X.link(dve, tt(xhid[:, 2 * e, :], ps[:, 2, 0:W], mo["sil"], ALU.mult))
                            X.link(dve, tt(xhid[:, 2 * e + 1, :], ps[:, 4, 0:W], xsil, ALU.mult))
                            for f in range(FT):
                                t = FT * e + f
                                X.link(dve, tt(xhid[:, t, :], xhid[:, t, :], ps[:, 1, 0:W], ALU.mult))
                        for ch in range(2):
                            X.link(dve, ts(mo["PT"][:, ch, :], pos_row, mo["more_at"][:, ch, k:k + 1], None, ALU.is_equal))
                        for m in range(DC):
                            p = m % 2
                            dve.wait_ge(x_pe[layer].sem, X_PE * k + (6 + m + 2))
                            g = modt[:, layer, 40 + m, :]
                            tmp = mo["tmp"][:, 0:64]
                            X.link(dve, stt(xT[:, m, 0:TH], ps[:, 2 * p, 0:TH], g[:, 0:1], xT[:, m, 0:TH], ALU.mult, ALU.add))
                            X.link(dve, stt(xT[:, m, TH:TP], ps[:, 2 * p + 1, 0:TP - TH], g[:, 0:1], xT[:, m, TH:TP],
                                            ALU.mult, ALU.add))
                            X.link(dve, tt(by_seq(tmp), by_seq(ps[:, 2 * p + 1, TP - TH:TH]), over_t(g[:, 1:NV]), ALU.mult))
                            X.link(dve, tt(xT[:, m, TP:T], xT[:, m, TP:T], tmp, ALU.add))

            moe(0)
            further_windows(0)
            norm(2)

            wE = col("wE", 3, MT, 4)
            V.link(dve, dve.memset(first["gx"], 0.0))
            V.link(dve, dve.memset(first["gm"], 0.0))
            V.link(dve, dve.memset(first["xpad"][:, :, 0:3], 0.0))
            dve.wait_ge(conv_in, 32)
            cw = col("cw", 4, MT)

            def weight_of(w, i):
                return wE[:, w, i, :] if isinstance(i, int) else wE[:, w, bass.ds(i, 1), :].rearrange("p a o -> p (a o)")

            def block_diagonal(dst, w, i):
                return tt(dst.rearrange("p (m o) -> p m o", o=4), col("bd").unsqueeze(2).broadcast_to([P, 32, 4]),
                          weight_of(w, i).unsqueeze(1).broadcast_to([P, 32, 4]), ALU.mult)

            def gate_weights(dst, w, i):
                g = first["wg"][:, w, bass.ds(i, 1)].rearrange("p a n o -> p (a n) o")
                return tt(dst, g, weight_of(w, i).unsqueeze(1).broadcast_to([P, 8, 4]), ALU.mult)

            def inner(u, i, guarded):
                if guarded:
                    dve.wait_ge(s["gates_full"].sem, i - 1)
                two4 = lambda ap: ap.rearrange("p (a b) -> p a b", a=2)[:, :, 0:4]
                V.link(dve, gate_weights(first["pr"], 0, i))
                V.link(dve, gate_weights(first["pr2"], 1, i))
                V.link(dve, tt(first["pr"], first["pr"], first["pr2"], ALU.add))
                V.link(dve, dve.tensor_reduce(two4(first["gx"][:, u, :]), first["pr"].rearrange(
                    "p (a b) o -> p a b o", a=2), AX.X, ALU.add))
                V.link(dve, gate_weights(first["pr"], 2, i))
                V.link(dve, dve.tensor_reduce(two4(first["gm"][:, u, :]), first["pr"].rearrange(
                    "p (a b) o -> p a b o", a=2), AX.X, ALU.add))
                s["bdv_ready"].on(block_diagonal(first["bdv"][:, u, :], 2, i))
                xp = first["xpad"][:, u, :]
                pads = xp[:, 3 + TP:].rearrange("p (b t) -> p b t", b=NB)
                c0 = first["conv0"][:, bass.ds(i, 1), :].rearrange("p a (b t) -> p (a b) t", t=3)
                V.link(dve, dve.tensor_copy(pads[:, :, 0:3], c0))
                dve.wait_ge(s["xm_ready"].sem, 3 * i + 3)
                dve.wait_ge(s["xc_ready"].sem, i)
                acc = first["acc"]
                for tap in range(4):
                    w = cw[:, tap, i:i + 1] if isinstance(i, int) else cw[:, tap, bass.ds(i, 1)]
                    cb = col("cb")[:, bass.ds(i, 1)]
                    for dst, src in ((acc[:, 0:TP], xp[:, tap:tap + TP]), (by_seq(acc[:, TP:T]), pads[:, :, tap:tap + TS])):
                        if tap == 0:
                            ins = ts(dst, src, w, cb, ALU.mult, ALU.add)
                        else:
                            ins = stt(dst, src, w, dst, ALU.mult, ALU.add)
                    if tap < 3:
                        V.link(dve, ins)
                co = at(first["convout"], i)
                s["conv_acc"].on(ins)
                dve.tensor_copy(co[:, 0:3], xp[:, TP:TP + 3])
                dve.tensor_copy(co[:, 3:].rearrange("p (b t) -> p b t", b=NB), pads[:, :, TS:TS + 3])
                dve.wait_ge(s["v_full"].sem, i + 1)
                vt = ml["vtok"][:, :, bass.ds(P * i, P)]
                dve.tensor_copy(vt[:, 0:4, :], shaped(ps[:, 4, :], 4, P))
                s["v_read"].link(dve, dve.tensor_copy(vt[0:64, 4, :], ps[0:64, 5, 0:P]))

            inner(0, 0, False)
            inner(1, 1, False)
            with looped(dve, MT // 2 - 1, {V: 2 * 10, s["bdv_ready"]: 2, s["conv_acc"]: 2, s["v_read"]: 2}) as i:
                for u in range(2):
                    inner(u, 2 * i + (u + 2), True)

            def head_weights(h):
                bdq = ml["W"].rearrange("p a b -> p (a b)")
                for w in range(2):
                    for i in range(HT):
                        ins = block_diagonal(bdq[:, (HT * w + i) * P:(HT * w + i + 1) * P], w, HT * h + i)
                s["bd_ready"].on(ins)

            dve.wait_ge(s["gates_full"].sem, MT)
            dve.wait_ge(out_done, 16)
            head_weights(0)
            ig, gb, gu, t1, t2 = (gate[n][0:MH, :] for n in ("ig", "b", "u", "t1", "t2"))
            for dst, r0 in ((ig, 0), (t1, 32)):
                V.link(dve, dve.tensor_copy(dst[:, 0:TP], ps[r0:r0 + MH, 6, :]))
                V.link(dve, dve.tensor_copy(dst[:, TP:T], ps[r0:r0 + MH, 7, 0:64]))
            V.link(dve, ts(ig, ig, col("big")[0:MH, :], None, ALU.add))
            V.link(dve, ts(t1, t1, col("bfg")[0:MH, :], None, ALU.add))
            s["abs_ready"].link(dve, stt(t2, t1, -1.0, t1, ALU.mult, ALU.max))
            V.link(dve, ts(t1, t1, 0.0, None, ALU.min))
            dve.wait_ge(s["soft_ready"].sem, 1)
            V.link(dve, tt(t1, t1, t2, ALU.subtract))
            V.link(dve, dve.tensor_tensor_scan(gb, col("whole")[0:MH, :], t1, 0.0, ALU.mult, ALU.add))
            V.link(dve, tt(gu, ig, gb, ALU.subtract))
            V.link(dve, dve.tensor_copy(t2, gu))
            V.link(dve, ts(t2[:, 0:1], gu[:, 0:1], 0.0, None, ALU.max))
            m0 = col("m0")[0:MH, :]
            V.link(dve, tt(by_seq(t2[:, TP:T])[:, :, 0:1], by_seq(gu[:, TP:T])[:, :, 0:1], m0.unsqueeze(2), ALU.max))
            cut = gate["cut"][0:MH, :]
            V.link(dve, ts(cut, col("whole")[0:MH, :], -1.0, BIG, ALU.add, ALU.mult))
            V.link(dve, dve.tensor_tensor_scan(ig, cut, t2, 0.0, ALU.add, ALU.max))
            V.link(dve, tt(gb, gb, ig, ALU.add))
            rows = ml["rows"]
            V.link(dve, ts(rows[0:MH, :], ig, -1.0, None, ALU.mult))
            V.link(dve, dve.tensor_copy(rows[32:32 + MH, :], gb))
            V.link(dve, dve.tensor_copy(t2[:, 0:1], gb[:, TP - 1:TP]))
            V.link(dve, dve.tensor_copy(t2[:, 1:NV].unsqueeze(2), by_seq(gb[:, TP:T])[:, :, TS - 1:TS]))
            V.link(dve, ts(t1[:, 0:TP], gu[:, 0:TP], ig[:, TP - 1:TP], None, ALU.subtract))
            V.link(dve, tt(by_seq(t1[:, TP:T]), by_seq(gu[:, TP:T]), over_t(by_seq(ig[:, TP:T])[:, :, TS - 1]), ALU.subtract))
            s["dec_ready"].on(tt(by_seq(gb[:, TP:T]), over_t(m0), by_seq(ig[:, TP:T]), ALU.subtract))
            dve.wait_ge(s["dec_exp"].sem, 1)
            V.link(dve, dve.tensor_copy(rows[64:64 + MH, :], t1))
            s["rows_ready"].link(dve, dve.tensor_copy(rows[96:96 + MH, TP:T], gb[:, TP:T]))
            dve.wait_ge(s["turned_g"].sem, 1)
            for n, dst in enumerate((ml["utok"], ml["wtok"])):
                V.link(dve, dve.tensor_copy(dst[:, 0:4, :], shaped(ps[:, 4, 32 * n:32 * n + 16], 4, MH)))
                s["tok_ready"].link(dve, dve.tensor_copy(dst[0:64, 4, :], ps[0:64, 4, 32 * n + 16:32 * n + 20]))

            ub = USES["b"]
            n0 = col("n0", MT, NB)
            for h in range(MH):
                hb = ub + N_HEADB * h
                if h == 0:
                    dve.wait_ge(out_done, 32)
                dve.wait_ge(s["kt_full"].sem, h + 1)
                p = (hb + 8) % 2
                pair_free[p].on(ts(ml["ktok"][0:64, 4, :], ps[0:64, 2 * p, :], ml["wtok"][0:64, 4, h:h + 1], KS,
                                   ALU.mult, ALU.mult))
                for j in range(4):
                    ins = ts(ml["ktok"][:, j, :], ps[:, 4 + j, :], ml["wtok"][:, j, h:h + 1], KS, ALU.mult, ALU.mult)
                s["kt_read"].link(dve, ins)
                for pp in range(2):
                    dve.wait_ge(pair_free[pp].sem, (hb + 14 - 2 * pp) // 2)
                for i in range(HT):
                    tmp = mx["rs"]
                    V.link(dve, tt(tmp, ml["kz"][:, i, :], mx["mu"], ALU.mult))
                    no = ml["nout"][:, HT * h + i, :]
                    V.link(dve, dve.tensor_reduce(no[:, 0:1], tmp[:, 0:TP], AX.X, ALU.add))
                    V.link(dve, dve.tensor_reduce(no[:, 1:NV], by_seq(tmp[:, TP:T]), AX.X, ALU.add))
                wl = by_seq(mx["wcb"])[:, :, TS - 1]
                nh = n0[:, HT * h:HT * (h + 1), :]
                V.link(dve, tt(shaped(mx["rs"][:, 0:HT * NB], HT, NB), nh, wl.unsqueeze(1).broadcast_to([P, HT, NB]), ALU.mult))
                no = ml["nout"][:, HT * h:HT * (h + 1), 1:NV]
                s["n_ready"].link(dve, tt(no, no, shaped(mx["rs"][:, 0:HT * NB], HT, NB), ALU.add))
                qs = ml["q"][:, :, TP:T]
                V.link(dve, tt(mx["qw"], qs, mx["wcb"].unsqueeze(1).broadcast_to([P, HT, 64]), ALU.mult))
                dve.wait_ge(s["s_full"].sem, h + 1)

                def weight(j):
                    n = TP - P * j if j < 4 else 64
                    m = P if j < 4 else 64
                    w = ml["W"][0:m, j % 2, 0:n]
                    src = mx["nM"][0:m, P * j:P * j + n]
                    s["w_ready"].link(dve, ts(w, src, ml["utok"][0:m, j, h:h + 1], 0.0, ALU.add, ALU.min))

                weight(0)
                for j in range(TJ):
                    if j + 1 < TJ:
                        weight(j + 1)
                    dve.wait_ge(s["w_exp"].sem, 5 * h + j + 1)
                    if j < 4:
                        n = TP - P * j
                        Pj = mx[f"P{j}"]
                        V.link(dve, tt(Pj, ps[:, 4 + j, 0:n], ml["W"][:, j % 2, 0:n], ALU.mult))
                        s["p_ready"].link(dve, tt(Pj[:, 0:P], Pj[:, 0:P], causal, ALU.mult))
                    else:
                        p = (hb + 13) % 2
                        pair_free[p].on(tt(mx["Ps"][0:64, :], ps[0:64, 2 * p, 0:64], ml["W"][0:64, 0, 0:64], ALU.mult))
                        dve.wait_ge(pair_free[p].sem, (hb + 13) // 2 + 1)
                        s["p_ready"].link(dve, tt(mx["Ps"][0:64, :], mx["Ps"][0:64, :], causal_s[0:64, :], ALU.mult))
                s["qw_ready"].on(tt(qn.rearrange("p i (b t) -> p i b t", b=NB),
                                    mx["qw"].rearrange("p i (b t) -> p i b t", b=NB), over_t(nh), ALU.mult))
                V.link(dve, dve.memset(alone, 0.0))

                def one_sequence(b):
                    if b >= 2:
                        dve.memset(alone[:, b % 2, :, TS * (b - 2):TS * (b - 1)], 0.0)
                    of_b = slice(TS * b, TS * (b + 1))
                    s["alone_ready"].on(dve.tensor_copy(alone[:, b % 2, :, of_b], mx["qw"][:, :, of_b]))

                one_sequence(0)
                one_sequence(1)
                for b in range(NB):
                    n = NB * h + b
                    C = shaped(ml["C"][:, n % 2, :], HT, MD)
                    dve.wait_ge(s["num_s"].sem, 9 * h + b + 2)
                    if b + 2 < NB:
                        one_sequence(b + 2)
                    for k in range(HT):
                        dve.wait_ge(s["upd_c"].sem, HT * n + k + 1)
                        s["c_done"].on(stt(C[:, k, :], C[:, k, :], mx["wcb"][:, TS * b + TS - 1:TS * (b + 1)],
                                           ps[:, 4 + k, :], ALU.mult, ALU.add))
                rd = mx["rs"]

                def guard_den(dst, den, emn):
                    V.link(dve, ts(dst, den, -1.0, None, ALU.mult))
                    V.link(dve, tt(dst, dst, den, ALU.max))
                    V.link(dve, tt(dst, dst, emn, ALU.max))
                    V.link(dve, dve.reciprocal(dst, dst))

                n = hb + 15
                p = n % 2
                dve.wait_ge(s["num_full"].sem, h + 1)
                guard_den(rd[:, TP:T], ps[:, 2 * p + 1, 0:64], mx["emn"][:, TP:T])
                dve.wait_ge(s["turned_s"].sem, h + 1)
                ins = tt(ml["q"][:, :, TP:T], shaped(ps[:, 2 * p, 0:256], HT, 64),
                         rd[:, TP:T].unsqueeze(1).broadcast_to([P, HT, 64]), ALU.mult)
                pair_free[p].on(ins)
                fb = 17 * h + 12
                n += 1
                p = n % 2
                dve.wait_ge(s["b_full"].sem, fb + 1)
                V.link(dve, ts(rd[:, 0:TP], ps[:, 2 * p, :], -1.0, None, ALU.mult))
                pair_free[p].on(tt(rd[:, 0:TP], rd[:, 0:TP], ps[:, 2 * p, :], ALU.max))
                dve.wait_ge(pair_free[p].sem, n // 2 + 1)
                V.link(dve, tt(rd[:, 0:TP], rd[:, 0:TP], mx["emn"][:, 0:TP], ALU.max))
                V.link(dve, dve.reciprocal(rd[:, 0:TP], rd[:, 0:TP]))
                for i in range(HT):
                    n += 1
                    p = n % 2
                    dve.wait_ge(s["b_full"].sem, fb + 2 + i)
                    pair_free[p].on(tt(ml["q"][:, i, 0:TP], ps[:, 2 * p, :], rd[:, 0:TP], ALU.mult))
                n += 2
                p = n % 2
                dve.wait_ge(s["mu_full"].sem, h + 1)
                pair_free[p].on(ts(two(mx["mu"]), halves(p), 1.0 / MD, None, ALU.mult))
                dve.wait_ge(pair_free[p].sem, n // 2 + 1)
                q, z = ml["q"], ml["kz"]
                s["rs_h"].link(dve, tt(q, q, mx["mu"].unsqueeze(1).broadcast_to([P, HT, T]), ALU.subtract))
                if h + 1 < MH:
                    for u in range(2):
                        dve.wait_ge(cp_out[u], 8 * HT * (h + 1))
                    head_weights(h + 1)
                dve.wait_ge(s["sqh_ready"].sem, h + 1)
                for i in range(HT):
                    V.link(dve, ts(q[:, i, :], q[:, i, :], col("mln")[:, HT * h + i:HT * h + i + 1], None, ALU.mult))
                dve.wait_ge(s["rsh_ready"].sem, h + 1)
                V.link(dve, tt(q, q, mx["rs"].unsqueeze(1).broadcast_to([P, HT, T]), ALU.mult))
                for i in range(HT):
                    xc = ml["xc"][:, HT * h + i, :]
                    V.link(dve, stt(q[:, i, :], xc, col("skip")[:, HT * h + i:HT * h + i + 1], q[:, i, :], ALU.mult, ALU.add))
                for p in range(2):
                    dve.wait_ge(pair_free[p].sem, (hb + N_HEADB) // 2)
                s["ho_ready"].link(dve, tt(ml["xc"][:, HT * h:HT * (h + 1), :], q, z, ALU.mult))

            dve.wait_ge(x_back, 16)
            gated(used, SLOTS["md"], 2, USES["md"], 1, 0, ml["W"][:, 0, 0:64])
            moe(1)
            further_windows(1)
            norm(4)


def kernel(**inputs):
    import concourse.bacc as _bacc
    from concourse.bass_utils import run_bass_kernel_spmd as _run

    a = {k: np.asarray(v) for k, v in inputs.items()}
    f32 = np.float32

    def features(x):
        return np.moveaxis(x.reshape(x.shape[:-1] + (-1, P)), -1, 0)

    cols = np.zeros((P, NCOL), f32)

    def put(name, x):
        at, n = COLS[name]
        x = np.asarray(x, f32)
        x = x.reshape(x.shape[0], -1)
        assert x.shape[1] == n, (name, x.shape, n)
        cols[:x.shape[0], at:at + n] = x

    c = np.concatenate([a["c_prompt"], a["c_sample"]], 0)
    put("c", np.moveaxis(features(c), 1, 2))
    put("bada", features(a["b_ada"]))
    put("ng", features(a["norm_g"]))
    put("fg", features(a["final_g"]))
    put("hgn", a["hg_norm"][0][:, None])
    put("lb", features(a["hg_lb"]))
    put("cw", features(a["ml_conv_w"][0]))
    put("cb", features(a["ml_conv_b"][0]))
    headwise = np.stack([a[n][0].transpose(0, 2, 1).reshape(MT, P, 4) for n in ("ml_wq", "ml_wk", "ml_wv")], 0)
    put("wE", headwise.transpose(2, 0, 1, 3))
    put("mln", features(a["ml_norm"][0]))
    put("skip", features(a["ml_skip"][0]))
    wr = np.concatenate([a["moe_wrg"], a["moe_wre"].reshape(LAYERS, D, NE)], 2)
    put("wr", wr.reshape(LAYERS, DC, P, 20).transpose(2, 0, 1, 3))
    put("rb", np.concatenate([a["moe_brg"], a["moe_bre"].reshape(LAYERS, NE)], 1).T)
    put("n0", a["state_mlstm_n"][0].reshape(NB, MT, P).transpose(2, 1, 0))
    put("big", a["ml_big"].T)
    put("bfg", a["ml_bfg"].T)
    put("m0", a["state_mlstm_m"][0].T)
    t = np.arange(T)
    put("ident", np.eye(P))
    put("ones", np.ones((P, P)))
    put("causal", np.triu(np.ones((P, P))))
    r = np.arange(NB * TS)
    put("causal_s", (r[:, None] // TS == r[None] // TS) & (r[:, None] <= r[None]))
    put("own", r[:, None] // TS == np.arange(NB)[None])
    starts = np.where(t < TP, t % P == 0, (t - TP) % TS == 0)
    whole = np.where(t < TP, t == 0, (t - TP) % TS == 0)
    put("whole", np.tile(np.where(whole, 0.0, 1.0), (MH, 1)))
    put("rank", np.tile(np.arange(4, 0, -1), (P, 1)))
    put("bd", np.arange(P)[:, None] // 4 == np.arange(32)[None])
    put("eps", np.full((P, 1), EPS))
    put("part", np.arange(P)[:, None])

    def tiles(w):
        k, m = w.shape
        w = w.reshape(k // 1024, 8, P, m // P, P).transpose(3, 0, 2, 1, 4)
        return w.reshape(-1, P, SLOT)

    def ada_tiles(w):
        w = w.reshape(4, 2, P, 12, 512).transpose(3, 0, 2, 1, 4)
        return w.reshape(-1, P, SLOT)

    win = a["hg_win"][0].reshape(D, 4, H, P)[:, [1, 0, 3, 2]]
    parts = {
        "ada0": ada_tiles(a["w_ada"][0]), "ada1": ada_tiles(a["w_ada"][1]),
        "hg": tiles(win.transpose(0, 2, 1, 3).reshape(D, -1)),
        "wo": tiles(a["hg_wo"][0]),
        "xm": tiles(a["ml_wup"][0][:, :MI]), "z": tiles(a["ml_wup"][0][:, MI:]),
        "md": tiles(a["ml_wdown"][0])}
    for l in range(LAYERS):
        w13 = np.stack([a["moe_w1"][l].reshape(NE, D, FT, P), a["moe_w3"][l].reshape(NE, D, FT, P)], 3)
        w13 = tiles(w13.transpose(1, 0, 2, 3, 4).reshape(D, -1)).reshape(G, 2 * KG, P, SLOT)
        w2 = a["moe_w2"][l].reshape(G, KG, P, D)
        parts[f"moe{l}"] = np.concatenate([w13, w2], 1).reshape(-1, P, SLOT)
    wstream = np.empty((NSLOT, P, SLOT), f32)
    for name, w in parts.items():
        wstream[SLOTS[name]:SLOTS[name] + len(w)] = w

    x = np.concatenate([a["x_prompt"].reshape(TP, D), a["x_sample"].reshape(NB * TS, D)], 0)
    wg = np.concatenate([a["ml_wig"][0], a["ml_wfg"][0]], 1).reshape(3, MT, 32, 4, 8)
    wg = np.broadcast_to(wg.transpose(0, 1, 2, 4, 3)[:, :, :, None], (3, MT, 32, 4, 8, 4))
    c0 = a["state_mlstm_c"][0].transpose(1, 0, 2, 3).reshape(MH * NB, HT, P, MD)
    arrays = {
        "cols": cols, "wstream": wstream, "keep": np.tile(np.where(starts, 0.0, 1.0), (P, 1)),
        "xT": x.reshape(T, DC, P).transpose(2, 1, 0),
        "hg0": a["state_hgrn"][0].transpose(1, 2, 0, 3).reshape(H, P, NB * P),
        "wg": wg.reshape(3, MT, P, 32).transpose(2, 0, 1, 3).reshape(P, -1),
        "conv0": a["state_conv"][0].reshape(NB, 3, MT, P).transpose(3, 2, 0, 1).reshape(P, -1),
        "c0": c0.transpose(0, 2, 1, 3).reshape(MH * NB, P, HT * MD)}
    arrays = {k: np.ascontiguousarray(v, f32) for k, v in arrays.items()}
    outs = {"y": (P, DC, T), "hg_p": (H, P, P), "hg_s": (H, P, NB * P), "mc_p": (MH, HT, P, MD),
            "mc_s": (MH * NB, P, HT * MD), "mn": (P, MT * NV), "mm": (MH, NV), "conv": (P, MT * 3 * NV)}

    nc = _bacc.Bacc("TRN2", target_bir_lowering=False, num_devices=1)
    io = {k: nc.dram_tensor(f"in_{k}", list(v.shape), F32, kind="ExternalInput").ap() for k, v in arrays.items()}
    io["out"] = {k: nc.dram_tensor(f"out_{k}", list(v), F32, kind="ExternalOutput").ap() for k, v in outs.items()}
    io["x_dram"] = nc.dram_tensor("x_dram", [P, DC, T], F32, kind="Internal").ap()
    build(nc, io)
    res = _run(nc, [{f"in_{k}": v for k, v in arrays.items()}], core_ids=[0]).results[0]
    o = {k: np.asarray(res[f"out_{k}"]) for k in outs}

    y = o["y"].transpose(2, 1, 0).reshape(T, D)
    mn = o["mn"].reshape(P, MT, NV).transpose(2, 1, 0).reshape(NV, MH, MD)
    conv = o["conv"].reshape(P, MT, NV, 3).transpose(2, 3, 1, 0).reshape(NV, 3, MI)
    mm = o["mm"].T
    hg_s = o["hg_s"].reshape(H, P, NB, P).transpose(2, 0, 1, 3)
    mc_s = o["mc_s"].reshape(MH, NB, P, HT, MD).transpose(1, 0, 3, 2, 4).reshape(NB, MH, MD, MD)
    return (y[:TP].reshape(1, TP, D), y[TP:].reshape(NB, TS, D), o["hg_p"][None, None],
            o["mc_p"].reshape(1, 1, MH, MD, MD), mn[None, :1], mm[None, :1], conv[None, :1],
            hg_s[None], mc_s[None], mn[None, 1:], mm[None, 1:], conv[None, 1:])
```
